# Optimizing a Trainium2 kernel written in Bass

```python
import jax, jax.numpy as jnp
from jax import lax
import numpy as np

D_MODEL = 1024
BATCH = 1
SEQ = 512
DEPTH = 2

MEM_LEN = 256
EPS = 1e-6
ATTN_HEADS = 4
ATTN_HEAD_DIM = 64
ATTN_WIDTH = ATTN_HEADS * ATTN_HEAD_DIM
DILATED_PATTERNS = ((128, 1), (512, 4), (2048, 16))
WINDOW_BLOCK = 128
ROPE_THETA = 500000.0
ROPE_DIM = ATTN_HEAD_DIM // 4
CONV_GROUPS = 4
CONV_WIDTH = D_MODEL // 4
CONV_K = 3
GDN_HEADS = 4
GDN_HEAD_DIM = 128
GDN_WIDTH = GDN_HEADS * GDN_HEAD_DIM
GDN_CONV_K = 4
GDN_CHUNK = 64
MIX_WIDTH = ATTN_WIDTH + CONV_WIDTH + GDN_WIDTH
IN_SPLITS = (ATTN_WIDTH, ATTN_WIDTH, ATTN_WIDTH,
             CONV_WIDTH, CONV_WIDTH, CONV_WIDTH,
             GDN_WIDTH, GDN_WIDTH, GDN_WIDTH, GDN_HEADS, GDN_HEADS, GDN_WIDTH)
IN_WIDTH = 3 * ATTN_WIDTH + 3 * CONV_WIDTH + 4 * GDN_WIDTH + 2 * GDN_HEADS
XATTN_HEADS = 4
XATTN_HEAD_DIM = D_MODEL // XATTN_HEADS
XATTN_WIDTH = XATTN_HEADS * XATTN_HEAD_DIM
FFN_HIDDEN = -(-8 * D_MODEL // (3 * 256)) * 256


def rms_norm(x, w):
    x32 = x.astype(jnp.float32)
    y = x32 * lax.rsqrt(jnp.mean(x32 * x32, axis=-1, keepdims=True) + EPS)
    return (y * w.astype(jnp.float32)).astype(x.dtype)

def causal_depthwise_conv(x, w):
    K, C = w.shape
    return lax.conv_general_dilated(x, w[:, None, :].astype(x.dtype), window_strides=(1,),
                                    padding=[(K - 1, 0)], dimension_numbers=('NWC', 'WIO', 'NWC'),
                                    feature_group_count=C)

def rotary_tables(positions):
    inv_freq = jnp.float32(ROPE_THETA) ** (-jnp.arange(0, ROPE_DIM, 2, dtype=jnp.float32) / ROPE_DIM)
    ang = positions.astype(jnp.float32)[..., None] * inv_freq
    return jnp.cos(ang)[:, :, None, :], jnp.sin(ang)[:, :, None, :]

def apply_partial_rotary(x, cos, sin):
    half = ROPE_DIM // 2
    x1 = x[..., :half].astype(jnp.float32)
    x2 = x[..., half:ROPE_DIM].astype(jnp.float32)
    rot = jnp.concatenate([x1 * cos - x2 * sin, x2 * cos + x1 * sin], axis=-1).astype(x.dtype)
    return jnp.concatenate([rot, x[..., ROPE_DIM:]], axis=-1)

def dilated_window_attention(q, k, v, dilation, n_back):
    B, S, H, Dh = q.shape
    QB = WINDOW_BLOCK
    L = S // dilation
    nb = -(-L // QB)
    Lp = nb * QB

    def to_residue(t):
        t = t.reshape(B, L, dilation, H, Dh).transpose(0, 2, 1, 3, 4).reshape(B * dilation, L, H, Dh)
        t = jnp.pad(t, ((0, 0), (0, Lp - L), (0, 0), (0, 0)))
        return t.reshape(B * dilation, nb, QB, H, Dh)

    def with_prev(t):
        prev = jnp.pad(t[:, :-1], ((0, 0), (1, 0), (0, 0), (0, 0), (0, 0)))
        return jnp.concatenate([prev, t], axis=2)

    qb = to_residue(q)
    kw = with_prev(to_residue(k))
    vw = with_prev(to_residue(v))
    s = jnp.einsum('bnqhd,bnkhd->bnhqk', qb, kw, preferred_element_type=jnp.float32)
    qi = jnp.arange(nb)[:, None, None] * QB + jnp.arange(QB)[None, :, None]
    kj = jnp.arange(nb)[:, None, None] * QB - QB + jnp.arange(2 * QB)[None, None, :]
    dist = qi - kj
    mask = (dist >= 0) & (dist <= n_back) & (kj >= 0)
    s = jnp.where(mask[None, :, None], s, -jnp.inf)
    m = jnp.max(s, axis=-1, keepdims=True)
    p = jnp.exp(s - m)
    l = jnp.sum(p, axis=-1, keepdims=True)
    o = jnp.einsum('bnhqk,bnkhd->bnqhd', (p / l).astype(v.dtype), vw)
    lse = (m + jnp.log(l))[..., 0]
    o = o.reshape(B, dilation, Lp, H, Dh)[:, :, :L].transpose(0, 2, 1, 3, 4).reshape(B, S, H, Dh)
    lse = lse.transpose(0, 1, 3, 2).reshape(B, dilation, Lp, H)[:, :, :L]
    lse = lse.transpose(0, 2, 1, 3).reshape(B, S, H)
    return o, lse

def dilated_attention_mixer(q, k, v, cos, sin):
    B, S, _ = q.shape
    q = q.reshape(B, S, ATTN_HEADS, ATTN_HEAD_DIM)
    k = k.reshape(B, S, ATTN_HEADS, ATTN_HEAD_DIM)
    v = v.reshape(B, S, ATTN_HEADS, ATTN_HEAD_DIM)
    q = apply_partial_rotary(q, cos, sin) * (ATTN_HEAD_DIM ** -0.5)
    k = apply_partial_rotary(k, cos, sin)
    outs, lses = [], []
    for window, dilation in DILATED_PATTERNS:
        o, lse = dilated_window_attention(q, k, v, dilation, window // dilation)
        outs.append(o.astype(jnp.float32))
        lses.append(lse)
    wts = jax.nn.softmax(jnp.stack(lses, axis=0), axis=0)
    o = jnp.einsum('pbsh,pbshd->bshd', wts, jnp.stack(outs, axis=0))
    return o.reshape(B, S, ATTN_WIDTH).astype(q.dtype)

def short_conv_mixer(b_gate, c_gate, xv, conv_w):
    return b_gate * causal_depthwise_conv(c_gate * xv, conv_w)

def gated_delta_rule(q, k, v, g, beta):
    B, S, H, Dk = q.shape
    Dv = v.shape[-1]
    C = GDN_CHUNK
    N = S // C

    def chunks(t):
        return jnp.moveaxis(t.reshape(B, N, C, H, *t.shape[3:]), 3, 1)

    q, k, v, g, beta = chunks(q), chunks(k), chunks(v), chunks(g), chunks(beta)
    decay = jnp.cumsum(g, axis=-1)
    causal = jnp.tril(jnp.ones((C, C), dtype=bool))
    strict = jnp.tril(jnp.ones((C, C), dtype=bool), -1)
    rel = jnp.exp(jnp.where(causal, decay[..., :, None] - decay[..., None, :], -jnp.inf))
    k_beta = k * beta[..., None]
    a = jnp.where(strict, jnp.einsum('bhnik,bhnjk->bhnij', k_beta, k) * rel, 0.0)
    eye = jnp.broadcast_to(jnp.eye(C, dtype=jnp.float32), a.shape)
    rhs = jnp.concatenate([v * beta[..., None], k_beta * jnp.exp(decay)[..., None]], axis=-1)
    sol = lax.linalg.triangular_solve(eye + a, rhs, left_side=True, lower=True, unit_diagonal=True)
    u, w = sol[..., :Dv], sol[..., Dv:]
    attn = jnp.where(causal, jnp.einsum('bhnik,bhnjk->bhnij', q, k) * rel, 0.0)
    q_dec = q * jnp.exp(decay)[..., None]
    k_dec = k * jnp.exp(decay[..., -1:] - decay)[..., None]
    chunk_decay = jnp.exp(decay[..., -1])

    def step(state, inp):
        q_i, k_i, u_i, w_i, attn_i, cd_i = inp
        v_new = u_i - jnp.einsum('bhck,bhkv->bhcv', w_i, state)
        o_i = (jnp.einsum('bhck,bhkv->bhcv', q_i, state)
               + jnp.einsum('bhij,bhjv->bhiv', attn_i, v_new))
        state = state * cd_i[..., None, None] + jnp.einsum('bhck,bhcv->bhkv', k_i, v_new)
        return state, o_i

    xs = tuple(jnp.moveaxis(t, 2, 0) for t in (q_dec, k_dec, u, w, attn, chunk_decay))
    state0 = jnp.zeros((B, H, Dk, Dv), jnp.float32)
    _, o = lax.scan(step, state0, xs)
    return o.transpose(1, 0, 3, 2, 4).reshape(B, S, H, Dv)

def gated_deltanet_mixer(q, k, v, a, b, gate, conv_w, a_log, dt_bias, norm_w):
    B, S, _ = q.shape
    qkv = jax.nn.silu(causal_depthwise_conv(jnp.concatenate([q, k, v], axis=-1), conv_w))
    q, k, v = jnp.split(qkv.astype(jnp.float32), 3, axis=-1)
    q = q.reshape(B, S, GDN_HEADS, GDN_HEAD_DIM)
    k = k.reshape(B, S, GDN_HEADS, GDN_HEAD_DIM)
    v = v.reshape(B, S, GDN_HEADS, GDN_HEAD_DIM)
    q = q * lax.rsqrt(jnp.sum(q * q, axis=-1, keepdims=True) + EPS) * (GDN_HEAD_DIM ** -0.5)
    k = k * lax.rsqrt(jnp.sum(k * k, axis=-1, keepdims=True) + EPS)
    g = -jnp.exp(a_log.astype(jnp.float32)) * jax.nn.softplus(a.astype(jnp.float32) + dt_bias.astype(jnp.float32))
    beta = jax.nn.sigmoid(b.astype(jnp.float32))
    o = gated_delta_rule(q, k, v, g, beta)
    gate = jax.nn.silu(gate.astype(jnp.float32)).reshape(B, S, GDN_HEADS, GDN_HEAD_DIM)
    o = rms_norm(o, norm_w) * gate
    return o.reshape(B, S, GDN_WIDTH).astype(gate.dtype if gate.dtype == q.dtype else gate.dtype)

def memory_cross_attention(h, mem, w_q, w_kv, w_o):
    B, S, _ = h.shape
    M = mem.shape[1]
    q = (h @ w_q).reshape(B, S, XATTN_HEADS, XATTN_HEAD_DIM)
    k, v = jnp.split(mem @ w_kv, 2, axis=-1)
    k = k.reshape(B, M, XATTN_HEADS, XATTN_HEAD_DIM)
    v = v.reshape(B, M, XATTN_HEADS, XATTN_HEAD_DIM)
    s = jnp.einsum('bshd,bmhd->bhsm', q, k, preferred_element_type=jnp.float32) * (XATTN_HEAD_DIM ** -0.5)
    p = jax.nn.softmax(s, axis=-1)
    o = jnp.einsum('bhsm,bmhd->bshd', p.astype(v.dtype), v).reshape(B, S, XATTN_WIDTH)
    return o @ w_o

def swiglu_ffn(h, w_gate_up, w_down):
    gate, up = jnp.split(h @ w_gate_up, 2, axis=-1)
    return (jax.nn.silu(gate) * up) @ w_down

def first_inputs(seed: int = 0) -> dict:
    key = jax.random.key(seed)
    ks = jax.random.split(key, 24)
    f32 = jnp.float32

    def dense(k, shape, fan_in):
        return jax.random.normal(k, shape, f32) * (fan_in ** -0.5)

    def gain(k, shape):
        return 1.0 + 0.02 * jax.random.normal(k, shape, f32)

    x = jax.random.normal(ks[0], (BATCH, SEQ, D_MODEL), f32)
    mem = jax.random.normal(ks[1], (BATCH, MEM_LEN, D_MODEL), f32)
    positions = (jax.random.randint(ks[2], (BATCH, 1), 0, 4096, dtype=jnp.int32)
                 + jnp.arange(SEQ, dtype=jnp.int32)[None, :])
    dt = jnp.exp(jax.random.uniform(ks[3], (DEPTH, GDN_HEADS), f32, np.log(1e-3), np.log(1e-1)))
    return {
        'x': x,
        'mem': mem,
        'positions': positions,
        'norm_mix_pre': gain(ks[4], (DEPTH, D_MODEL)),
        'norm_mix_post': gain(ks[5], (DEPTH, D_MODEL)),
        'w_in': dense(ks[6], (DEPTH, D_MODEL, IN_WIDTH), D_MODEL),
        'conv_short': dense(ks[7], (DEPTH, CONV_K, CONV_WIDTH), CONV_K),
        'conv_gdn': dense(ks[8], (DEPTH, GDN_CONV_K, 3 * GDN_WIDTH), GDN_CONV_K),
        'gdn_a_log': jnp.log(jax.random.uniform(ks[9], (DEPTH, GDN_HEADS), f32, 1.0, 16.0)),
        'gdn_dt_bias': dt + jnp.log(-jnp.expm1(-dt)),
        'gdn_norm': gain(ks[10], (DEPTH, GDN_HEAD_DIM)),
        'w_out': dense(ks[11], (DEPTH, MIX_WIDTH, D_MODEL), MIX_WIDTH),
        'norm_mem': gain(ks[12], (DEPTH, D_MODEL)),
        'norm_xattn_pre': gain(ks[13], (DEPTH, D_MODEL)),
        'norm_xattn_post': gain(ks[14], (DEPTH, D_MODEL)),
        'w_xq': dense(ks[15], (DEPTH, D_MODEL, XATTN_WIDTH), D_MODEL),
        'w_xkv': dense(ks[16], (DEPTH, D_MODEL, 2 * XATTN_WIDTH), D_MODEL),
        'w_xo': dense(ks[17], (DEPTH, XATTN_WIDTH, D_MODEL), XATTN_WIDTH),
        'norm_ffn_pre': gain(ks[18], (DEPTH, D_MODEL)),
        'norm_ffn_post': gain(ks[19], (DEPTH, D_MODEL)),
        'w_gate_up': dense(ks[20], (DEPTH, D_MODEL, 2 * FFN_HIDDEN), D_MODEL),
        'w_down': dense(ks[21], (DEPTH, FFN_HIDDEN, D_MODEL), FFN_HIDDEN),
    }

def first_block(x, mem, positions, norm_mix_pre, norm_mix_post, w_in, conv_short, conv_gdn,
              gdn_a_log, gdn_dt_bias, gdn_norm, w_out, norm_mem, norm_xattn_pre, norm_xattn_post,
              w_xq, w_xkv, w_xo, norm_ffn_pre, norm_ffn_post, w_gate_up, w_down):
    cos, sin = rotary_tables(positions)
    split_idx = [int(i) for i in np.cumsum(IN_SPLITS)[:-1]]
    h = x
    for l in range(DEPTH):
        hn = rms_norm(h, norm_mix_pre[l])
        proj = hn @ w_in[l]
        (aq, ak, av, cb, cc, cx, gq, gk, gv, ga, gb, gg) = jnp.split(proj, split_idx, axis=-1)
        y_attn = dilated_attention_mixer(aq, ak, av, cos, sin)
        y_conv = short_conv_mixer(cb, cc, cx, conv_short[l])
        y_gdn = gated_deltanet_mixer(gq, gk, gv, ga, gb, gg, conv_gdn[l],
                                     gdn_a_log[l], gdn_dt_bias[l], gdn_norm[l]).astype(proj.dtype)
        mix = jnp.concatenate([y_attn.astype(proj.dtype), y_conv, y_gdn], axis=-1) @ w_out[l]
        h = h + rms_norm(mix, norm_mix_post[l])
        hn = rms_norm(h, norm_xattn_pre[l])
        xa = memory_cross_attention(hn, rms_norm(mem, norm_mem[l]), w_xq[l], w_xkv[l], w_xo[l])
        h = h + rms_norm(xa, norm_xattn_post[l])
        hn = rms_norm(h, norm_ffn_pre[l])
        h = h + rms_norm(swiglu_ffn(hn, w_gate_up[l], w_down[l]), norm_ffn_post[l])
    return h


GRID_W = 64
CTX_LEN = 256
HEAD_DIM = 64
ROPE_THETA_2 = 10000.0
Q_BLOCK = 128
NEG_INF = -1e30
ATTN_SCALE = HEAD_DIM ** -0.5

A_HEADS = 8
A_KV_HEADS = 2
B_HEADS = 8
B_KV_HEADS = 2
B_WINDOW = 128
C_WIDTH = 512
C_CONV = 31
D_HEADS = 8
NA_KH = 8
NA_KW = 16

A_Q = A_HEADS * HEAD_DIM
A_KV = A_KV_HEADS * HEAD_DIM
B_Q = B_HEADS * HEAD_DIM
B_KV = B_KV_HEADS * HEAD_DIM
D_W = D_HEADS * HEAD_DIM
EVEN_WIDTHS = (A_Q, A_KV, A_KV, A_Q, B_Q, B_KV, B_KV, B_Q)
ODD_WIDTHS = (C_WIDTH, C_WIDTH, C_WIDTH, D_W, D_W, D_W, D_W)
EVEN_IN = sum(EVEN_WIDTHS)
ODD_IN = sum(ODD_WIDTHS)
EVEN_MIX = A_Q + B_Q
ODD_MIX = C_WIDTH + D_W


def rms_norm_2(x, g):
    xf = x.astype(jnp.float32)
    y = xf * lax.rsqrt(jnp.mean(xf * xf, axis=-1, keepdims=True) + EPS)
    return (y * g.astype(jnp.float32)).astype(x.dtype)

def layer_norm(x, g, b):
    xf = x.astype(jnp.float32)
    mu = jnp.mean(xf, axis=-1, keepdims=True)
    var = jnp.mean(jnp.square(xf - mu), axis=-1, keepdims=True)
    y = (xf - mu) * lax.rsqrt(var + EPS)
    return (y * g.astype(jnp.float32) + b.astype(jnp.float32)).astype(x.dtype)

def split_cols(h, widths):
    offs = [int(o) for o in np.cumsum(widths)[:-1]]
    return jnp.split(h, offs, axis=-1)

def heads(t, n_heads):
    return t.reshape(t.shape[:-1] + (n_heads, HEAD_DIM))

def group(q, kv_heads):
    return q.reshape(q.shape[:-2] + (kv_heads, q.shape[-2] // kv_heads, HEAD_DIM))

def axial_rope_tables(n):
    t = jnp.arange(n)
    row = (t // GRID_W).astype(jnp.float32)
    col = (t % GRID_W).astype(jnp.float32)
    half = HEAD_DIM // 2
    freqs = ROPE_THETA_2 ** (-jnp.arange(0, half, 2, dtype=jnp.float32) / half)
    ang = jnp.concatenate([row[:, None] * freqs, col[:, None] * freqs], axis=-1)
    return jnp.cos(ang), jnp.sin(ang)

def apply_rope(x, cos, sin):
    xf = x.astype(jnp.float32)
    x1, x2 = xf[..., 0::2], xf[..., 1::2]
    c, s = cos[None, :, None, :], sin[None, :, None, :]
    out = jnp.stack([x1 * c - x2 * s, x1 * s + x2 * c], axis=-1).reshape(x.shape)
    return out.astype(x.dtype)

def gqa_attend(q, k, v, bias=None, sink=None):
    s = jnp.einsum("bqhgd,bkhd->bhgqk", q, k, preferred_element_type=jnp.float32) * ATTN_SCALE
    if bias is not None:
        s = s + bias
    if sink is not None:
        sink_col = jnp.broadcast_to(sink.astype(jnp.float32)[None, :, :, None, None], s.shape[:-1] + (1,))
        p = jax.nn.softmax(jnp.concatenate([s, sink_col], axis=-1), axis=-1)[..., :-1]
    else:
        p = jax.nn.softmax(s, axis=-1)
    return jnp.einsum("bhgqk,bkhd->bqhgd", p.astype(v.dtype), v)

def even_mixer(h_lat, h_ctx, w_in, w_out, q_gain, k_gain, sink, cos, sin, update_ctx):
    bsz, n, _ = h_lat.shape
    ctx_len = h_ctx.shape[1]
    n_blk = n // Q_BLOCK
    ga, gb = A_HEADS // A_KV_HEADS, B_HEADS // B_KV_HEADS
    sink = sink.reshape(B_KV_HEADS, gb)

    def project(h):
        aq, ak, av, ag, bq, bk, bv, bg = split_cols(h @ w_in, EVEN_WIDTHS)
        aq = rms_norm_2(heads(aq, A_HEADS), q_gain)
        ak = rms_norm_2(heads(ak, A_KV_HEADS), k_gain)
        return (aq, ak, heads(av, A_KV_HEADS), ag,
                heads(bq, B_HEADS), heads(bk, B_KV_HEADS), heads(bv, B_KV_HEADS), bg)

    aq, ak, av, ag, bq, bk, bv, bg = project(h_lat)
    c_aq, c_ak, c_av, c_ag, c_bq, c_bk, c_bv, c_bg = project(h_ctx)
    aq, ak, bq, bk = (apply_rope(t, cos, sin) for t in (aq, ak, bq, bk))

    ka = jnp.concatenate([c_ak, ak], axis=1)
    va = jnp.concatenate([c_av, av], axis=1)
    qa_blk = jnp.moveaxis(group(aq, A_KV_HEADS).reshape(bsz, n_blk, Q_BLOCK, A_KV_HEADS, ga, HEAD_DIM), 1, 0)
    oa = lax.map(lambda qb: gqa_attend(qb, ka, va), qa_blk)
    oa = jnp.moveaxis(oa, 0, 1).reshape(bsz, n, A_Q)

    band = Q_BLOCK + 2 * B_WINDOW
    kb_pad = jnp.pad(bk, ((0, 0), (B_WINDOW, B_WINDOW), (0, 0), (0, 0)))
    vb_pad = jnp.pad(bv, ((0, 0), (B_WINDOW, B_WINDOW), (0, 0), (0, 0)))
    rel = jnp.arange(band)[None, :] - B_WINDOW - jnp.arange(Q_BLOCK)[:, None]
    in_band = jnp.abs(rel) <= B_WINDOW
    ctx_open = jnp.zeros((Q_BLOCK, ctx_len), jnp.float32)
    qb_blk = jnp.moveaxis(group(bq, B_KV_HEADS).reshape(bsz, n_blk, Q_BLOCK, B_KV_HEADS, gb, HEAD_DIM), 1, 0)

    def b_block(args):
        blk, qb = args
        start = blk * Q_BLOCK
        kpos = start - B_WINDOW + jnp.arange(band)
        valid = in_band & ((kpos >= 0) & (kpos < n))[None, :]
        bias = jnp.concatenate([ctx_open, jnp.where(valid, 0.0, NEG_INF)], axis=-1)
        kk = jnp.concatenate([c_bk, lax.dynamic_slice_in_dim(kb_pad, start, band, axis=1)], axis=1)
        vv = jnp.concatenate([c_bv, lax.dynamic_slice_in_dim(vb_pad, start, band, axis=1)], axis=1)
        return gqa_attend(qb, kk, vv, bias, sink)

    ob = lax.map(b_block, (jnp.arange(n_blk), qb_blk))
    ob = jnp.moveaxis(ob, 0, 1).reshape(bsz, n, B_Q)

    y_lat = jnp.concatenate([oa * jax.nn.silu(ag), ob * jax.nn.silu(bg)], axis=-1) @ w_out
    if not update_ctx:
        return y_lat, None
    oa_c = gqa_attend(group(c_aq, A_KV_HEADS), c_ak, c_av).reshape(bsz, ctx_len, A_Q)
    ob_c = gqa_attend(group(c_bq, B_KV_HEADS), c_bk, c_bv, sink=sink).reshape(bsz, ctx_len, B_Q)
    y_ctx = jnp.concatenate([oa_c * jax.nn.silu(c_ag), ob_c * jax.nn.silu(c_bg)], axis=-1) @ w_out
    return y_lat, y_ctx

def conformer_conv(val, glu_gate, silu_gate, dw_w, dw_b, ln_g, ln_b):
    u = val * jax.nn.sigmoid(glu_gate)
    u = lax.conv_general_dilated(u, dw_w.reshape(C_CONV, 1, C_WIDTH), window_strides=(1,),
                                 padding=[(C_CONV // 2, C_CONV // 2)],
                                 dimension_numbers=("NWC", "WIO", "NWC"),
                                 feature_group_count=C_WIDTH) + dw_b
    u = jax.nn.silu(layer_norm(u, ln_g, ln_b))
    return u * jax.nn.silu(silu_gate)

def odd_mixer(h_lat, h_ctx, w_in, w_out, dw_w, dw_b, ln_g, ln_b, rpb, update_ctx):
    bsz, n, _ = h_lat.shape
    ctx_len = h_ctx.shape[1]
    rows = n // GRID_W
    kh = min(NA_KH, rows)

    cv, cgl, cg, dq, dk, dv, dg = split_cols(h_lat @ w_in, ODD_WIDTHS)
    x_cv, x_cgl, x_cg, x_dq, x_dk, x_dv, x_dg = split_cols(h_ctx @ w_in, ODD_WIDTHS)
    c_dk, c_dv = heads(x_dk, D_HEADS), heads(x_dv, D_HEADS)

    oc = conformer_conv(cv, cgl, cg, dw_w, dw_b, ln_g, ln_b)

    q_rows = jnp.moveaxis(heads(dq, D_HEADS).reshape(bsz, rows, GRID_W, D_HEADS, HEAD_DIM), 1, 0)
    k_grid = heads(dk, D_HEADS).reshape(bsz, rows, GRID_W, D_HEADS, HEAD_DIM)
    v_grid = heads(dv, D_HEADS).reshape(bsz, rows, GRID_W, D_HEADS, HEAD_DIM)
    cols = jnp.arange(GRID_W)
    col_start = jnp.clip(cols - NA_KW // 2, 0, GRID_W - NA_KW)
    col_in = (cols[None, :] >= col_start[:, None]) & (cols[None, :] < col_start[:, None] + NA_KW)
    col_mask = jnp.where(col_in, 0.0, NEG_INF)
    dc_idx = jnp.clip(cols[None, :] - cols[:, None] + NA_KW - 1, 0, 2 * NA_KW - 2)
    rpb = rpb.astype(jnp.float32)
    ctx_open = jnp.zeros((D_HEADS, GRID_W, ctx_len), jnp.float32)

    def d_row(args):
        r, qr = args
        rs = jnp.clip(r - kh // 2, 0, rows - kh)
        kr = lax.dynamic_slice_in_dim(k_grid, rs, kh, axis=1).reshape(bsz, kh * GRID_W, D_HEADS, HEAD_DIM)
        vr = lax.dynamic_slice_in_dim(v_grid, rs, kh, axis=1).reshape(bsz, kh * GRID_W, D_HEADS, HEAD_DIM)
        dr_idx = rs + jnp.arange(kh) - r + NA_KH - 1
        bias = rpb[:, dr_idx][:, :, dc_idx] + col_mask[None, None]
        bias = jnp.transpose(bias, (0, 2, 1, 3)).reshape(D_HEADS, GRID_W, kh * GRID_W)
        bias = jnp.concatenate([ctx_open, bias], axis=-1)[None, :, None]
        kk = jnp.concatenate([c_dk, kr], axis=1)
        vv = jnp.concatenate([c_dv, vr], axis=1)
        return gqa_attend(qr[:, :, :, None, :], kk, vv, bias).reshape(bsz, GRID_W, D_W)

    od = lax.map(d_row, (jnp.arange(rows), q_rows))
    od = jnp.moveaxis(od, 0, 1).reshape(bsz, n, D_W)

    y_lat = jnp.concatenate([oc, od * jax.nn.silu(dg)], axis=-1) @ w_out
    if not update_ctx:
        return y_lat, None
    oc_c = conformer_conv(x_cv, x_cgl, x_cg, dw_w, dw_b, ln_g, ln_b)
    od_c = gqa_attend(heads(x_dq, D_HEADS)[:, :, :, None, :], c_dk, c_dv).reshape(bsz, ctx_len, D_W)
    y_ctx = jnp.concatenate([oc_c, od_c * jax.nn.silu(x_dg)], axis=-1) @ w_out
    return y_lat, y_ctx

def modulation(cond, w, b):
    m = jax.nn.silu(cond) @ w + b
    return jnp.split(m, 3, axis=-1)

def second_inputs(seed: int = 0) -> dict:
    key = jax.random.key(seed)
    ks = jax.random.split(key, 24)
    n_even = (DEPTH + 1) // 2
    n_odd = DEPTH // 2
    f32 = jnp.float32

    def nrm(k, shape, scale):
        return jax.random.normal(k, shape, f32) * scale

    return {
        "x": nrm(ks[0], (BATCH, SEQ, D_MODEL), 1.0),
        "c": nrm(ks[1], (BATCH, D_MODEL), 1.0),
        "ctx": nrm(ks[2], (BATCH, CTX_LEN, D_MODEL), 1.0),
        "c_ctx": nrm(ks[3], (D_MODEL,), 1.0),
        "mod_w": nrm(ks[4], (DEPTH, D_MODEL, 3 * D_MODEL), 0.5 * D_MODEL ** -0.5),
        "mod_b": nrm(ks[5], (DEPTH, 3 * D_MODEL), 0.02),
        "norm_g": 1.0 + nrm(ks[6], (DEPTH, D_MODEL), 0.05),
        "ev_w_in": nrm(ks[7], (n_even, D_MODEL, EVEN_IN), D_MODEL ** -0.5),
        "ev_w_out": nrm(ks[8], (n_even, EVEN_MIX, D_MODEL), EVEN_MIX ** -0.5),
        "a_q_gain": 1.0 + nrm(ks[9], (n_even, HEAD_DIM), 0.05),
        "a_k_gain": 1.0 + nrm(ks[10], (n_even, HEAD_DIM), 0.05),
        "b_sink": nrm(ks[11], (n_even, B_HEADS), 0.5),
        "od_w_in": nrm(ks[12], (n_odd, D_MODEL, ODD_IN), D_MODEL ** -0.5),
        "od_w_out": nrm(ks[13], (n_odd, ODD_MIX, D_MODEL), ODD_MIX ** -0.5),
        "c_dw_w": nrm(ks[14], (n_odd, C_CONV, C_WIDTH), C_CONV ** -0.5),
        "c_dw_b": nrm(ks[15], (n_odd, C_WIDTH), 0.02),
        "c_ln_g": 1.0 + nrm(ks[16], (n_odd, C_WIDTH), 0.05),
        "c_ln_b": nrm(ks[17], (n_odd, C_WIDTH), 0.02),
        "d_rpb": nrm(ks[18], (n_odd, D_HEADS, 2 * NA_KH - 1, 2 * NA_KW - 1), 0.1),
        "final_g": 1.0 + nrm(ks[19], (D_MODEL,), 0.05),
    }

def second_block(x, c, ctx, c_ctx, mod_w, mod_b, norm_g, ev_w_in, ev_w_out, a_q_gain, a_k_gain, b_sink,
              od_w_in, od_w_out, c_dw_w, c_dw_b, c_ln_g, c_ln_b, d_rpb, final_g):
    n = x.shape[1]
    cos, sin = axial_rope_tables(n)
    x_lat, x_ctx = x, ctx
    for i in range(DEPTH):
        update_ctx = i < DEPTH - 1
        sh_l, sc_l, g_l = modulation(c, mod_w[i], mod_b[i])
        sh_c, sc_c, g_c = modulation(c_ctx, mod_w[i], mod_b[i])
        h_lat = rms_norm_2(x_lat, norm_g[i]) * (1.0 + sc_l[:, None, :]) + sh_l[:, None, :]
        h_ctx = rms_norm_2(x_ctx, norm_g[i]) * (1.0 + sc_c) + sh_c
        j = i // 2
        if i % 2 == 0:
            y_lat, y_ctx = even_mixer(h_lat, h_ctx, ev_w_in[j], ev_w_out[j], a_q_gain[j], a_k_gain[j],
                                      b_sink[j], cos, sin, update_ctx)
        else:
            y_lat, y_ctx = odd_mixer(h_lat, h_ctx, od_w_in[j], od_w_out[j], c_dw_w[j], c_dw_b[j],
                                     c_ln_g[j], c_ln_b[j], d_rpb[j], update_ctx)
        x_lat = x_lat + g_l[:, None, :] * y_lat
        if update_ctx:
            x_ctx = x_ctx + g_c * y_ctx
    return rms_norm_2(x_lat, final_g)


def setup_inputs(seed=0):
    out = dict(first_inputs(seed))
    for name, value in second_inputs(seed + 1).items():
        if name != "x":
            out[name + "_2"] = value
    return out


def reference(
    x, mem, positions, norm_mix_pre, norm_mix_post, w_in, conv_short, conv_gdn, gdn_a_log,
    gdn_dt_bias, gdn_norm, w_out, norm_mem, norm_xattn_pre, norm_xattn_post, w_xq, w_xkv, w_xo,
    norm_ffn_pre, norm_ffn_post, w_gate_up, w_down, c_2, ctx_2, c_ctx_2, mod_w_2, mod_b_2,
    norm_g_2, ev_w_in_2, ev_w_out_2, a_q_gain_2, a_k_gain_2, b_sink_2, od_w_in_2, od_w_out_2,
    c_dw_w_2, c_dw_b_2, c_ln_g_2, c_ln_b_2, d_rpb_2, final_g_2,
):
    x = first_block(
        x, mem, positions, norm_mix_pre, norm_mix_post, w_in, conv_short, conv_gdn, gdn_a_log,
        gdn_dt_bias, gdn_norm, w_out, norm_mem, norm_xattn_pre, norm_xattn_post, w_xq, w_xkv,
        w_xo, norm_ffn_pre, norm_ffn_post, w_gate_up, w_down,
    )
    return second_block(
        x, c_2, ctx_2, c_ctx_2, mod_w_2, mod_b_2, norm_g_2, ev_w_in_2, ev_w_out_2, a_q_gain_2,
        a_k_gain_2, b_sink_2, od_w_in_2, od_w_out_2, c_dw_w_2, c_dw_b_2, c_ln_g_2, c_ln_b_2,
        d_rpb_2, final_g_2,
    )


_drawn_inputs = setup_inputs


def setup_inputs(seed=0):
    import zlib

    import numpy as np

    out = dict(_drawn_inputs(seed))
    spreads = {}
    factors = {'gdn_norm': 3.819,
     'norm_xattn_pre': 2.991,
     'norm_xattn_post': 2.98,
     'norm_ffn_pre': 2.729,
     'norm_ffn_post': 3.915,
     'ctx_2': 8.0,
     'c_ctx_2': 3.63,
     'mod_b_2': 8.0,
     'norm_g_2': 8.0,
     'a_q_gain_2': 8.0,
     'a_k_gain_2': 8.0,
     'b_sink_2': 8.0,
     'c_dw_b_2': 60.599,
     'c_ln_g_2': 32.172,
     'c_ln_b_2': 64.0,
     'd_rpb_2': 169.419}
    for name, (base, spread) in spreads.items():
        noise = np.random.default_rng([zlib.crc32(name.encode()), seed]).standard_normal(out[name].shape)
        drawn = base * np.exp(spread * noise) if base else spread * noise
        out[name] = __import__('jax').numpy.asarray(drawn.astype(out[name].dtype))
    for name, factor in factors.items():
        out[name] = (out[name] * factor).astype(out[name].dtype)
    return out
```

```python
from contextlib import ExitStack

import numpy as np
import concourse.bass as bass
from concourse import mybir

P = 128
D = 1024
KC = D // P
S = 512
TT = S // P
M = 256
MT = M // P
DEPTH = 2
EPS = 1e-6
AH, AD = 4, 64
GH, GD = 4, 128
GK = 4
CK = 3
XH, XD = 4, 256
FH = 2816
FC = FH // P
ROPE_HALF = 8
NEG = -1.0e30
QH = 8
CC = 4
CT = 31
NROW = 8
GW = 64
RAW, SPLIT = 3, 2
UNROLL = RAW * SPLIT
BANKS = 8

SPLITS = np.cumsum([0, 256, 256, 256, 256, 256, 256, 512, 512, 512, 4, 4, 512]).tolist()
AQ, AK, AV, CB, CG, CX, GQ, GKK, GV, GA, GB, GG, _END = SPLITS
EVEN = np.cumsum([0, 512, 128, 128, 512, 512, 128, 128, 512]).tolist()


def in_jobs():
    jobs = []
    for h in range(GH):
        jobs += [(f"gk{h}", GKK + P * h, P), (f"gq{h}", GQ + P * h, P), (f"gv{h}", GV + P * h, P)]
    jobs.insert(3, ("ab", GA, 2 * GH))
    for c in range(2):
        jobs += [(f"aq{c}", AQ + P * c, P), (f"ak{c}", AK + P * c, P), (f"av{c}", AV + P * c, P)]
    for c in range(2):
        jobs += [(f"cg{c}", CG + P * c, P), (f"cx{c}", CX + P * c, P), (f"cb{c}", CB + P * c, P)]
    jobs += [(f"gg{h}", GG + P * h, P) for h in range(GH)]
    return jobs


def even_jobs():
    names = ["ak", "bk", "av", "bv"]
    at = {"aq": EVEN[0], "ak": EVEN[1], "av": EVEN[2], "ag": EVEN[3],
          "bq": EVEN[4], "bk": EVEN[5], "bv": EVEN[6], "bg": EVEN[7]}
    jobs = [(n, at[n], P) for n in names]
    for n in ("aq", "bq", "ag", "bg"):
        jobs += [(f"{n}{c}", at[n] + P * c, P) for c in range(4)]
    return jobs


def odd_jobs():
    names = ["cv", "cl", "cg", "dq", "dk", "dv", "dg"]
    at = {n: 512 * i for i, n in enumerate(names)}
    jobs = []
    for c in range(4):
        jobs += [(f"cv{c}", at["cv"] + P * c, P, False), (f"cl{c}", at["cl"] + P * c, P, False)]
    for n in ("cg", "dk", "dv", "dq", "dg"):
        jobs += [(f"{n}{c}", at[n] + P * c, P, n in ("dk", "dv")) for c in range(4)]
    return jobs


def weight_chunks():
    out = []
    for l in range(DEPTH):
        out += [("w_in", l, c0, n) for _, c0, n in in_jobs()]
        out += [("w_out", l, P * c, P) for c in range(KC)]
        out += [("w_xkv", l, P * c, P) for c in range(2 * KC)]
        out += [("w_xq", l, P * c, P) for c in range(KC)]
        out += [("w_xo", l, P * c, P) for c in range(KC)]
        for j in range(FC):
            out += [("w_gate_up", l, P * j, P), ("w_gate_up", l, FH + P * j, P)]
        out += [("w_down", l, P * c, P) for c in range(KC)]
    out += [("ev_w_in_2", 0, c0, n) for _, c0, n in even_jobs()]
    out += [("ev_w_out_2", 0, P * c, P) for c in range(KC)]
    out += [("od_w_in_2", 0, c0, n) for _, c0, n, _ in odd_jobs()]
    out += [("od_w_out_2", 0, P * c, P) for c in range(KC)]
    return out


def packed_weights(inputs):
    blocks = []
    for name, l, c0, n in weight_chunks():
        w = inputs[name][l][:, c0:c0 + n]
        if n < P:
            w = np.pad(w, ((0, 0), (0, P - n)))
        blocks.append(w.reshape(-1, P, P))
    blocks = np.concatenate(blocks)
    tiles = blocks.reshape(-1, KC, P, P).transpose(0, 2, 1, 3)
    return np.ascontiguousarray(tiles.reshape(-1, P, KC * P))


def tile_count():
    return sum((FC if name == "w_down" else KC) for name, *_ in weight_chunks()) // KC


class Columns:

    def __init__(self):
        self.at, self.n = {}, 0

    def add(self, name, width):
        self.at[name] = (self.n, width)
        self.n += width

    def __getitem__(self, name):
        return self.at[name]


def param_columns():
    c = Columns()
    for l in range(DEPTH):
        for name in ("mix_pre", "mix_post", "mem", "x_pre", "x_post", "f_pre", "f_post"):
            c.add(f"{name}{l}", KC)
        c.add(f"conv_short{l}", 2 * CK)
        c.add(f"conv_gdn{l}", 12 * GK)
        c.add(f"gdn_norm{l}", 1)
        c.add(f"dt_bias{l}", GH)
        c.add(f"a_log{l}", GH)
    for i in range(DEPTH):
        c.add(f"norm_g{i}", KC)
        c.add(f"mod_b{i}", 3 * KC)
    c.add("q_gain", 1)
    c.add("k_gain", 1)
    c.add("sink", QH)
    c.add("dw_w", CC * CT)
    c.add("dw_b", CC)
    c.add("ln_g", CC)
    c.add("ln_b", CC)
    c.add("final_g", KC)
    c.add("cond", 2 * KC)
    return c


def packed_params(inputs):
    c = param_columns()
    out = np.zeros((P, c.n), np.float32)

    def put(name, a):
        at, width = c[name]
        out[:, at:at + width] = a

    def cols(v):
        return np.asarray(v).reshape(-1, P).T

    def rows(v):
        return np.broadcast_to(np.asarray(v)[None, :], (P, len(v)))

    for l in range(DEPTH):
        for name, src in (("mix_pre", "norm_mix_pre"), ("mix_post", "norm_mix_post"), ("mem", "norm_mem"),
                          ("x_pre", "norm_xattn_pre"), ("x_post", "norm_xattn_post"),
                          ("f_pre", "norm_ffn_pre"), ("f_post", "norm_ffn_post")):
            put(f"{name}{l}", cols(inputs[src][l]))
        put(f"conv_short{l}", inputs["conv_short"][l].reshape(CK, 2, P).transpose(2, 1, 0).reshape(P, -1))
        put(f"conv_gdn{l}", inputs["conv_gdn"][l].reshape(GK, 12, P).transpose(2, 1, 0).reshape(P, -1))
        put(f"gdn_norm{l}", cols(inputs["gdn_norm"][l]))
        put(f"dt_bias{l}", rows(inputs["gdn_dt_bias"][l]))
        put(f"a_log{l}", rows(inputs["gdn_a_log"][l]))
    for i in range(DEPTH):
        put(f"norm_g{i}", cols(inputs["norm_g_2"][i]))
        put(f"mod_b{i}", cols(inputs["mod_b_2"][i]))
    put("q_gain", np.tile(inputs["a_q_gain_2"][0], 2)[:, None])
    put("k_gain", np.tile(inputs["a_k_gain_2"][0], 2)[:, None])
    put("sink", rows(inputs["b_sink_2"][0]))
    put("dw_w", inputs["c_dw_w_2"][0].reshape(CT, CC, P).transpose(2, 1, 0).reshape(P, -1))
    put("dw_b", cols(inputs["c_dw_b_2"][0]))
    put("ln_g", cols(inputs["c_ln_g_2"][0]))
    put("ln_b", cols(inputs["c_ln_b_2"][0]))
    put("final_g", cols(inputs["final_g_2"]))
    put("cond", np.stack([cols(inputs["c_2"][0]), cols(inputs["c_ctx_2"])], -1).reshape(P, -1))
    return out


def const_columns():
    c = Columns()
    for name in ("ident", "ones", "upto", "neg_future", "rope1", "rope2", "head_ones"):
        c.add(name, P)
    for s in range(7):
        c.add(f"level{s}", P)
    c.add("inv_freq", 1)
    c.add("eps", 1)
    c.add("eps_q", 1)
    c.add("half_pi", 1)
    c.add("zero", 1)
    return c


def constants():
    c = const_columns()
    out = np.zeros((P, c.n), np.float32)
    j, i = np.arange(P)[:, None], np.arange(P)[None, :]

    def put(name, a):
        at, width = c[name]
        out[:, at:at + width] = a

    put("ident", j == i)
    put("ones", 1.0)
    put("upto", j <= i)
    put("neg_future", np.where(i >= j, 0.0, NEG))
    swap = np.zeros((P, P), np.float32)
    for h in range(0, P, AD):
        for r in range(ROPE_HALF):
            swap[h + ROPE_HALF + r, h + r] = -1.0
            swap[h + r, h + ROPE_HALF + r] = 1.0
    put("rope1", swap)
    swap = np.zeros((P, P), np.float32)
    for r in range(0, P, 2):
        swap[r + 1, r] = -1.0
        swap[r, r + 1] = 1.0
    put("rope2", swap)
    put("head_ones", (j // 64) == (i // 64))
    for s in range(7):
        put(f"level{s}", ((i >> s) % 2 == 1) & ((j >> s) == (i >> s) - 1))
    freq = np.float32(500000.0) ** (-np.arange(0, 2 * ROPE_HALF, 2, dtype=np.float32) / (2 * ROPE_HALF))
    lane = np.arange(P) % AD
    put("inv_freq", np.where(lane < 2 * ROPE_HALF, freq[lane % ROPE_HALF], 0.0)[:, None])
    put("eps", EPS)
    put("eps_q", EPS * GD)
    put("half_pi", np.pi / 2)
    return out


def count_mask():
    q, k = np.arange(P)[:, None], np.arange(S)[None, :]
    dist = q + (S - P) - k
    n = (dist <= 128).astype(int) + (dist % 4 == 0) + (dist % 16 == 0)
    n = np.where(dist >= 0, n, 0)
    return np.where(n > 0, np.log(np.maximum(n, 1)), NEG).astype(np.float32)


def axial_tables():
    t = np.arange(S)
    row, col = (t // GW).astype(np.float32), (t % GW).astype(np.float32)
    freqs = np.float32(10000.0) ** (-np.arange(0, 32, 2, dtype=np.float32) / 32)
    ang = np.concatenate([row[:, None] * freqs, col[:, None] * freqs], -1)
    ang = np.repeat(ang, 2, axis=1)
    ang = np.concatenate([ang, ang], 1).T
    return np.ascontiguousarray(np.stack([np.cos(ang), np.sin(ang)], 1).astype(np.float32))


def band_mask():
    q, k = np.arange(P)[:, None], np.arange(3 * P)[None, :] - P
    return np.where(np.abs(k - q) <= 128, 0.0, NEG).astype(np.float32)


def column_mask():
    cols = np.arange(GW)
    start = np.clip(cols - 8, 0, GW - 16)
    inside = (cols[None] >= start[:, None]) & (cols[None] < start[:, None] + 16)
    return np.tile(np.where(inside, 0.0, NEG), (2, 1)).astype(np.float32)


class Book:

    def __init__(self, known=None):
        self.known = known
        self.marks, self.count, self.jobs, self.tiles = {}, {}, {}, 0
        self.sem = None

    def mark(self, event, name, value):
        assert event not in self.marks, event
        self.marks[event] = name, value

    def done(self, name, *key, by=1):
        self.count[name] = self.count.get(name, 0) + by
        self.mark((name, *key), name, self.count[name])
        return self.sem(name), by

    def loaded(self, name, *key):
        return self.done(name, *key, by=16)

    def when(self, *event):
        name, value = self.known.marks[event] if self.known else ("start", 1)
        if name == "bank_free":
            n = self.known.jobs[value]
            name, value = f"bank_free{n % BANKS}", n // BANKS + 1
        return self.sem(name), value

    def claim(self, pe, banks, *key):
        n = len(self.jobs)
        assert key not in self.jobs, key
        self.jobs[key] = n
        if n >= BANKS:
            pe.wait_ge(self.sem(f"bank_free{n % BANKS}"), n // BANKS)
        return banks[n % BANKS]

    def filled(self, *key):
        return self.done("bank_filled", *key)

    def bank(self, eng, banks, *key):
        eng.wait_ge(*self.when("bank_filled", *key))
        return banks[(self.known.jobs[key] if self.known else 0) % BANKS]

    def freed(self, *key, also=None):
        n = self.known.jobs[key] if self.known else 0
        if also:
            self.mark(also, "bank_free", key)
        return self.sem(f"bank_free{n % BANKS}"), 1

    def tile_used(self, *key):
        self.tiles += 1
        if key:
            self.mark(("bank_filled", *key), "w_used", self.tiles)
        return self.sem("w_used"), 1


def build(nc, dram, out, book, stop=None):
    f32, f32r, i32 = mybir.dt.float32, mybir.dt.float32r, mybir.dt.int32
    ALU, ACT, AX = mybir.AluOpType, mybir.ActivationFunctionType, mybir.AxisListType
    done, loaded, when = book.done, book.loaded, book.when
    pc, cc = param_columns(), const_columns()
    ctx = ExitStack()
    sems = {}

    def sem(name):
        if name not in sems:
            sems[name] = ctx.enter_context(nc.semaphore(name))
        return sems[name]

    book.sem = sem

    def sb(stack, name, shape, dt=f32):
        return stack.enter_context(nc.sbuf_tensor(name, shape, dt))

    with ctx:
        hT = sb(ctx, "hT", [P, KC, S])
        w_raw = sb(ctx, "w_raw", [P, RAW, KC * P])
        w_hi = sb(ctx, "w_hi", [P, SPLIT, KC * P], f32r)
        w_lo = sb(ctx, "w_lo", [P, SPLIT, KC * P], f32r)
        par = sb(ctx, "par", [P, pc.n])
        con = sb(ctx, "con", [P, cc.n])
        rope_t = sb(ctx, "rope_t", [P, 2, S])
        rstd = sb(ctx, "rstd", [P, S])
        mod = sb(ctx, "mod", [P, DEPTH, 3 * KC, 2])
        mod_gain = sb(ctx, "mod_gain", [P, 2, KC])
        cond = sb(ctx, "cond", [P, KC, 2])
        col = sb(ctx, "col", [P, 256])
        with ExitStack() as a1:
            a_hi = sb(a1, "a_hi", [P, KC, S], f32r)
            a_lo = sb(a1, "a_lo", [P, KC, S], f32r)
            tmp = sb(a1, "tmp", [P, KC, S])
            with ExitStack() as a1n:
                sq = sb(a1n, "sq", [P, 2, S])
                sqacc = sb(a1n, "sqacc", [P, S])
                spread = sb(a1n, "spread", [P, S])
            mod_raw = sb(a1, "mod_raw", [P, 2, KC * P])
        with ExitStack() as a2:
            x_inv = sb(a2, "x_inv", [P, TT, S])
            xt_inv = sb(a2, "xt_inv", [P, TT, S])
            at_mat = sb(a2, "at_mat", [P, TT, S])
            rel_t = sb(a2, "rel_t", [P, TT, S])
        with ExitStack() as a3:
            b_hi = sb(a3, "b_hi", [P, KC, S + M], f32r)
            b_lo = sb(a3, "b_lo", [P, KC, S + M], f32r)
        with ExitStack() as a4:
            d_s = sb(a4, "d_s", [P, 2, S + M])
            d_pt = sb(a4, "d_pt", [P, 6, S])
            d_bias = sb(a4, "d_bias", [P, 2, 15 * GW])
            col_mask = sb(a4, "col_mask", [P, GW])
        top = ExitStack()
        ctx.enter_context(top)
        sb(top, "region_a", [P, KC * (S + M) * 2 + KC * M])
        with ExitStack() as u1:
            g_qkv = sb(u1, "g_qkv", [P, 12, S])
            g_gate = sb(u1, "g_gate", [P, GH, S])
            with ExitStack() as u1a:
                a_qk = sb(u1a, "a_qk", [P, 4, S])
                a_v = sb(u1a, "a_v", [P, 2, S])
                cv_in = sb(u1a, "cv_in", [P, 3, S])
                a_vt = sb(u1a, "a_vt", [P, TT, AH * AD])
                s_buf = sb(u1a, "s_buf", [P, 2, S])
                p_t = sb(u1a, "p_t", [P, TT, S])
                cmask = sb(u1a, "cmask", [P, S])
                pad = sb(u1a, "pad", [P, 2, S + 8])
                acc = sb(u1a, "acc", [P, 2, S])
                pos = sb(u1a, "pos", [P, S], i32)
                ab = sb(u1a, "ab", [8, S])
            with ExitStack() as u1b:
                attn_t = sb(u1b, "attn_t", [P, TT, S])
                k_dec = sb(u1b, "k_dec", [P, TT, S])
                v_beta = sb(u1b, "v_beta", [P, TT, S])
                dec = sb(u1b, "dec", [P, TT, S])
                state = sb(u1b, "state", [P, 2, S])
                yv = sb(u1b, "yv", [P, 4, S])
                o_t = sb(u1b, "o_t", [P, GH, S])
            with ExitStack() as u1c:
                y_mix = sb(u1c, "y_mix", [P, KC, S])
        with ExitStack() as u2:
            xq = sb(u2, "xq", [P, KC, S])
            xk = sb(u2, "xk", [P, KC, M])
            xv = sb(u2, "xv", [P, KC, M])
            y_x = sb(u2, "y_x", [P, KC, S])
            m_in = sb(u2, "m_in", [P, KC, M])
            m_hi = sb(u2, "m_hi", [P, KC, M], f32r)
            m_lo = sb(u2, "m_lo", [P, KC, M], f32r)
            xvt = sb(u2, "xvt", [P, MT, D])
            x_s = sb(u2, "x_s", [P, 2, M])
            x_pt = sb(u2, "x_pt", [P, MT, S])
        with ExitStack() as u3:
            f_hi = sb(u3, "f_hi", [P, FC, S], f32r)
            f_lo = sb(u3, "f_lo", [P, FC, S], f32r)
        with ExitStack() as u4:
            cT = sb(u4, "cT", [P, KC, M])
            with ExitStack() as u5:
                e_q = sb(u5, "e_q", [P, 2 * CC, S + M])
                e_kd = sb(u5, "e_kd", [P, 4, S + M])
                e_vt = sb(u5, "e_vt", [P, 6, 2 * P])
                bmask = sb(u5, "bmask", [P, 3 * P])
                e_t = sb(u5, "e_t", [P, 2, S + M])
                with ExitStack() as u5a:
                    e_s = sb(u5a, "e_s", [P, 2, S + M])
                    e_pt = sb(u5a, "e_pt", [P, 6, S])
                with ExitStack() as u5b:
                    e_raw = sb(u5b, "e_raw", [P, 4, S + M])
            with ExitStack() as u6:
                d_k = sb(u6, "d_k", [P, CC, S + M])
                d_vt = sb(u6, "d_vt", [P, 6, 4 * P])
                d_q = sb(u6, "d_q", [P, CC, S])
                d_g = sb(u6, "d_g", [P, CC, S])
                c_g = sb(u6, "c_g", [P, CC, S])
                c_u = sb(u6, "c_u", [P, CC, S + CT - 1])
                c_y = sb(u6, "c_y", [P, CC, S])
                d_v = sb(u6, "d_v", [P, CC, S + M])
        banks = [ctx.enter_context(nc.psum_tensor(f"bank{i}", [P, 512], f32)) for i in range(BANKS)]

        def C(name, a=0, b=None):
            at, w = cc[name]
            return con[:, at + a:at + (w if b is None else b)]

        def G(name, c):
            return par[:, pc[name][0] + c:pc[name][0] + c + 1]

        def head(ap, h):
            return ap[:, P * h:P * h + P]

        ones, ident = C("ones"), C("ident")
        filled, freed = book.filled, book.freed

        def claim(pe, *key):
            return book.claim(pe, banks, *key)

        def bank(eng, *key):
            return book.bank(eng, banks, *key)

        tiles = book.known.tiles if book.known else UNROLL * 2
        turns = tiles // UNROLL

        def load_tile(sp, t, slot, first):
            if not first:
                sp.wait_ge(sem("w_split"), t - (RAW - 1))
            sp.dma_start(w_raw[:, slot, :], dram["w_tiles"][t]).then_inc(sem(f"w_loaded{slot}"), 16)

        def load_weights(sp):
            for t in range(RAW):
                load_tile(sp, t, t, True)
            with sp.Fori(1, tiles // RAW, 1) as n:
                for s in range(RAW):
                    load_tile(sp, n * RAW + s, s, False)
            for t in range(RAW * (tiles // RAW), tiles):
                load_tile(sp, t, t % RAW, False)

        def split_tile(pool, t, uses, raw, slot, first):
            pool.wait_ge(sem(f"w_loaded{raw}"), 16 * uses)
            if not first:
                pool.wait_ge(sem("w_used"), t - (SPLIT - 1))
            zero = C("zero").broadcast_to([P, KC * P])
            nc.gpsimd.tensor_tensor(w_hi[:, slot, :], w_raw[:, raw, :], zero, ALU.add).then_inc(sem("w_rounded"), 1)
            pool.wait_ge(sem("w_rounded"), t + 1)
            nc.gpsimd.tensor_tensor(w_lo[:, slot, :], w_raw[:, raw, :], w_hi[:, slot, :].bitcast(f32),
                                    ALU.subtract).then_inc(sem("w_split"), 1)

        def split_weights(pool):
            pool.wait_ge(*when("params", 1))
            for t in range(UNROLL):
                split_tile(pool, t, t // RAW + 1, t % RAW, t % SPLIT, t < SPLIT)
            with pool.Fori(1, turns, 1) as n:
                for s in range(UNROLL):
                    split_tile(pool, n * UNROLL + s, n * SPLIT + s // RAW + 1, s % RAW, s % SPLIT, False)
            for t in range(turns * UNROLL, tiles):
                split_tile(pool, t, t // RAW + 1, t % RAW, t % SPLIT, False)

        blocks = [0]

        def product(pe, key, inputs, kc=KC, width=P, need=None):
            outs = [claim(pe, name, *key) for name, _, _, _ in inputs]
            for k in range(kc):
                t, b = divmod(blocks[0], KC)
                if b == 0:
                    pe.wait_ge(sem("w_split"), t + 1)
                if need:
                    for event in need(k):
                        pe.wait_ge(*when(*event))
                wh = w_hi[:, t % SPLIT, b * P:b * P + width]
                wl = w_lo[:, t % SPLIT, b * P:b * P + width]
                for i, (name, hi, lo, n) in enumerate(inputs):
                    o = outs[i][:width, :n]
                    pe.matmul(o, wh, hi[:, k, :n], start=k == 0, stop=False)
                    pe.matmul(o, wh, lo[:, k, :n], start=False, stop=False)
                    mm = pe.matmul(o, wl, hi[:, k, :n], start=False, stop=k == kc - 1)
                    last = i == len(inputs) - 1
                    if k == kc - 1 and not last:
                        mm.then_inc(*filled(name, *key))
                if b == KC - 1:
                    mm.then_inc(*book.tile_used(*((name, *key) if k == kc - 1 else ())))
                elif k == kc - 1:
                    mm.then_inc(*filled(name, *key))
                blocks[0] += 1

        def pre_norm_act(act, key, gain, src, hi, n, sources, after=(), between=None):
            for c in range(KC):
                act.wait_ge(*when(*sources(c)))
                if c == 0:
                    for event in after:
                        act.wait_ge(*when(*event))
                act.activation(hi[:, c, :n], src[:, c, :n], ACT.Copy, scale=G(gain, c)).then_inc(*done("hi", *key, c))
            squares_act(act, key, lambda c: src[:, c, :n], n)
            if between:
                between()
            rms_act(act, key, n)

        def squares_act(act, key, src, n, wait=None):
            for c in range(KC):
                if wait:
                    act.wait_ge(*when(*wait(c)))
                if c >= 2:
                    act.wait_ge(*when("sq_added", *key, c - 2))
                act.activation(sq[:, c % 2, :n], src(c), ACT.Square).then_inc(*done("sq", *key, c))

        def rms_act(act, key, n, scale=1.0 / D):
            b = bank(act, "ssq", *key)
            act.activation(col[:, 0:n // P], b[:, 0:n // P], ACT.Sqrt, bias=C("eps"), scale=scale)\
               .then_inc(*freed("ssq", *key, also=("rms", *key)))

        def rstd_act(act, key, n):
            b = bank(act, "rstd", *key)
            act.activation(rstd[:, :n], b[:, :n], ACT.Copy).then_inc(*freed("rstd", *key, also=("rstd_in", *key)))

        def sum_squares_dve(dve, key, n):
            for c in range(KC):
                dve.wait_ge(*when("sq", *key, c))
                if c == 0:
                    op = dve.tensor_copy(sqacc[:, :n], sq[:, 0, :n])
                else:
                    dve.wait_ge(*when("sq_added", *key, c - 1))
                    op = dve.tensor_tensor(sqacc[:, :n], sqacc[:, :n], sq[:, c % 2, :n], ALU.add)
                op.then_inc(*done("sq_added", *key, c))

        def spread_dve(dve, key, n):
            m = n // P
            dve.wait_ge(*when("rms", *key))
            dve.reciprocal(col[:, 4:4 + m], col[:, 0:m]).then_inc(*done("rrms", *key))
            dve.wait_ge(*when("rrms", *key))
            for t in range(m):
                op = dve.tensor_scalar(spread[:, P * t:P * t + P], ident, col[:, 4 + t:5 + t], None, ALU.mult)
            op.then_inc(*done("spread", *key))

        def pre_norm_dve(dve, key, gain, src, hi, lo, n):
            for c in range(KC):
                dve.wait_ge(*when("hi", *key, c))
                dve.scalar_tensor_tensor(out=lo[:, c, :n], in0=src[:, c, :n], scalar=G(gain, c),
                                         in1=hi[:, c, :n].bitcast(f32), op0=ALU.mult, op1=ALU.subtract)\
                   .then_inc(*done("lo", *key, c))
            sum_squares_dve(dve, key, n)
            spread_dve(dve, key, n)

        def post_norm_act(act, key, y):
            for c in range(KC):
                b = bank(act, "y", *key, c)
                act.activation(y[:, c, :], b[:, :], ACT.Copy).then_inc(*freed("y", *key, c, also=("y_in", *key, c)))
                act.wait_ge(*when("y_in", *key, c))
                if c >= 2:
                    act.wait_ge(*when("sq_added", *key, c - 2))
                act.activation(sq[:, c % 2, :], y[:, c, :], ACT.Square).then_inc(*done("sq", *key, c))
            rms_act(act, key, S)

        def post_norm_dve(dve, key, gain, y):
            sum_squares_dve(dve, key, S)
            spread_dve(dve, key, S)
            post_apply_dve(dve, key, gain, y)

        def post_apply_dve(dve, key, gain, y):
            b = bank(dve, "rstd", *key)
            for c in range(KC):
                dve.scalar_tensor_tensor(out=y[:, c, :], in0=y[:, c, :], scalar=G(gain, c), in1=b[:, :],
                                         op0=ALU.mult, op1=ALU.mult)\
                   .then_inc(*(freed("rstd", *key, also=("y_normed", *key, c)) if c == KC - 1
                               else done("y_normed", *key, c)))
            for c in range(KC):
                dve.wait_ge(*when("y_normed", *key, c))
                dve.tensor_tensor(hT[:, c, :], hT[:, c, :], y[:, c, :], ALU.add).then_inc(*done("h", *key, c))

        def split_act(act, src, c, key, n=S, hi=None):
            act.activation((a_hi if hi is None else hi)[:, c, :n], src, ACT.Copy).then_inc(*done("hi", *key, c))

        def split_dve(dve, src, c, key, n=S, hi=None, lo=None):
            dve.wait_ge(*when("hi", *key, c))
            dve.tensor_tensor((a_lo if lo is None else lo)[:, c, :n], src,
                              (a_hi if hi is None else hi)[:, c, :n].bitcast(f32), ALU.subtract)\
               .then_inc(*done("lo", *key, c))

        def inputs_ready(key):
            return lambda k: [("hi", *key, k), ("lo", *key, k)]

        def att_scores_pe(pe, key, u, unit):
            for i, (k0, nk, mms, _) in enumerate(unit["parts"]):
                b = claim(pe, "s", *key, u, i)
                for j, (q, k) in enumerate(mms):
                    mm = pe.matmul(b[:, :nk], q, k, start=j == 0, stop=j == len(mms) - 1)
                mm.then_inc(*filled("s", *key, u, i))

        def att_turn_pe(pe, key, u, unit, s):
            pe.wait_ge(*when("p", *key, u))
            c = 0
            for i, (k0, nk, _, _) in enumerate(unit["parts"]):
                b = claim(pe, "pt", *key, u, i)
                for j in range(nk // P):
                    mm = pe.transpose(b[:, P * j:P * j + P], s[:, u % 2, c:c + P], ident)
                    c += P
                mm.then_inc(*filled("pt", *key, u, i))

        def att_values_pe(pe, key, units, us, pt, vt):
            for u in us:
                for i in range(len(units[u]["parts"])):
                    pe.wait_ge(*when("pt_in", *key, u, i))
            head_no = units[us[0]]["head"]
            spans = {}
            for u in us:
                for k0, nk, _, _ in units[u]["parts"]:
                    for kt in range(k0 // P, (k0 + nk) // P):
                        q0 = units[u]["q0"]
                        lo, hi = spans.get(kt, (q0, q0))
                        spans[kt] = (min(lo, q0), max(hi, q0 + P))
            order = sorted(spans, key=lambda kt: spans[kt][0] - spans[kt][1])
            base = units[us[0]]["q0"]
            for o in range(len(vt(0, head_no))):
                b = claim(pe, "o", *key, us[-1], o)
                for n, kt in enumerate(order):
                    lo, hi = spans[kt]
                    v = vt(kt, head_no)[o]
                    mm = pe.matmul(b[:v.shape[-1], lo - base:hi - base], v, pt[:, kt, lo - base:hi - base],
                                   start=n == 0, stop=n == len(order) - 1, skip_group_check=True)
                mm.then_inc(*filled("o", *key, us[-1], o))

        def head_end(units, u):
            return u == len(units) - 1 or units[u + 1]["group"] != units[u]["group"]

        def group_of(units, u):
            return [v for v in range(u + 1) if units[v]["group"] == units[u]["group"]]

        def attention_pe(pe, key, units, s, pt, vt, need=()):
            for event in need:
                pe.wait_ge(*when(*event))
            pending = None
            for u in range(len(units) + 2):
                if u < len(units):
                    att_scores_pe(pe, key, u, units[u])
                if pending is not None:
                    att_values_pe(pe, key, units, group_of(units, pending), pt, vt)
                    pending = None
                if 1 <= u <= len(units):
                    att_turn_pe(pe, key, u - 1, units[u - 1], s)
                    if head_end(units, u - 1):
                        pending = u - 1

        def att_col(u, i):
            return col[:, 16 + 8 * (u % 2) + i:17 + 8 * (u % 2) + i]

        def attention_dve(dve, key, units, s, before=None):
            def maxima(u):
                parts = units[u]["parts"]
                if u >= 2:
                    dve.wait_ge(*when("bank_filled", "pt", *key, u - 2, len(units[u - 2]["parts"]) - 1))
                c = 0
                for i, (k0, nk, _, mask) in enumerate(parts):
                    b = bank(dve, "s", *key, u, i)
                    m = C("zero").broadcast_to([P, nk]) if mask is None else mask
                    if i:
                        dve.wait_ge(*when("s_in", *key, u, i - 1))
                    first = units[u]["sink"] if units[u].get("sink") is not None else -3.0e38
                    dve.tensor_tensor_reduce(s[:, u % 2, c:c + nk], b[:, :nk], m, 1.0,
                                             att_col(u, i - 1) if i else first, ALU.add, ALU.max,
                                             att_col(u, i))\
                       .then_inc(*freed("s", *key, u, i, also=("s_in", *key, u, i)))
                    c += nk
                dve.wait_ge(*when("s_in", *key, u, len(parts) - 1))
                if u >= 2:
                    dve.wait_ge(*when("p", *key, u - 2))
                dve.tensor_scalar(att_col(u, 2), att_col(u, len(parts) - 1), -1.0, None, ALU.mult)\
                   .then_inc(*done("max", *key, u))

            def divide(u):
                n = sum(nk for _, nk, _, _ in units[u]["parts"])
                dve.wait_ge(*when("exp", *key, u))
                if units[u].get("sink") is not None:
                    dve.tensor_tensor(att_col(u, 3), att_col(u, 3), att_col(u, 5), ALU.add)\
                       .then_inc(*done("sum_sink", *key, u))
                    dve.wait_ge(*when("sum_sink", *key, u))
                dve.reciprocal(att_col(u, 4), att_col(u, 3)).then_inc(*done("rsum", *key, u))
                dve.wait_ge(*when("rsum", *key, u))
                dve.tensor_scalar(s[:, u % 2, :n], s[:, u % 2, :n], att_col(u, 4), None, ALU.mult)\
                   .then_inc(*done("p", *key, u))

            for u in range(len(units) + 1):
                if u < len(units):
                    if before:
                        before(u)
                    maxima(u)
                if u:
                    divide(u - 1)

        def attention_act(act, key, units, s, pt, take):
            pending, last_out = None, None
            for u in range(len(units) + 2):
                if u < len(units):
                    n = sum(nk for _, nk, _, _ in units[u]["parts"])
                    act.wait_ge(*when("max", *key, u))
                    if units[u].get("sink") is not None:
                        act.activation(att_col(u, 5), units[u]["sink"], ACT.Exp, bias=att_col(u, 2))\
                           .then_inc(*done("exp_sink", *key, u))
                    act.activation(s[:, u % 2, :n], s[:, u % 2, :n], ACT.Exp, bias=att_col(u, 2),
                                   accum_out=att_col(u, 3)).then_inc(*done("exp", *key, u))
                if pending is not None:
                    take(act, pending)
                    last_out, pending = pending, None
                if 1 <= u <= len(units):
                    unit = units[u - 1]
                    for i, (k0, nk, _, _) in enumerate(unit["parts"]):
                        b = bank(act, "pt", *key, u - 1, i)
                        base = units[group_of(units, u - 1)[0]]["q0"]
                        q0 = unit["q0"] - base
                        act.activation(pt[:, k0 // P:(k0 + nk) // P, q0:q0 + P],
                                       b[:, :nk].rearrange("p (k q) -> p k q", q=P), ACT.Copy)\
                           .then_inc(*freed("pt", *key, u - 1, i, also=("pt_in", *key, u - 1, i)))
                    if head_end(units, u - 1):
                        pending = u - 1

        JOBS = in_jobs()
        GDN = [n for n, _, _ in JOBS if n[:2] in ("gk", "gq", "gv")]

        def g_index(name):
            return 3 * int(name[2]) + {"gq": 0, "gk": 1, "gv": 2}[name[:2]]

        def conv_index(name):
            return int(name[2]) + {"gq": 0, "gk": 4, "gv": 8}[name[:2]]

        def att_units(l):
            units = []
            for h in range(AH):
                lo = AD * (h % 2)
                for t in range(TT):
                    q = a_qk[lo:lo + AD, 2 * (h // 2), P * t:P * t + P]
                    k = a_qk[lo:lo + AD, 2 * (h // 2) + 1, 0:P * (t + 1)]
                    units.append({"head": h, "group": h, "q0": P * t,
                                  "parts": [(0, P * (t + 1), [(q, k)], cmask[:, P * (TT - 1 - t):S])]})
            return units

        def in_product_pe(pe, l):
            for i, (name, _, width) in enumerate(JOBS):
                product(pe, (l,), [(name, a_hi, a_lo, S)], width=width,
                        need=inputs_ready(("mix", l)) if i == 0 else None)
                if i == 0:
                    ssq_pe(pe, ("mix", l), S)
                if i == 2:
                    rstd_pe(pe, ("mix", l), S)

        def in_product_dve(dve, l):
            for r in range(2):
                dve.memset(pad[:, r, 0:GK - 1], 0.0).then_inc(*done("pad_zero", l, r))
            dve.wait_ge(*when("pad_zero", l, 1))
            dve.wait_ge(*when("rstd_in", "mix", l))
            for name, _, width in JOBS:
                b = bank(dve, name, l)
                kind = name[:2]
                if name in GDN:
                    i = GDN.index(name)
                    x, y, w = pad[:, i % 2, :], acc[:, i % 2, :], conv_index(name) * GK
                    dve.tensor_tensor(x[:, GK - 1:GK - 1 + S], b[:, :], rstd[:, :], ALU.mult)\
                       .then_inc(*freed(name, l, also=("conv_in", l, i)))
                    dve.wait_ge(*when("conv_in", l, i))
                    if i >= 2:
                        dve.wait_ge(*when("silu", l, i - 2))
                    for j in range(GK):
                        tap = G(f"conv_gdn{l}", w + j)
                        if j == 0:
                            op = dve.tensor_scalar(y, x[:, 0:S], tap, None, ALU.mult)
                        else:
                            dve.wait_ge(*when("tap", l, i, j - 1))
                            op = dve.scalar_tensor_tensor(out=y, in0=x[:, j:j + S], scalar=tap, in1=y,
                                                          op0=ALU.mult, op1=ALU.add)
                        op.then_inc(*done("tap", l, i, j))
                elif kind == "ab":
                    dve.tensor_tensor(ab[:, :], b[0:2 * GH, :], rstd[0:2 * GH, :], ALU.mult)\
                       .then_inc(*freed(name, l, also=("ab_in", l)))
                elif kind in ("aq", "ak"):
                    c = int(name[2])
                    dve.scalar_tensor_tensor(out=a_qk[:, 2 * c + (kind == "ak"), :], in0=b[:, :],
                                             scalar=AD ** -0.5 if kind == "aq" else 1.0, in1=rstd[:, :],
                                             op0=ALU.mult, op1=ALU.mult)\
                       .then_inc(*freed(name, l, also=("qk_in", l, 2 * c + (kind == "ak"))))
                elif kind == "av":
                    dve.tensor_tensor(a_v[:, int(name[2]), :], b[:, :], rstd[:, :], ALU.mult)\
                       .then_inc(*freed(name, l, also=("av_in", l, int(name[2]))))
                elif kind in ("cg", "cx", "cb"):
                    j = ("cg", "cx", "cb").index(kind)
                    if j == 0 and name[2] == "1":
                        dve.wait_ge(*when("short", l, 0))
                    dve.tensor_tensor(cv_in[:, j, :], b[:, :], rstd[:, :], ALU.mult)\
                       .then_inc(*freed(name, l, also=(kind, l, int(name[2]))))
                    if kind == "cb":
                        short_conv_dve(dve, l, int(name[2]))
                elif kind == "gg":
                    dve.tensor_tensor(g_gate[:, int(name[2]), :], b[:, :], rstd[:, :], ALU.mult)\
                       .then_inc(*freed(name, l, also=("gate_in", l, int(name[2]))))

        def short_conv_dve(dve, l, c):
            x, y = pad[:, c, :], acc[:, c, :]
            dve.wait_ge(*when("cx", l, c))
            dve.wait_ge(*when("silu", l, len(GDN) - 1))
            dve.tensor_tensor(x[:, GK - 1:GK - 1 + S], cv_in[:, 0, :], cv_in[:, 1, :], ALU.mult)\
               .then_inc(*done("short_in", l, c))
            dve.wait_ge(*when("short_in", l, c))
            for j in range(CK):
                tap = G(f"conv_short{l}", CK * c + j)
                xs = x[:, GK - CK + j:GK - CK + j + S]
                if j == 0:
                    op = dve.tensor_scalar(y, xs, tap, None, ALU.mult)
                else:
                    dve.wait_ge(*when("short_tap", l, c, j - 1))
                    op = dve.scalar_tensor_tensor(out=y, in0=xs, scalar=tap, in1=y, op0=ALU.mult, op1=ALU.add)
                op.then_inc(*done("short_tap", l, c, j))
            dve.wait_ge(*when("short_tap", l, c, CK - 1))
            dve.wait_ge(*when("cb", l, c))
            dve.tensor_tensor(tmp[:, 2 + c, :], cv_in[:, 2, :], y, ALU.mult).then_inc(*done("short", l, c))

        def in_product_act(act, l):
            for i, name in enumerate(GDN):
                act.wait_ge(*when("tap", l, i, GK - 1))
                act.activation(g_qkv[:, g_index(name), :], acc[:, i % 2, :], ACT.Silu).then_inc(*done("silu", l, i))
            for h in range(GH):
                act.wait_ge(*when("gate_in", l, h))
                act.activation(g_gate[:, h, :], g_gate[:, h, :], ACT.Silu).then_inc(*done("gate", l, h))

        def att_prep_pe(pe, l):
            for i in range(4):
                pe.wait_ge(*when("qk_in", l, i))
                b = claim(pe, "swap", l, i)
                pe.matmul(b[:, :], C("rope1"), a_qk[:, i, :], start=True, stop=True).then_inc(*filled("swap", l, i))
            pe.wait_ge(*when("av_in", l, 0))
            pe.wait_ge(*when("av_in", l, 1))
            for g in range(2):
                b = claim(pe, "avt", l, g)
                for t in range(2):
                    for c in range(2):
                        mm = pe.transpose(b[:, P * (2 * t + c):P * (2 * t + c) + P],
                                          a_v[:, c, P * (2 * g + t):P * (2 * g + t) + P], ident)
                mm.then_inc(*filled("avt", l, g))

        def att_prep_dve(dve, l):
            dve.wait_ge(*when("rope_table", 1))
            for i in range(4):
                b = bank(dve, "swap", l, i)
                dve.tensor_tensor(s_buf[:, i % 2, :], b[:, :], rope_t[:, 1, :], ALU.mult)\
                   .then_inc(*freed("swap", l, i, also=("swapped", l, i)))
                dve.tensor_tensor(a_qk[:, i, :], a_qk[:, i, :], rope_t[:, 0, :], ALU.mult)\
                   .then_inc(*done("cos_part", l, i))
                dve.wait_ge(*when("swapped", l, i))
                dve.wait_ge(*when("cos_part", l, i))
                dve.tensor_tensor(a_qk[:, i, :], a_qk[:, i, :], s_buf[:, i % 2, :], ALU.add)\
                   .then_inc(*done("roped", l, i))
            dve.wait_ge(*when("roped", l, 3))

        def att_prep_act(act, l):
            act.dma_start(cmask[:, :], dram["count_mask"]).then_inc(*loaded("cmask", l))
            for g in range(2):
                b = bank(act, "avt", l, g)
                act.activation(a_vt[:, 2 * g:2 * g + 2, :], b[:, :].rearrange("p (t n) -> p t n", t=2), ACT.Copy)\
                   .then_inc(*freed("avt", l, g, also=("avt_in", l, g)))

        def att_take_act(l):
            def take(act, u):
                h = u // TT
                b = bank(act, "o", "att", l, u, 0)
                act.activation(tmp[AD * (h % 2):AD * (h % 2) + AD, h // 2, :], b[0:AD, :], ACT.Copy)\
                   .then_inc(*freed("o", "att", l, u, 0, also=("att_out", l, h)))
            return take

        def ssq_pe(pe, key, n):
            pe.wait_ge(*when("sq_added", *key, KC - 1))
            b = claim(pe, "ssq", *key)
            for t in range(n // P):
                mm = pe.matmul(b[:, t:t + 1], sqacc[:, P * t:P * t + P], ones[:, 0:1], start=True, stop=True)
            mm.then_inc(*filled("ssq", *key))

        def rstd_pe(pe, key, n):
            pe.wait_ge(*when("spread", *key))
            b = claim(pe, "rstd", *key)
            pe.matmul(b[:, :n], ones, spread[:, :n], start=True, stop=True).then_inc(*filled("rstd", *key))

        AB, Z, EX, GL, BE, L2, DC, CD, KD, NB, NA = 32, 64, 80, 96, 112, 128, 160, 192, 208, 224, 240
        NH = TT * GH

        def cols(at, n=NH):
            return col[:, at:at + n]

        def colnh(at, n, h):
            return col[:, at + GH * n + h:at + GH * n + h + 1]

        def by_head(first, n):
            return g_qkv[:, first:12:3, P * n:P * n + P]

        def banked(b):
            return b[:, :].rearrange("p (h n) -> p h n", h=GH)

        def over_heads(ap):
            return ap[:, None, :].broadcast_to([P, GH, P])

        ROWS = ("decay", "rk", "rq", "beta")

        def gdn_pe(pe, l):
            b = claim(pe, "l2", l)
            for i in range(2 * GH):
                pe.wait_ge(*when("l2_sq", l, i))
                w, h = divmod(i, GH)
                for n in range(TT):
                    at = NH * w + GH * n + h
                    mm = pe.matmul(b[:, at:at + 1], tmp[:, 4 + i % 4, P * n:P * n + P], ones[:, 0:1],
                                   start=True, stop=True)
                mm.then_inc(*(filled("l2", l) if i == 2 * GH - 1 else done("l2_mm", l, i)))
            pe.wait_ge(*when("ab_in", l))
            b = claim(pe, "abt", l)
            for n in range(TT):
                mm = pe.transpose(b[:, 8 * n:8 * n + 8], ab[0:8, P * n:P * n + P], ident[0:8, 0:8])
            mm.then_inc(*filled("abt", l))
            pe.wait_ge(*when("g", l))
            b = claim(pe, "decay", l)
            pe.matmul(b[:, 0:NH], C("upto"), cols(GL), start=True, stop=True)
            pe.matmul(b[:, NH:2 * NH], ones, cols(GL), start=True, stop=True).then_inc(*filled("decay", l))
            for n in range(TT):
                for w, name in enumerate(ROWS):
                    pe.wait_ge(*when("diag", l, n, w))
                    b = claim(pe, "row", l, n, w)
                    pe.matmul(b[:, :], ones, (spread if w % 2 == 0 else sqacc)[:, :], start=True, stop=True)\
                      .then_inc(*filled("row", l, n, w))
            for n in range(TT):
                pe.wait_ge(*when("normed", l, n, 0))
                pe.wait_ge(*when("normed", l, n, 1))
                tok = slice(P * n, P * n + P)
                b = claim(pe, "kk", l, n)
                for h in range(GH):
                    k = g_qkv[:, 3 * h + 1, tok]
                    mm = pe.matmul(head(b, h), k, k, start=True, stop=True)
                mm.then_inc(*filled("kk", l, n))
                b = claim(pe, "kq", l, n)
                for h in range(GH):
                    mm = pe.matmul(head(b, h), g_qkv[:, 3 * h + 1, tok], g_qkv[:, 3 * h, tok], start=True, stop=True)
                mm.then_inc(*filled("kq", l, n))
                for name, j in (("kt", 1), ("vt", 2)):
                    b = claim(pe, name, l, n)
                    for h in range(GH):
                        mm = pe.transpose(head(b, h), g_qkv[:, 3 * h + j, tok], ident)
                    mm.then_inc(*filled(name, l, n))
            for n in range(TT):
                pe.wait_ge(*when("xt", l, 0, n))
                b = claim(pe, "x1", l, n)
                for h in range(GH):
                    mm = pe.transpose(head(b, h), head(xt_inv[:, n, :], h), ident)
                mm.then_inc(*filled("x1", l, n))
            for s in range(1, 7):
                for n in range(TT):
                    pe.wait_ge(*when("level", l, s, n))
                    pe.wait_ge(*when("x", l, s - 1, n))
                    b = claim(pe, "y", l, s, n)
                    for h in range(GH):
                        mm = pe.matmul(head(b, h), head(tmp[:, 4 + n, :], h), head(x_inv[:, n, :], h),
                                       start=True, stop=True)
                    mm.then_inc(*filled("y", l, s, n))
                for n in range(TT):
                    pe.wait_ge(*when("y_in", l, s, n))
                    pe.wait_ge(*when("xt", l, s - 1, n))
                    if s < 6:
                        b = claim(pe, "px", l, s, n)
                        for h in range(GH):
                            mm = pe.matmul(head(b, h), head(xt_inv[:, n, :], h), head(yv[:, n, :], h),
                                           start=True, stop=True)
                        mm.then_inc(*filled("px", l, s, n))
                    b = claim(pe, "pxt", l, s, n)
                    for h in range(GH):
                        mm = pe.matmul(head(b, h), head(yv[:, n, :], h), head(xt_inv[:, n, :], h),
                                       start=True, stop=True)
                    mm.then_inc(*filled("pxt", l, s, n))
            for n in range(TT):
                tok = slice(P * n, P * n + P)
                st = state[:, (n - 1) % 2, :]
                if n:
                    pe.wait_ge(*when("state", l, n - 1))
                    b = claim(pe, "ks", l, n)
                    for h in range(GH):
                        mm = pe.matmul(head(b, h), g_qkv[:, 3 * h + 1, tok], head(st, h), start=True, stop=True)
                    mm.then_inc(*filled("ks", l, n))
                    pe.wait_ge(*when("rhs", l, n))
                else:
                    pe.wait_ge(*when("vbeta", l, 0))
                pe.wait_ge(*when("xt", l, 6, n))
                rhs = yv[:, n % 2, :] if n else v_beta[:, 0, :]
                b = claim(pe, "vn", l, n)
                for h in range(GH):
                    mm = pe.matmul(head(b, h), head(xt_inv[:, n, :], h), head(rhs, h), start=True, stop=True)
                mm.then_inc(*filled("vn", l, n))
                pe.wait_ge(*when("vn_in", l, n))
                vn = yv[:, 2 + n % 2, :]
                if n < TT - 1:
                    b = claim(pe, "su", l, n)
                    for h in range(GH):
                        mm = pe.matmul(head(b, h), head(k_dec[:, n, :], h), head(vn, h), start=True, stop=True)
                    mm.then_inc(*filled("su", l, n))
                pe.wait_ge(*when("q_dec", l, n))
                b = claim(pe, "go", l, n)
                for h in range(GH):
                    if n:
                        pe.matmul(head(b, h), head(st, h), g_qkv[:, 3 * h, tok], start=True, stop=False)
                    mm = pe.matmul(head(b, h), head(vn, h), head(attn_t[:, n, :], h), start=n == 0, stop=True)
                mm.then_inc(*filled("go", l, n))
            b = claim(pe, "l2o", l)
            for h in range(GH):
                pe.wait_ge(*when("o_sq", l, h))
                for n in range(TT):
                    mm = pe.matmul(b[:, GH * n + h:GH * n + h + 1], tmp[:, 4 + h, P * n:P * n + P], ones[:, 0:1],
                                   start=True, stop=True)
            mm.then_inc(*filled("l2o", l))
            for n in range(TT):
                pe.wait_ge(*when("o_diag", l, n))
                b = claim(pe, "o_row", l, n)
                pe.matmul(b[:, :], ones, (spread if n % 2 == 0 else sqacc)[:, :], start=True, stop=True)\
                  .then_inc(*filled("o_row", l, n))

        def gdn_act(act, l):
            for i in range(2 * GH):
                w, h = divmod(i, GH)
                if i == 0:
                    act.wait_ge(*when("silu", l, len(GDN) - 1))
                if i >= 4:
                    act.wait_ge(*when("l2_mm", l, i - 4))
                act.activation(tmp[:, 4 + i % 4, :], g_qkv[:, 3 * h + w, :], ACT.Square).then_inc(*done("l2_sq", l, i))
            act.wait_ge(*when("abs_z", l))
            act.activation(cols(EX), cols(EX), ACT.Exp, scale=-1.0).then_inc(*done("exp_z", l))
            act.activation(cols(BE).rearrange("p (n h) -> p n h", h=GH),
                           cols(AB, 2 * NH).rearrange("p (n h) -> p n h", h=2 * GH)[:, :, GH:2 * GH],
                           ACT.Exp, scale=-1.0).then_inc(*done("exp_b", l))
            act.activation(cols(NA, GH), par[:, pc[f"a_log{l}"][0]:pc[f"a_log{l}"][0] + GH], ACT.Exp)\
               .then_inc(*done("exp_a", l))
            act.wait_ge(*when("exp_z", l))
            act.activation(cols(EX), cols(EX), ACT.Ln, bias=ones[:, 0:1]).then_inc(*done("ln_z", l))
            act.wait_ge(*when("kd", l))
            act.activation(cols(CD), cols(DC + NH), ACT.Exp).then_inc(*done("chunk_decay", l))
            act.activation(cols(KD), cols(KD), ACT.Exp).then_inc(*done("k_decay", l))
            act.activation(cols(NB), cols(DC), ACT.Exp).then_inc(*done("exp_d", l))
            b = bank(act, "l2", l)
            act.activation(cols(L2), b[:, 0:NH], ACT.Sqrt, bias=C("eps_q"), scale=float(GD)).then_inc(*done("rms_q", l))
            act.activation(cols(L2 + NH), b[:, NH:2 * NH], ACT.Sqrt, bias=C("eps"))\
               .then_inc(*freed("l2", l, also=("rms_k", l)))
            for n in range(TT):
                b = bank(act, "row", l, n, 0)
                act.activation(dec[:, n, :], b[:, :], ACT.Exp).then_inc(*done("dec", l, n))
                act.wait_ge(*when("rel_in", l, n))
                act.activation(rel_t[:, n, :], rel_t[:, n, :], ACT.Exp).then_inc(*done("rel", l, n))
            for n in range(TT):
                act.wait_ge(*when("k_decay", l))
                b = bank(act, "kt", l, n)
                for h in range(GH):
                    op = act.activation(head(k_dec[:, n, :], h), head(b, h), ACT.Copy, scale=colnh(KD, n, h))
                op.then_inc(*freed("kt", l, n, also=("kdec", l, n)))
                if n == 0:
                    act.wait_ge(*when("beta", l))
                b = bank(act, "vt", l, n)
                for h in range(GH):
                    op = act.activation(head(v_beta[:, n, :], h), head(b, h), ACT.Copy, scale=colnh(BE, n, h))
                op.then_inc(*freed("vt", l, n, also=("vbeta", l, n)))
            for n in range(TT):
                b = bank(act, "x1", l, n)
                act.activation(x_inv[:, n, :], b[:, :], ACT.Copy).then_inc(*freed("x1", l, n, also=("x", l, 0, n)))
            for s in range(1, 7):
                for n in range(TT):
                    if s >= 2:
                        act.wait_ge(*when("xt", l, s - 1, n))
                    b = bank(act, "y", l, s, n)
                    act.activation(yv[:, n, :], b[:, :], ACT.Copy).then_inc(*freed("y", l, s, n, also=("y_in", l, s, n)))
            for n in range(TT):
                b = bank(act, "vn", l, n)
                if n == 0:
                    act.wait_ge(*when("xt", l, 6, TT - 1))
                act.activation(yv[:, 2 + n % 2, :], b[:, :], ACT.Copy).then_inc(*freed("vn", l, n, also=("vn_in", l, n)))
                b = bank(act, "go", l, n)
                act.activation(o_t[:, :, P * n:P * n + P], banked(b), ACT.Copy)\
                   .then_inc(*freed("go", l, n, also=("o", l, n)))
            act.wait_ge(*when("o", l, TT - 1))
            for h in range(GH):
                act.activation(tmp[:, 4 + h, :], o_t[:, h, :], ACT.Square).then_inc(*done("o_sq", l, h))
            b = bank(act, "l2o", l)
            act.activation(cols(L2), b[:, 0:NH], ACT.Sqrt, bias=C("eps"), scale=1.0 / GD)\
               .then_inc(*freed("l2o", l, also=("rms_o", l)))
            for c in range(KC):
                if c == 0:
                    act.wait_ge(*when("att_out", l, AH - 1))
                    act.wait_ge(*when("short", l, 1))
                if c == 4:
                    act.wait_ge(*when("gated", l, GH - 1))
                split_act(act, tmp[:, c, :] if c < 4 else o_t[:, c - 4, :], c, ("out", l))

        def gdn_dve(dve, l):
            NHv = lambda at: cols(at).rearrange("p (n h) -> p n h", h=GH)
            b = bank(dve, "abt", l)
            dve.tensor_copy(cols(AB, 2 * NH), b[:, 0:2 * NH]).then_inc(*freed("abt", l, also=("ab_col", l)))
            dve.wait_ge(*when("ab_col", l))
            dt = par[:, pc[f"dt_bias{l}"][0]:pc[f"dt_bias{l}"][0] + GH]
            abv = cols(AB, 2 * NH).rearrange("p (n h) -> p n h", h=2 * GH)
            dve.tensor_tensor(NHv(Z), abv[:, :, 0:GH], dt[:, None, :].broadcast_to([P, TT, GH]), ALU.add)\
               .then_inc(*done("z", l))
            dve.wait_ge(*when("z", l))
            dve.scalar_tensor_tensor(out=cols(EX), in0=cols(Z), scalar=-1.0, in1=cols(Z), op0=ALU.mult, op1=ALU.max)\
               .then_inc(*done("abs_z", l))
            dve.wait_ge(*when("ln_z", l))
            dve.scalar_tensor_tensor(out=cols(GL), in0=cols(Z), scalar=0.0, in1=cols(EX), op0=ALU.max, op1=ALU.add)\
               .then_inc(*done("softplus", l))
            dve.tensor_scalar(cols(BE), cols(BE), 1.0, None, ALU.add).then_inc(*done("one_exp_b", l))
            dve.wait_ge(*when("softplus", l))
            dve.scalar_tensor_tensor(out=NHv(GL), in0=NHv(GL), scalar=-1.0,
                                     in1=cols(NA, GH)[:, None, :].broadcast_to([P, TT, GH]),
                                     op0=ALU.mult, op1=ALU.mult).then_inc(*done("g", l))
            dve.wait_ge(*when("one_exp_b", l))
            dve.reciprocal(cols(BE), cols(BE)).then_inc(*done("beta", l))
            b = bank(dve, "decay", l)
            dve.tensor_copy(cols(DC, 2 * NH), b[:, 0:2 * NH]).then_inc(*freed("decay", l, also=("decays", l)))
            dve.wait_ge(*when("decays", l))
            dve.tensor_tensor(cols(KD), cols(DC + NH), cols(DC), ALU.subtract).then_inc(*done("kd", l))
            dve.wait_ge(*when("exp_d", l))
            dve.wait_ge(*when("beta", l))
            dve.scalar_tensor_tensor(out=cols(NB), in0=cols(NB), scalar=-1.0, in1=cols(BE), op0=ALU.mult,
                                     op1=ALU.mult).then_inc(*done("neg_beta_exp_d", l))
            dve.wait_ge(*when("rms_k", l))
            dve.reciprocal(cols(L2, 2 * NH), cols(L2, 2 * NH)).then_inc(*done("l2_inv", l))
            dve.wait_ge(*when("l2_inv", l))
            sources = (GL, L2 + NH, L2, BE)

            def diag(n, w):
                i = 4 * n + w
                if i >= 2:
                    dve.wait_ge(*when("bank_filled", "row", l, (i - 2) // 4, (i - 2) % 4))
                buf = spread if w % 2 == 0 else sqacc
                for h in range(GH):
                    op = dve.tensor_scalar(head(buf[:, :], h), C("upto") if w == 0 else ident,
                                           colnh(sources[w], n, h), None, ALU.mult)
                op.then_inc(*done("diag", l, n, w))

            def rows(n, w):
                b = bank(dve, "row", l, n, w)
                if w == 0:
                    dve.wait_ge(*when("dec", l, n))
                    for h in range(GH):
                        op = dve.scalar_tensor_tensor(out=head(rel_t[:, n, :], h), in0=head(b, h),
                                                      scalar=colnh(DC, n, h), in1=C("neg_future"),
                                                      op0=ALU.subtract, op1=ALU.add)
                    op.then_inc(*freed("row", l, n, w, also=("rel_in", l, n)))
                elif w < 3:
                    x = by_head(2 - w, n)
                    dve.tensor_tensor(x, x, banked(b), ALU.mult)\
                       .then_inc(*freed("row", l, n, w, also=("normed", l, n, 2 - w)))
                else:
                    dve.tensor_copy(at_mat[:, n, :], b[:, :]).then_inc(*freed("row", l, n, w, also=("beta_row", l, n)))

            steps = [(n, w) for n in range(TT) for w in range(4)]
            for i in range(len(steps) + 1):
                if i < len(steps):
                    diag(*steps[i])
                if i:
                    rows(*steps[i - 1])
            for n in range(TT):
                dve.wait_ge(*when("rel", l, n))
                dve.wait_ge(*when("beta_row", l, n))
                dve.tensor_tensor(at_mat[:, n, :], at_mat[:, n, :], rel_t[:, n, :], ALU.mult).then_inc(*done("beta_rel", l, n))
                dve.wait_ge(*when("beta_rel", l, n))
                b = bank(dve, "kk", l, n)
                dve.tensor_tensor(at_mat[:, n, :], at_mat[:, n, :], b[:, :], ALU.mult)\
                   .then_inc(*freed("kk", l, n, also=("a", l, n)))
                b = bank(dve, "kq", l, n)
                dve.tensor_tensor(attn_t[:, n, :], rel_t[:, n, :], b[:, :], ALU.mult)\
                   .then_inc(*freed("kq", l, n, also=("attn", l, n)))
                x = by_head(0, n)
                dve.wait_ge(*when("attn", l, n))
                dve.tensor_tensor(x, x, dec[:, n, :].rearrange("p (h n) -> p h n", h=GH), ALU.mult)\
                   .then_inc(*done("q_dec", l, n))
                dve.wait_ge(*when("a", l, n))
                xt3 = xt_inv[:, n, :].rearrange("p (h n) -> p h n", h=GH)
                dve.tensor_tensor(xt3, at_mat[:, n, :].rearrange("p (h n) -> p h n", h=GH),
                                  over_heads(C("level0")), ALU.mult).then_inc(*done("level0", l, n))
                dve.wait_ge(*when("level0", l, n))
                dve.tensor_tensor(xt3, over_heads(ident), xt3, ALU.subtract).then_inc(*done("xt", l, 0, n))
            for s in range(1, 7):
                for n in range(TT):
                    if s >= 2:
                        dve.wait_ge(*when("bank_filled", "y", l, s - 1, n))
                    else:
                        dve.wait_ge(*when("a", l, n))
                    dve.tensor_tensor(tmp[:, 4 + n, :].rearrange("p (h n) -> p h n", h=GH),
                                      at_mat[:, n, :].rearrange("p (h n) -> p h n", h=GH),
                                      over_heads(C(f"level{s}")), ALU.mult).then_inc(*done("level", l, s, n))
                for n in range(TT):
                    if s < 6:
                        b = bank(dve, "px", l, s, n)
                        dve.tensor_tensor(x_inv[:, n, :], x_inv[:, n, :], b[:, :], ALU.subtract)\
                           .then_inc(*freed("px", l, s, n, also=("x", l, s, n)))
                    b = bank(dve, "pxt", l, s, n)
                    dve.tensor_tensor(xt_inv[:, n, :], xt_inv[:, n, :], b[:, :], ALU.subtract)\
                       .then_inc(*freed("pxt", l, s, n, also=("xt", l, s, n)))
            for n in range(TT):
                if n:
                    b = bank(dve, "ks", l, n)
                    for h in range(GH):
                        op = dve.scalar_tensor_tensor(out=head(yv[:, n % 2, :], h), in0=head(b, h),
                                                      scalar=colnh(NB, n, h), in1=head(v_beta[:, n, :], h),
                                                      op0=ALU.mult, op1=ALU.add)
                    op.then_inc(*freed("ks", l, n, also=("rhs", l, n)))
                if n < TT - 1:
                    b = bank(dve, "su", l, n)
                    if n == 0:
                        dve.tensor_copy(state[:, 0, :], b[:, :]).then_inc(*freed("su", l, n, also=("state", l, n)))
                    else:
                        dve.wait_ge(*when("state", l, n - 1))
                        for h in range(GH):
                            op = dve.scalar_tensor_tensor(out=head(state[:, n % 2, :], h),
                                                          in0=head(state[:, (n - 1) % 2, :], h),
                                                          scalar=colnh(CD, n, h), in1=head(b, h),
                                                          op0=ALU.mult, op1=ALU.add)
                        op.then_inc(*freed("su", l, n, also=("state", l, n)))
            dve.wait_ge(*when("rms_o", l))
            dve.reciprocal(cols(L2), cols(L2)).then_inc(*done("o_inv", l))
            dve.wait_ge(*when("o_inv", l))
            for n in range(TT):
                if n >= 2:
                    dve.wait_ge(*when("bank_filled", "o_row", l, n - 2))
                buf = spread if n % 2 == 0 else sqacc
                for h in range(GH):
                    op = dve.tensor_scalar(head(buf[:, :], h), ident, colnh(L2, n, h), None, ALU.mult)
                op.then_inc(*done("o_diag", l, n))
                b = bank(dve, "o_row", l, n)
                x = o_t[:, :, P * n:P * n + P]
                dve.tensor_tensor(x, x, banked(b), ALU.mult).then_inc(*freed("o_row", l, n, also=("o_normed", l, n)))
            dve.wait_ge(*when("o_normed", l, TT - 1))
            dve.wait_ge(*when("gate", l, GH - 1))
            for h in range(GH):
                dve.wait_ge(*when("o_normed", l, h))
                dve.scalar_tensor_tensor(out=o_t[:, h, :], in0=o_t[:, h, :], scalar=G(f"gdn_norm{l}", 0),
                                         in1=g_gate[:, h, :], op0=ALU.mult, op1=ALU.mult).then_inc(*done("gated", l, h))
            for c in range(KC):
                split_dve(dve, tmp[:, c, :] if c < 4 else o_t[:, c - 4, :], c, ("out", l))

        LAT, CTX = slice(0, S), slice(S, S + M)
        PARTS = (("lat", hT, LAT, S, 0), ("ctx", None, CTX, M, 1))
        EJ = even_jobs()
        OJ = odd_jobs()

        def stream(p):
            return hT if p == "lat" else cT

        def mod_gain_dve(dve, i):
            g = par[:, pc[f"norm_g{i}"][0]:pc[f"norm_g{i}"][0] + KC]
            if i:
                dve.wait_ge(*when("shifted_in", 0, "ctx", KC - 1))
            dve.wait_ge(*when("mod_out", i, 3 * KC - 1))
            for w in range(2):
                dve.scalar_tensor_tensor(out=mod_gain[:, w, :], in0=mod[:, i, KC:2 * KC, w], scalar=1.0, in1=g,
                                         op0=ALU.add, op1=ALU.mult).then_inc(*done("mod_gain", i, w))
            dve.wait_ge(*when("mod_gain", i, 1))

        def mod_norm_act(act, i, p, n, w, sources):
            key = ("m2", i, p)
            x = stream(p)
            squares_act(act, key, lambda c: x[:, c, :n], n, wait=sources)
            rms_act(act, key, n)
            rstd_act(act, key, n)
            o = 0 if p == "lat" else S
            for c in range(KC):
                act.wait_ge(*when("scaled", i, p, c))
                act.activation(b_hi[:, c, o:o + n], mod_tmp(i)[:, c % 2, :n], ACT.Identity, bias=mod[:, i, c, w:w + 1])\
                   .then_inc(*done("hi", i, p, c))

        def mod_tmp(i):
            return e_t if i == 0 else c_y

        def mod_norm_dve(dve, i, p, n, w):
            key = ("m2", i, p)
            x = stream(p)
            sum_squares_dve(dve, key, n)
            spread_dve(dve, key, n)
            dve.wait_ge(*when("rstd_in", *key))
            o = 0 if p == "lat" else S
            t = mod_tmp(i)
            for c in range(KC + 1):
                if c < KC:
                    if c >= 2:
                        dve.wait_ge(*when("shifted_in", i, p, c - 2))
                    dve.scalar_tensor_tensor(out=t[:, c % 2, :n], in0=x[:, c, :n], scalar=mod_gain[:, w, c:c + 1],
                                             in1=rstd[:, :n], op0=ALU.mult, op1=ALU.mult).then_inc(*done("scaled", i, p, c))
                if c:
                    e = c - 1
                    dve.wait_ge(*when("hi", i, p, e))
                    dve.scalar_tensor_tensor(out=b_lo[:, e, o:o + n], in0=t[:, e % 2, :n],
                                             scalar=mod[:, i, e, w:w + 1], in1=b_hi[:, e, o:o + n].bitcast(f32),
                                             op0=ALU.add, op1=ALU.subtract).then_inc(*done("shifted_in", i, p, e))

        def mod_norm_pe(pe, i, p, n):
            ssq_pe(pe, ("m2", i, p), n)
            rstd_pe(pe, ("m2", i, p), n)

        def both(name):
            return [(f"{name}/lat", b_hi, b_lo, S), (f"{name}/ctx", b_hi[:, :, S:], b_lo[:, :, S:], M)]

        def mod_ready(i):
            return lambda k: [("shifted_in", i, "lat", k), ("shifted_in", i, "ctx", k)]

        def e_place(name):
            if name in ("ak", "av", "bk", "bv"):
                return e_raw[:, ("ak", "bk", "av", "bv").index(name), :]
            return e_q[:, int(name[2]) + (CC if name[0] == "b" else 0), :]

        E_IN = [n for n, _, _ in EJ if n[1] in "kvq"]
        E_GATE = [n for n, _, _ in EJ if n[1] == "g"]
        NORMED = ["ak"] + [f"aq{c}" for c in range(CC)]
        ROPED = ["ak", "bk"] + [f"{x}q{c}" for x in "ab" for c in range(CC)]

        def even_in_pe(pe):
            for i, name in enumerate(E_IN):
                product(pe, (0,), both(name), need=mod_ready(0) if i == 0 else None)

        def even_in_act(act):
            for name in E_IN:
                scale = AD ** -0.5 if name[:2] == "bq" else 1.0
                for p, _, sl, n, _ in PARTS:
                    b = bank(act, f"{name}/{p}", 0)
                    act.activation(e_place(name)[:, sl], b[:, :n], ACT.Copy, scale=scale)\
                       .then_inc(*freed(f"{name}/{p}", 0, also=("e_in", name, p)))

        def even_prep_pe(pe):
            for i, name in enumerate(NORMED):
                for p, _, sl, n, _ in PARTS:
                    pe.wait_ge(*when("e_sq", name, p))
                    b = claim(pe, "e_ssq", name, p)
                    pe.matmul(b[:, :n], C("head_ones"), e_t[:, i % 2, sl], start=True, stop=True)\
                      .then_inc(*filled("e_ssq", name, p))
            for i, name in enumerate(ROPED):
                pe.wait_ge(*(when("e_normed", name, "lat") if name in NORMED else when("e_in", name, "lat")))
                b = claim(pe, "e_swap", name)
                pe.matmul(b[:, :], C("rope2"), e_place(name)[:, LAT], start=True, stop=True).then_inc(*filled("e_swap", name))
            for j, name in enumerate(("av", "bv")):
                pe.wait_ge(*when("e_in", name, "ctx"))
                for g, tiles_ in enumerate((range(4), range(4, 6))):
                    b = claim(pe, "e_vt", name, g)
                    for m, t in enumerate(tiles_):
                        mm = pe.transpose(b[:, P * m:P * m + P], e_place(name)[:, P * t:P * t + P], ident)
                    mm.then_inc(*filled("e_vt", name, g))

        def even_prep_act(act):
            for i, name in enumerate(NORMED):
                for p, _, sl, n, _ in PARTS:
                    if i >= 2:
                        act.wait_ge(*when("e_normed", NORMED[i - 2], p))
                    act.activation(e_t[:, i % 2, sl], e_place(name)[:, sl], ACT.Square).then_inc(*done("e_sq", name, p))
                for p, _, sl, n, _ in PARTS:
                    b = bank(act, "e_ssq", name, p)
                    act.activation(e_t[:, i % 2, sl], b[:, :n], ACT.Sqrt, bias=C("eps"), scale=1.0 / AD)\
                       .then_inc(*freed("e_ssq", name, p, also=("e_rms", name, p)))
            for j, name in enumerate(("av", "bv")):
                for g in range(2):
                    b = bank(act, "e_vt", name, g)
                    n = 4 if g == 0 else 2
                    act.activation(e_vt[:, 4 * g:4 * g + n, P * j:P * j + P],
                                   b[:, :P * n].rearrange("p (t n) -> p t n", n=P), ACT.Copy)\
                       .then_inc(*freed("e_vt", name, g, also=("e_vt_in", name, g)))
            for j, name in enumerate(("ak", "bk")):
                act.wait_ge(*when("e_roped", name))
                for g in range(2):
                    for half in range(2):
                        act.activation(e_kd[AD * half:AD * half + AD, 2 * j + g, :],
                                       e_place(name)[AD * g:AD * g + AD, :], ACT.Copy)\
                           .then_inc(*done("e_kd", j, g, half))

        def even_prep_dve(dve):
            dve.tensor_scalar(col[:, 8:9], G("q_gain", 0), AD ** -0.5, None, ALU.mult).then_inc(*done("q_gain8"))
            dve.wait_ge(*when("q_gain8"))
            for i, name in enumerate(NORMED):
                for p, _, sl, n, _ in PARTS:
                    dve.wait_ge(*when("e_rms", name, p))
                    dve.reciprocal(e_t[:, i % 2, sl], e_t[:, i % 2, sl]).then_inc(*done("e_rrms", name, p))
                    dve.wait_ge(*when("e_rrms", name, p))
                    dve.scalar_tensor_tensor(out=e_place(name)[:, sl], in0=e_place(name)[:, sl],
                                             scalar=G("k_gain", 0) if name == "ak" else col[:, 8:9],
                                             in1=e_t[:, i % 2, sl], op0=ALU.mult, op1=ALU.mult)\
                       .then_inc(*done("e_normed", name, p))
            dve.wait_ge(*when("axial"))
            for i, name in enumerate(ROPED):
                x = e_place(name)[:, LAT]
                t = e_t[:, i % 2, LAT]
                if i >= 2:
                    dve.wait_ge(*when("e_roped", ROPED[i - 2]))
                else:
                    dve.wait_ge(*when("e_normed", NORMED[-1], "ctx"))
                    dve.wait_ge(*when("e_normed", NORMED[-2], "ctx"))
                b = bank(dve, "e_swap", name)
                dve.tensor_tensor(t, b[:, :], rope_t[:, 1, :], ALU.mult)\
                   .then_inc(*freed("e_swap", name, also=("e_sin", name)))
                dve.tensor_tensor(x, x, rope_t[:, 0, :], ALU.mult).then_inc(*done("e_cos", name))
                dve.wait_ge(*when("e_sin", name))
                dve.wait_ge(*when("e_cos", name))
                dve.tensor_tensor(x, x, t, ALU.add).then_inc(*done("e_roped", name))

        def even_units():
            units = []
            for x in range(2):
                for h in range(QH):
                    lo, g = AD * (h % 2), h // 4
                    q = e_q[lo:lo + AD, CC * x + h // 2, :]
                    k = e_kd[lo:lo + AD, 2 * x + g, :]
                    sink = G("sink", h) if x else None
                    for t in range(TT):
                        qt = q[:, P * t:P * t + P]
                        a, z = (0, TT) if x == 0 else (max(0, t - 1), min(TT, t + 2))
                        mask = bmask[:, P * (a - t + 1):P * (z - t + 1)] if x else None
                        units.append({"head": QH * x + h, "group": (x, h, "lat"), "q0": P * t, "sink": sink,
                                      "parts": [(P * a, P * (z - a), [(qt, k[:, P * a:P * z])], mask),
                                                (S, M, [(qt, k[:, CTX])], None)]})
                    for t in range(MT):
                        qt = q[:, S + P * t:S + P * t + P]
                        units.append({"head": QH * x + h, "group": (x, h, "ctx"), "q0": S + P * t, "sink": sink,
                                      "parts": [(S, M, [(qt, k[:, CTX])], None)]})
            return units

        def even_values(kt, h):
            x, g = h // QH, (h % QH) // 4
            return [e_vt[:, kt, P * x + AD * g:P * x + AD * g + AD]]

        def even_take(units):
            def take(act, u):
                h = units[u]["head"]
                lo = AD * (h % 2)
                sl, n = (LAT, S) if units[u]["group"][2] == "lat" else (CTX, M)
                b = bank(act, "o", "even", u, 0)
                act.activation(e_q[lo:lo + AD, h // 2, sl], b[0:AD, :n], ACT.Copy)\
                   .then_inc(*freed("o", "even", u, 0, also=("e_out", h, units[u]["group"][2])))
            return take

        def even_gate_pe(pe):
            for name in E_GATE:
                product(pe, (0,), both(name))

        def even_gate_act(act):
            for i, name in enumerate(E_GATE):
                c = int(name[2]) + (CC if name[0] == "b" else 0)
                for p, _, sl, n, _ in PARTS:
                    if i >= 2:
                        act.wait_ge(*when("e_gated", c - 2, p))
                    b = bank(act, f"{name}/{p}", 0)
                    act.activation(e_t[:, i % 2, sl], b[:, :n], ACT.Silu)\
                       .then_inc(*freed(f"{name}/{p}", 0, also=("e_gate", c, p)))
            for c in range(KC):
                for p in ("lat", "ctx"):
                    act.wait_ge(*when("e_gated", c, p))
                split_act(act, e_q[:, c, :], c, ("e_mix",), n=S + M, hi=b_hi)

        def even_gate_dve(dve):
            for c in range(KC):
                for p, _, sl, n, _ in PARTS:
                    dve.wait_ge(*when("e_gate", c, p))
                    dve.wait_ge(*when("e_out", 2 * c + 1, p))
                    dve.tensor_tensor(e_q[:, c, sl], e_q[:, c, sl], e_t[:, c % 2, sl], ALU.mult)\
                       .then_inc(*done("e_gated", c, p))
            for c in range(KC):
                split_dve(dve, e_q[:, c, :], c, ("e_mix",), n=S + M, hi=b_hi, lo=b_lo)

        def even_out_pe(pe):
            for c in range(KC):
                product(pe, (0, c), both("e_y"), need=inputs_ready(("e_mix",)) if c == 0 else None)

        def even_out_dve(dve):
            for c in range(KC):
                for p, _, sl, n, w in PARTS:
                    b = bank(dve, f"e_y/{p}", 0, c)
                    x = stream(p)[:, c, :n]
                    dve.scalar_tensor_tensor(out=x, in0=b[:, :n], scalar=mod[:, 0, 2 * KC + c, w:w + 1], in1=x,
                                             op0=ALU.mult, op1=ALU.add)\
                       .then_inc(*freed(f"e_y/{p}", 0, c, also=("h2", p, c)))

        def odd_in_pe(pe):
            for i, (name, _, _, with_ctx) in enumerate(OJ):
                product(pe, (1,), both(name) if with_ctx else both(name)[:1], need=mod_ready(1) if i == 0 else None)

        def odd_in_act(act):
            for name, _, _, with_ctx in OJ:
                c, kind = int(name[2]), name[:2]
                b = bank(act, f"{name}/lat", 1)
                if kind == "cv":
                    act.activation(c_u[:, c, CT // 2:CT // 2 + S], b[:, :], ACT.Copy)\
                       .then_inc(*freed(f"{name}/lat", 1, also=("c_val", c)))
                elif kind == "cl":
                    act.activation(c_g[:, c, :], b[:, :], ACT.Sigmoid)\
                       .then_inc(*freed(f"{name}/lat", 1, also=("c_glu", c)))
                elif kind == "cg":
                    act.wait_ge(*when("c_in", c))
                    act.activation(c_g[:, c, :], b[:, :], ACT.Silu)\
                       .then_inc(*freed(f"{name}/lat", 1, also=("c_gate", c)))
                elif kind == "dg":
                    act.activation(d_g[:, c, :], b[:, :], ACT.Silu)\
                       .then_inc(*freed(f"{name}/lat", 1, also=("d_gate", c)))
                elif kind == "dq":
                    act.activation(d_q[:, c, :], b[:, :], ACT.Copy, scale=AD ** -0.5)\
                       .then_inc(*freed(f"{name}/lat", 1, also=("dq", c)))
                else:
                    to = d_k if kind == "dk" else d_v
                    act.activation(to[:, c, LAT], b[:, :], ACT.Copy).then_inc(*freed(f"{name}/lat", 1, also=(kind, c, "lat")))
                    b = bank(act, f"{name}/ctx", 1)
                    act.activation(to[:, c, CTX], b[:, :M], ACT.Copy).then_inc(*freed(f"{name}/ctx", 1, also=(kind, c, "ctx")))

        def conformer_dve(dve):
            side = CT // 2
            for c in range(CC):
                for w, at in ((0, 0), (1, side + S)):
                    dve.memset(c_u[:, c, at:at + side], 0.0).then_inc(*done("c_zero", c, w))
            dve.wait_ge(*when("c_zero", CC - 1, 1))
            for c in range(CC):
                dve.wait_ge(*when("c_val", c))
                dve.wait_ge(*when("c_glu", c))
                u = c_u[:, c, side:side + S]
                dve.tensor_tensor(u, u, c_g[:, c, :], ALU.mult).then_inc(*done("c_in", c))
                dve.wait_ge(*when("c_in", c))
                for j in range(CT):
                    if j == 0:
                        op = dve.tensor_scalar(c_y[:, c, :], c_u[:, c, 0:S], G("dw_w", CT * c), G("dw_b", c),
                                               ALU.mult, ALU.add)
                    else:
                        dve.wait_ge(*when("c_tap", c, j - 1))
                        op = dve.scalar_tensor_tensor(out=c_y[:, c, :], in0=c_u[:, c, j:j + S],
                                                      scalar=G("dw_w", CT * c + j), in1=c_y[:, c, :],
                                                      op0=ALU.mult, op1=ALU.add)
                    op.then_inc(*done("c_tap", c, j))
            b = bank(dve, "c_sum")
            dve.wait_ge(*when("c_tap", CC - 1, CT - 1))
            dve.tensor_scalar(sqacc[:, :], b[:, :], 1.0 / (CC * P), None, ALU.mult)\
               .then_inc(*freed("c_sum", also=("c_mean",)))
            dve.wait_ge(*when("c_mean"))
            for c in range(CC):
                dve.tensor_tensor(c_y[:, c, :], c_y[:, c, :], sqacc[:, :], ALU.subtract).then_inc(*done("c_centred", c))
            dve.wait_ge(*when("c_std"))
            dve.reciprocal(spread[:, :], spread[:, :]).then_inc(*done("c_rstd"))
            dve.wait_ge(*when("c_rstd"))
            for c in range(CC):
                dve.wait_ge(*when("c_centred", c))
                dve.scalar_tensor_tensor(out=c_y[:, c, :], in0=c_y[:, c, :], scalar=G("ln_g", c), in1=spread[:, :],
                                         op0=ALU.mult, op1=ALU.mult).then_inc(*done("c_scaled", c))
            for c in range(CC):
                dve.wait_ge(*when("c_silu", c))
                dve.wait_ge(*when("c_gate", c))
                dve.tensor_tensor(c_y[:, c, :], c_y[:, c, :], c_g[:, c, :], ALU.mult).then_inc(*done("c_out", c))

        def conformer_pe(pe):
            b = claim(pe, "c_sum")
            for c in range(CC):
                pe.wait_ge(*when("c_tap", c, CT - 1))
                mm = pe.matmul(b[:, :], ones, c_y[:, c, :], start=c == 0, stop=c == CC - 1)
            mm.then_inc(*filled("c_sum"))
            b = claim(pe, "c_var")
            for c in range(CC):
                pe.wait_ge(*when("c_sq", c))
                mm = pe.matmul(b[:, :], ones, sq[:, c % 2, :], start=c == 0, stop=c == CC - 1)
                mm.then_inc(*(filled("c_var") if c == CC - 1 else done("c_sq_used", c)))

        def conformer_act(act):
            for c in range(CC):
                act.wait_ge(*when("c_centred", c))
                if c >= 2:
                    act.wait_ge(*when("c_sq_used", c - 2))
                act.activation(sq[:, c % 2, :], c_y[:, c, :], ACT.Square).then_inc(*done("c_sq", c))
            b = bank(act, "c_var")
            act.activation(spread[:, :], b[:, :], ACT.Sqrt, bias=C("eps"), scale=1.0 / (CC * P))\
               .then_inc(*freed("c_var", also=("c_std",)))
            for c in range(CC):
                act.wait_ge(*when("c_scaled", c))
                act.activation(c_y[:, c, :], c_y[:, c, :], ACT.Silu, bias=G("ln_b", c)).then_inc(*done("c_silu", c))

        def odd_turn_pe(pe):
            for kt in range(6):
                pe.wait_ge(*when("dv", CC - 1, "ctx"))
                b = claim(pe, "d_vt", kt)
                for c in range(CC):
                    mm = pe.transpose(b[:, P * c:P * c + P], d_v[:, c, P * kt:P * kt + P], ident)
                mm.then_inc(*filled("d_vt", kt))

        def odd_turn_act(act):
            for kt in range(6):
                b = bank(act, "d_vt", kt)
                act.activation(d_vt[:, kt, :], b[:, :], ACT.Copy).then_inc(*freed("d_vt", kt, also=("d_vt_in", kt)))

        ROWS15, WIDE = 2 * NROW - 1, 127

        def load_bias(act, h):
            rows = dram["rpb_rows"]
            if h == 0:
                act.wait_ge(*when("bank_filled", "dg3/lat", 1))
            for half in range(2):
                src = bass.AP(rows.tensor, (h * ROWS15 + 1 - half) * GW * WIDE + GW - 1,
                              [[WIDE - 1, GW], [GW * WIDE, ROWS15 - 1], [1, GW]])
                dst = d_bias[GW * half:GW * half + GW, h % 2, GW:].rearrange("p (r k) -> p r k", k=GW)
                act.dma_start(dst, src).then_inc(*loaded(f"bias_in{h % 2}", h, half))

        def odd_units():
            units = []
            for h in range(QH):
                lo, c = AD * (h % 2), h // 2
                for t in range(TT):
                    q = d_q[lo:lo + AD, c, P * t:P * t + P]
                    at = GW * (NROW - 1 - 2 * t)
                    units.append({"head": h, "group": h, "q0": P * t,
                                  "parts": [(0, S, [(q, d_k[lo:lo + AD, c, LAT])], d_bias[:, h % 2, at:at + S]),
                                            (S, M, [(q, d_k[lo:lo + AD, c, CTX])], None)]})
            return units

        def bias_dve(dve, h):
            dve.wait_ge(*when(f"bias_in{h % 2}", h, 1))
            if h == 0:
                dve.wait_ge(*when("col_mask"))
            x = d_bias[:, h % 2, GW:].rearrange("p (r k) -> p r k", k=GW)
            dve.tensor_tensor(x, x, col_mask[:, None, :].broadcast_to([P, ROWS15 - 1, GW]), ALU.add)\
               .then_inc(*done("bias", h))
            dve.wait_ge(*when("bias", h))

        def odd_take(act, u):
            h = u // TT
            lo = AD * (h % 2)
            b = bank(act, "o", "odd", u, 0)
            act.activation(d_q[lo:lo + AD, h // 2, :], b[0:AD, :], ACT.Copy)\
               .then_inc(*freed("o", "odd", u, 0, also=("d_out", h)))
            if h + 2 < QH:
                act.wait_ge(*when("s_in", "odd", u, 0))
                load_bias(act, h + 2)

        def odd_out_act(act):
            for c in range(KC):
                act.wait_ge(*(when("c_out", c) if c < CC else when("d_gated", c - CC)))
                split_act(act, (c_y if c < CC else d_q)[:, c % CC, :], c, ("d_mix",), hi=b_hi)

        def odd_out_dve(dve):
            for c in range(CC):
                dve.wait_ge(*when("d_out", 2 * c + 1))
                dve.wait_ge(*when("d_gate", c))
                dve.tensor_tensor(d_q[:, c, :], d_q[:, c, :], d_g[:, c, :], ALU.mult).then_inc(*done("d_gated", c))
            for c in range(KC):
                split_dve(dve, (c_y if c < CC else d_q)[:, c % CC, :], c, ("d_mix",), hi=b_hi, lo=b_lo)

        def second_pe(pe):
            for p, _, _, n, _ in PARTS:
                mod_norm_pe(pe, 0, p, n)
            even_in_pe(pe)
            even_prep_pe(pe)
            attention_pe(pe, ("even",), even_units(), e_s, e_pt, even_values,
                         need=[("e_roped", ROPED[-1]), ("e_kd", 1, 1, 1), ("e_vt_in", "bv", 1)])
            even_gate_pe(pe)
            even_out_pe(pe)
            for p, _, _, n, _ in PARTS:
                mod_norm_pe(pe, 1, p, n)
            odd_in_pe(pe)
            conformer_pe(pe)
            odd_turn_pe(pe)
            attention_pe(pe, ("odd",), odd_units(), d_s, d_pt,
                         lambda kt, h: [d_vt[:, kt, AD * h:AD * h + AD]],
                         need=[("d_vt_in", 5), ("dq", CC - 1), ("dk", CC - 1, "ctx")])
            for c in range(KC):
                product(pe, (1, c), [("d_y", b_hi, b_lo, S)], need=inputs_ready(("d_mix",)) if c == 0 else None)
            ssq_pe(pe, ("final",), S)
            rstd_pe(pe, ("final",), S)

        def second_act(act):
            act.wait_ge(*when("bank_filled", "y", "f_post", DEPTH - 1, KC - 1))
            act.dma_start(cT[:, :, :], dram["ctxT"]).then_inc(*loaded("c_in2"))
            act.dma_start(rope_t[:, :, :], dram["axial"]).then_inc(*loaded("axial"))
            act.dma_start(bmask[:, :], dram["band_mask"]).then_inc(*loaded("bmask"))
            mod_norm_act(act, 0, "lat", S, 0, lambda c: ("h", "f_post", DEPTH - 1, c))
            mod_norm_act(act, 0, "ctx", M, 1, lambda c: ("c_in2",))
            even_in_act(act)
            even_prep_act(act)
            attention_act(act, ("even",), even_units(), e_s, e_pt, even_take(even_units()))
            even_gate_act(act)
            mod_norm_act(act, 1, "lat", S, 0, lambda c: ("h2", "lat", c))
            mod_norm_act(act, 1, "ctx", M, 1, lambda c: ("h2", "ctx", c))
            odd_in_act(act)
            conformer_act(act)
            odd_turn_act(act)
            load_bias(act, 0)
            load_bias(act, 1)
            act.dma_start(col_mask[:, :], dram["column_mask"]).then_inc(*loaded("col_mask"))
            attention_act(act, ("odd",), odd_units(), d_s, d_pt, odd_take)
            odd_out_act(act)
            squares_act(act, ("final",), lambda c: hT[:, c, :], S, wait=lambda c: ("h3", c))
            rms_act(act, ("final",), S)
            for c in range(KC):
                act.wait_ge(*when("out_ready", c))
                act.dma_start(out[:, c, :], hT[:, c, :]).then_inc(*loaded("out", c))
            act.wait_ge(*when("out", KC - 1))

        def second_dve(dve):
            mod_gain_dve(dve, 0)
            for p, _, _, n, w in PARTS:
                mod_norm_dve(dve, 0, p, n, w)
            even_prep_dve(dve)
            dve.wait_ge(*when("bmask"))
            attention_dve(dve, ("even",), even_units(), e_s)
            even_gate_dve(dve)
            even_out_dve(dve)
            mod_gain_dve(dve, 1)
            for p, _, _, n, w in PARTS:
                mod_norm_dve(dve, 1, p, n, w)
            conformer_dve(dve)
            attention_dve(dve, ("odd",), odd_units(), d_s,
                          before=lambda u: bias_dve(dve, u // TT) if u % TT == 0 else None)
            odd_out_dve(dve)
            for c in range(KC):
                b = bank(dve, "d_y", 1, c)
                dve.scalar_tensor_tensor(out=hT[:, c, :], in0=b[:, :], scalar=mod[:, 1, 2 * KC + c, 0:1],
                                         in1=hT[:, c, :], op0=ALU.mult, op1=ALU.add)\
                   .then_inc(*freed("d_y", 1, c, also=("h3", c)))
            sum_squares_dve(dve, ("final",), S)
            spread_dve(dve, ("final",), S)
            b = bank(dve, "rstd", "final")
            for c in range(KC):
                dve.scalar_tensor_tensor(out=hT[:, c, :], in0=hT[:, c, :], scalar=G("final_g", c), in1=b[:, :],
                                         op0=ALU.mult, op1=ALU.mult)\
                   .then_inc(*(freed("rstd", "final", also=("out_ready", c)) if c == KC - 1
                               else done("out_ready", c)))

        def x_units(l):
            units = []
            for h in range(XH):
                for t in range(TT):
                    mms = [(xq[:, 2 * h + j, P * t:P * t + P], xk[:, 2 * h + j, :]) for j in range(2)]
                    units.append({"head": h, "group": h, "q0": P * t, "parts": [(0, M, mms, None)]})
            return units

        def memory_product_pe(pe, l):
            for c in range(2 * KC):
                product(pe, (l, c), [("kv", m_hi, m_lo, M)], need=inputs_ready(("mem", l)) if c == 0 else None)
                if c == 0:
                    ssq_pe(pe, ("mix_post", l), S)
                if c == 2:
                    rstd_pe(pe, ("mix_post", l), S)
            for g in range(4):
                pe.wait_ge(*when("kv_in", l, 2 * KC - 1))
                b = claim(pe, "xvt", l, g)
                for j in range(4):
                    c = 4 * (g % 2) + j
                    mm = pe.transpose(b[:, P * j:P * j + P], xv[:, c, P * (g // 2):P * (g // 2) + P], ident)
                mm.then_inc(*filled("xvt", l, g))

        def memory_act(act, l):
            act.wait_ge(*when("vn_in", l, TT - 1))
            act.wait_ge(*when("bank_filled", "go", l, TT - 1))
            act.dma_start(m_in[:, :, :], dram["memT"]).then_inc(*loaded("m_in", l))

        def memory_norm_act(act, l):
            pre_norm_act(act, ("mem", l), f"mem{l}", m_in, m_hi, M, lambda c: ("m_in", l))
            rstd_act(act, ("mem", l), M)

        def memory_product_dve(dve, l):
            dve.wait_ge(*when("rstd_in", "mem", l))
            key = ("mix_post", l)
            sum_squares_dve(dve, key, S)
            for c in range(2 * KC):
                if c == 1:
                    spread_dve(dve, key, S)
                if c == 3:
                    post_apply_dve(dve, key, f"mix_post{l}", y_x)
                b = bank(dve, "kv", l, c)
                dve.tensor_tensor((xk if c < KC else xv)[:, c % KC, :], b[:, :M], rstd[:, :M], ALU.mult)\
                   .then_inc(*freed("kv", l, c, also=("kv_in", l, c)))

        def memory_turn_act(act, l):
            for g in range(4):
                b = bank(act, "xvt", l, g)
                act.activation(xvt[:, g // 2, 4 * P * (g % 2):4 * P * (g % 2) + 4 * P], b[:, :], ACT.Copy)\
                   .then_inc(*freed("xvt", l, g, also=("xvt_in", l, g)))

        def x_product_pe(pe, l):
            for c in range(KC):
                product(pe, (l, c), [("xq", a_hi, a_lo, S)], need=inputs_ready(("x", l)) if c == 0 else None)
                if c == 0:
                    ssq_pe(pe, ("x", l), S)
                if c == 2:
                    rstd_pe(pe, ("x", l), S)

        def x_product_dve(dve, l):
            dve.wait_ge(*when("rstd_in", "x", l))
            for c in range(KC):
                b = bank(dve, "xq", l, c)
                dve.scalar_tensor_tensor(out=xq[:, c, :], in0=b[:, :], scalar=XD ** -0.5, in1=rstd[:, :],
                                         op0=ALU.mult, op1=ALU.mult).then_inc(*freed("xq", l, c, also=("xq_in", l, c)))

        def x_take_act(l):
            def take(act, u):
                h = u // TT
                for o in range(2):
                    c = 2 * h + o
                    b = bank(act, "o", "x", l, u, o)
                    act.activation(tmp[:, c, :], b[:, :], ACT.Copy).then_inc(*freed("o", "x", l, u, o, also=("x_out", l, c)))
                    act.wait_ge(*when("x_out", l, c))
                    split_act(act, tmp[:, c, :], c, ("xo", l))
            return take

        def ffn_pe(pe, l):
            for j in range(FC):
                product(pe, (l, j), [("gate_p", a_hi, a_lo, S)], need=inputs_ready(("f", l)) if j == 0 else None)
                if j == 0:
                    ssq_pe(pe, ("f", l), S)
                if j == 1:
                    rstd_pe(pe, ("f", l), S)
                product(pe, (l, j), [("up_p", a_hi, a_lo, S)])
                if j >= 2:
                    modulation_pe(pe, l, j - 2)
            for c in range(KC):
                product(pe, ("f_post", l, c), [("y", f_hi, f_lo, S)], kc=FC,
                        need=inputs_ready(("hid", l)) if c == 0 else None)

        def ffn_dve(dve, l):
            dve.wait_ge(*when("rstd_in", "f", l))

            def gate_up(j):
                r = 4 * (j % 2)
                if j >= 2:
                    dve.wait_ge(*when("lo", "hid", l, j - 2))
                b = bank(dve, "gate_p", l, j)
                dve.tensor_tensor(tmp[:, r, :], b[:, :], rstd[:, :], ALU.mult)\
                   .then_inc(*freed("gate_p", l, j, also=("gate_s", l, j)))
                b = bank(dve, "up_p", l, j)
                dve.tensor_tensor(tmp[:, r + 2, :], b[:, :], rstd[:, :], ALU.mult)\
                   .then_inc(*freed("up_p", l, j, also=("up_s", l, j)))

            def hidden(j):
                r = 4 * (j % 2)
                dve.wait_ge(*when("f_silu", l, j))
                dve.wait_ge(*when("up_s", l, j))
                dve.tensor_tensor(tmp[:, r + 3, :], tmp[:, r + 1, :], tmp[:, r + 2, :], ALU.mult)\
                   .then_inc(*done("hidden", l, j))
                split_dve(dve, tmp[:, r + 3, :], j, ("hid", l), hi=f_hi, lo=f_lo)

            for j in range(FC + 1):
                if j < FC:
                    gate_up(j)
                if j:
                    hidden(j - 1)

        def ffn_act(act, l):
            def silu(j):
                r = 4 * (j % 2)
                act.wait_ge(*when("gate_s", l, j))
                act.activation(tmp[:, r + 1, :], tmp[:, r, :], ACT.Silu).then_inc(*done("f_silu", l, j))

            def split(j):
                act.wait_ge(*when("hidden", l, j))
                split_act(act, tmp[:, 4 * (j % 2) + 3, :], j, ("hid", l), hi=f_hi)

            for j in range(FC + 1):
                if j < FC:
                    silu(j)
                if j:
                    split(j - 1)
                    modulation_act(act, l, j - 1)

        def modulation_pe(pe, l, j):
            for c in range(2 * j, min(2 * j + 2, 3 * KC)):
                pe.wait_ge(*when(f"mod_in{c % 2}", l, c))
                b = claim(pe, "mod", l, c)
                for k in range(KC):
                    mm = pe.matmul(b[:, 0:2], mod_raw[:, c % 2, P * k:P * k + P], cond[:, k, :],
                                   start=k == 0, stop=k == KC - 1)
                mm.then_inc(*filled("mod", l, c))

        def modulation_act(act, l, j):
            for c in range(2 * j - 2, min(2 * j, 3 * KC)):
                if c >= 0:
                    b = bank(act, "mod", l, c)
                    act.activation(mod[:, l, c, :], b[:, 0:2], ACT.Identity, bias=G(f"mod_b{l}", c))\
                       .then_inc(*freed("mod", l, c, also=("mod_out", l, c)))
            if j == 0:
                act.wait_ge(*when("rstd_in", "f", l))
            for c in range(2 * j, min(2 * j + 2, 3 * KC)):
                act.dma_start(mod_raw[:, c % 2, :], dram["mod_tiles"][l, c]).then_inc(*loaded(f"mod_in{c % 2}", l, c))

        def rope_table_dve(dve):
            two_pi = 2 * np.pi
            part1 = 6.28125
            part2 = two_pi - part1
            magic = 1.5 * 2.0 ** 23
            ang, n, r = acc[:, 0, :], acc[:, 1, :], pad[:, 0, 0:S]

            def step(op, i):
                op.then_inc(*done("rope_step", i))
                dve.wait_ge(*when("rope_step", i))

            dve.wait_ge(*when("pos"))
            dve.wait_ge(*when("params", 1))
            step(dve.tensor_copy(r, pos[:, :]), "f")
            step(dve.tensor_scalar(ang, r, C("inv_freq"), None, ALU.mult), "ang")
            for w, quarter in ((0, 0.25), (1, 0.0)):
                step(dve.tensor_scalar(n, ang, 1 / two_pi, quarter, ALU.mult, ALU.add), (w, 0))
                step(dve.tensor_scalar(n, n, magic, None, ALU.add), (w, 1))
                step(dve.tensor_scalar(n, n, magic, None, ALU.subtract), (w, 2))
                step(dve.scalar_tensor_tensor(out=r, in0=n, scalar=-part1, in1=ang, op0=ALU.mult, op1=ALU.add), (w, 3))
                step(dve.scalar_tensor_tensor(out=r, in0=n, scalar=-part2, in1=r, op0=ALU.mult, op1=ALU.add), (w, 4))
                step(dve.tensor_scalar(r, r, two_pi * quarter, 3.1415925, ALU.add, ALU.min), (w, 5))
                dve.tensor_scalar(rope_t[:, w, :], r, -3.1415925, None, ALU.max).then_inc(*done("angle", w))
                dve.wait_ge(*when("angle", w))

        def rope_table_act(act):
            for w in range(2):
                act.wait_ge(*when("angle", w))
                act.activation(rope_t[:, w, :], rope_t[:, w, :], ACT.Sin).then_inc(*done("rope_table", w))
            act.wait_ge(*when("rope_table", 1))

        def h_before(l):
            return (lambda c: ("h_in",)) if l == 0 else (lambda c: ("h", "f_post", l - 1, c))

        block = ctx.enter_context(nc.Block())
        layers = range(DEPTH)
        stopped = stop is not None

        @block.tensor
        def _(pe):
            pe.wait_ge(*when("params", 1))
            pe.wait_ge(*when("cond"))
            for l in layers:
                in_product_pe(pe, l)
                att_prep_pe(pe, l)
                attention_pe(pe, ("att", l), att_units(l), s_buf, p_t,
                             lambda kt, h: [a_vt[:, kt, AD * h:AD * h + AD]],
                             need=[("roped", l, i) for i in range(4)] + [("avt_in", l, 1)])
                gdn_pe(pe, l)
                for c in range(KC):
                    product(pe, ("mix_post", l, c), [("y", a_hi, a_lo, S)],
                            need=inputs_ready(("out", l)) if c == 0 else None)
                    if c == 3:
                        ssq_pe(pe, ("mem", l), M)
                    if c == 5:
                        rstd_pe(pe, ("mem", l), M)
                memory_product_pe(pe, l)
                x_product_pe(pe, l)
                attention_pe(pe, ("x", l), x_units(l), x_s, x_pt,
                             lambda kt, h: [xvt[:, kt, XD * h + P * o:XD * h + P * o + P] for o in range(2)],
                             need=[("xq_in", l, KC - 1), ("xvt_in", l, 3)])
                for c in range(KC):
                    product(pe, ("x_post", l, c), [("y", a_hi, a_lo, S)],
                            need=inputs_ready(("xo", l)) if c == 0 else None)
                ssq_pe(pe, ("x_post", l), S)
                rstd_pe(pe, ("x_post", l), S)
                ffn_pe(pe, l)
                ssq_pe(pe, ("f_post", l), S)
                rstd_pe(pe, ("f_post", l), S)
            if not stopped:
                second_pe(pe)

        @block.sync
        def _(sp):
            sp.dma_start(con[:, :], dram["consts"]).then_inc(*loaded("params", 0))
            sp.dma_start(par[:, :], dram["params"]).then_inc(*loaded("params", 1))
            load_weights(sp)

        @block.gpsimd
        def _(pool):
            split_weights(pool)

        @block.scalar
        def _(act):
            act.dma_start(pos[:, :], dram["positions"].broadcast_to([P, S])).then_inc(*loaded("pos"))
            act.dma_start(hT[:, :, :], dram["xT"]).then_inc(*loaded("h_in"))
            act.wait_ge(*when("params", 1))
            rope_table_act(act)
            act.activation(cond[:, :, :], par[:, pc["cond"][0]:pc["cond"][0] + 2 * KC].rearrange("p (k c) -> p k c", c=2),
                           ACT.Silu).then_inc(*done("cond"))
            for l in layers:
                pre_norm_act(act, ("mix", l), f"mix_pre{l}", hT, a_hi, S, h_before(l))
                rstd_act(act, ("mix", l), S)
                in_product_act(act, l)
                att_prep_act(act, l)
                attention_act(act, ("att", l), att_units(l), s_buf, p_t, att_take_act(l))
                gdn_act(act, l)
                memory_act(act, l)
                memory_norm_act(act, l)
                post_norm_act(act, ("mix_post", l), y_x)
                pre_norm_act(act, ("x", l), f"x_pre{l}", hT, a_hi, S, lambda c: ("h", "mix_post", l, c),
                             between=lambda: memory_turn_act(act, l))
                rstd_act(act, ("x", l), S)
                attention_act(act, ("x", l), x_units(l), x_s, x_pt, x_take_act(l))
                post_norm_act(act, ("x_post", l), y_x)
                pre_norm_act(act, ("f", l), f"f_pre{l}", hT, a_hi, S, lambda c: ("h", "x_post", l, c))
                rstd_act(act, ("f", l), S)
                ffn_act(act, l)
                post_norm_act(act, ("f_post", l), tmp)
            if stopped:
                for c in range(KC):
                    act.wait_ge(*when("h", "f_post", DEPTH - 1, c))
                act.dma_start(out, hT[:, :, :]).then_inc(*loaded("out"))
                act.wait_ge(*when("out"))
            else:
                second_act(act)

        @block.vector
        def _(dve):
            rope_table_dve(dve)
            for l in layers:
                pre_norm_dve(dve, ("mix", l), f"mix_pre{l}", hT, a_hi, a_lo, S)
                in_product_dve(dve, l)
                att_prep_dve(dve, l)
                dve.wait_ge(*when("cmask", l))
                attention_dve(dve, ("att", l), att_units(l), s_buf)
                gdn_dve(dve, l)
                pre_norm_dve(dve, ("mem", l), f"mem{l}", m_in, m_hi, m_lo, M)
                memory_product_dve(dve, l)
                pre_norm_dve(dve, ("x", l), f"x_pre{l}", hT, a_hi, a_lo, S)
                x_product_dve(dve, l)
                attention_dve(dve, ("x", l), x_units(l), x_s)
                for c in range(KC):
                    split_dve(dve, tmp[:, c, :], c, ("xo", l))
                post_norm_dve(dve, ("x_post", l), f"x_post{l}", y_x)
                pre_norm_dve(dve, ("f", l), f"f_pre{l}", hT, a_hi, a_lo, S)
                ffn_dve(dve, l)
                post_norm_dve(dve, ("f_post", l), f"f_post{l}", tmp)
            if not stopped:
                second_dve(dve)


def host_arrays(inputs):
    def turned(a):
        return np.ascontiguousarray(np.asarray(a).reshape(-1, KC, P).transpose(2, 1, 0))

    rpb = np.asarray(inputs["d_rpb_2"][0])
    return {
        "w_tiles": packed_weights(inputs),
        "mod_tiles": np.ascontiguousarray(np.asarray(inputs["mod_w_2"]).reshape(DEPTH, KC, P, 3 * KC, P)
                                          .transpose(0, 3, 2, 1, 4).reshape(DEPTH, 3 * KC, P, KC * P)),
        "params": packed_params(inputs),
        "consts": constants(),
        "positions": np.ascontiguousarray(np.asarray(inputs["positions"]).reshape(1, S)),
        "xT": turned(inputs["x"]),
        "memT": turned(inputs["mem"]),
        "ctxT": turned(inputs["ctx_2"]),
        "count_mask": count_mask(),
        "axial": axial_tables(),
        "band_mask": band_mask(),
        "column_mask": column_mask(),
        "rpb_rows": np.repeat(np.pad(rpb, ((0, 0), (0, 0), (48, 48)))[:, :, None, :], GW, axis=2),
    }


def kernel(stop=None, **inputs):
    import concourse.bacc as bacc
    from concourse.bass_utils import run_bass_kernel_spmd

    inputs = {k: np.asarray(v) for k, v in inputs.items()}
    arrays = host_arrays(inputs)

    def program(book):
        nc = bacc.Bacc("TRN2", target_bir_lowering=False, num_devices=1)
        dram = {name: nc.dram_tensor(name, a.shape, mybir.dt.from_np(a.dtype), kind="ExternalInput").ap()
                for name, a in arrays.items()}
        out = nc.dram_tensor("out", (P, KC, S), mybir.dt.float32, kind="ExternalOutput").ap()
        build(nc, dram, out, book, stop)
        return nc

    known = Book()
    program(known)
    nc = program(Book(known))

    r = run_bass_kernel_spmd(nc, [arrays], core_ids=[0])
    out = np.asarray(r.results[0]["out"])
    return np.ascontiguousarray(out.transpose(2, 1, 0).reshape(1, S, D))
```

```python
from contextlib import ExitStack

import numpy as np
import concourse.bass as bass
from concourse import mybir

P = 128
D = 1024
KC = D // P
S = 512
TT = S // P
M = 256
MT = M // P
DEPTH = 2
EPS = 1e-6
AH, AD = 4, 64
GH, GD = 4, 128
GK = 4
CK = 3
XH, XD = 4, 256
FH = 2816
FC = FH // P
ROPE_HALF = 8
NEG = -1.0e30
QH = 8
CC = 4
CT = 31
NROW = 8
GW = 64
RAW, SPLIT = 3, 2
UNROLL = RAW * SPLIT
BANKS = 8

SPLITS = np.cumsum([0, 256, 256, 256, 256, 256, 256, 512, 512, 512, 4, 4, 512]).tolist()
AQ, AK, AV, CB, CG, CX, GQ, GKK, GV, GA, GB, GG, _END = SPLITS
EVEN = np.cumsum([0, 512, 128, 128, 512, 512, 128, 128, 512]).tolist()


def in_jobs():
    jobs = []
    for h in range(GH):
        jobs += [(f"gk{h}", GKK + P * h, P), (f"gq{h}", GQ + P * h, P), (f"gv{h}", GV + P * h, P)]
    jobs.insert(3, ("ab", GA, 2 * GH))
    for c in range(2):
        jobs += [(f"aq{c}", AQ + P * c, P), (f"ak{c}", AK + P * c, P), (f"av{c}", AV + P * c, P)]
    for c in range(2):
        jobs += [(f"cg{c}", CG + P * c, P), (f"cx{c}", CX + P * c, P), (f"cb{c}", CB + P * c, P)]
    jobs += [(f"gg{h}", GG + P * h, P) for h in range(GH)]
    return jobs


def even_jobs():
    names = ["ak", "bk", "av", "bv"]
    at = {"aq": EVEN[0], "ak": EVEN[1], "av": EVEN[2], "ag": EVEN[3],
          "bq": EVEN[4], "bk": EVEN[5], "bv": EVEN[6], "bg": EVEN[7]}
    jobs = [(n, at[n], P) for n in names]
    for n in ("aq", "bq", "ag", "bg"):
        jobs += [(f"{n}{c}", at[n] + P * c, P) for c in range(4)]
    return jobs


def odd_jobs():
    names = ["cv", "cl", "cg", "dq", "dk", "dv", "dg"]
    at = {n: 512 * i for i, n in enumerate(names)}
    jobs = []
    for c in range(4):
        jobs += [(f"cv{c}", at["cv"] + P * c, P, False), (f"cl{c}", at["cl"] + P * c, P, False)]
    for n in ("dk", "dv", "dq", "cg", "dg"):
        jobs += [(f"{n}{c}", at[n] + P * c, P, n in ("dk", "dv")) for c in range(4)]
    return jobs


def weight_chunks():
    out = []
    for l in range(DEPTH):
        out += [("w_in", l, c0, n) for _, c0, n in in_jobs()]
        out += [("w_out", l, P * c, P) for c in range(KC)]
        out += [("w_xkv", l, P * c, P) for c in range(2 * KC)]
        out += [("w_xq", l, P * c, P) for c in range(KC)]
        out += [("w_xo", l, P * c, P) for c in range(KC)]
        for j in range(FC):
            out += [("w_gate_up", l, P * j, P), ("w_gate_up", l, FH + P * j, P)]
        out += [("w_down", l, P * c, P) for c in range(KC)]
    out += [("ev_w_in_2", 0, c0, n) for _, c0, n in even_jobs()]
    out += [("ev_w_out_2", 0, P * c, P) for c in range(KC)]
    out += [("od_w_in_2", 0, c0, n) for _, c0, n, _ in odd_jobs()]
    out += [("od_w_out_2", 0, P * c, P) for c in range(KC)]
    return out


def first_tile(wanted, layer):
    blocks = 0
    for name, l, *_ in weight_chunks():
        if (name, l) == (wanted, layer):
            return blocks // KC
        blocks += FC if name == "w_down" else KC


def packed_weights(inputs):
    blocks = []
    for name, l, c0, n in weight_chunks():
        w = inputs[name][l][:, c0:c0 + n]
        if n < P:
            w = np.pad(w, ((0, 0), (0, P - n)))
        blocks.append(w.reshape(-1, P, P))
    blocks = np.concatenate(blocks)
    tiles = blocks.reshape(-1, KC, P, P).transpose(0, 2, 1, 3)
    return np.ascontiguousarray(tiles.reshape(-1, P, KC * P))


class Columns:

    def __init__(self):
        self.at, self.n = {}, 0

    def add(self, name, width):
        self.at[name] = (self.n, width)
        self.n += width

    def __getitem__(self, name):
        return self.at[name]


def param_columns():
    c = Columns()
    for l in range(DEPTH):
        for name in ("mix_pre", "mix_post", "mem", "x_pre", "x_post", "f_pre", "f_post"):
            c.add(f"{name}{l}", KC)
        c.add(f"conv_short{l}", 2 * CK)
        c.add(f"conv_gdn{l}", 12 * GK)
        c.add(f"gdn_norm{l}", 1)
        c.add(f"dt_bias{l}", GH)
        c.add(f"a_log{l}", GH)
    for i in range(DEPTH):
        c.add(f"norm_g{i}", KC)
        c.add(f"mod_b{i}", 3 * KC)
    c.add("q_gain", 1)
    c.add("k_gain", 1)
    c.add("sink", QH)
    c.add("dw_w", CC * CT)
    c.add("dw_b", CC)
    c.add("ln_g", CC)
    c.add("ln_b", CC)
    c.add("final_g", KC)
    c.add("cond", 2 * KC)
    return c


def packed_params(inputs):
    c = param_columns()
    out = np.zeros((P, c.n), np.float32)

    def put(name, a):
        at, width = c[name]
        out[:, at:at + width] = a

    def cols(v):
        return np.asarray(v).reshape(-1, P).T

    def rows(v):
        return np.broadcast_to(np.asarray(v)[None, :], (P, len(v)))

    for l in range(DEPTH):
        for name, src in (("mix_pre", "norm_mix_pre"), ("mix_post", "norm_mix_post"), ("mem", "norm_mem"),
                          ("x_pre", "norm_xattn_pre"), ("x_post", "norm_xattn_post"),
                          ("f_pre", "norm_ffn_pre"), ("f_post", "norm_ffn_post")):
            put(f"{name}{l}", cols(inputs[src][l]))
        put(f"conv_short{l}", inputs["conv_short"][l].reshape(CK, 2, P).transpose(2, 1, 0).reshape(P, -1))
        put(f"conv_gdn{l}", inputs["conv_gdn"][l].reshape(GK, 12, P).transpose(2, 1, 0).reshape(P, -1))
        put(f"gdn_norm{l}", cols(inputs["gdn_norm"][l]))
        put(f"dt_bias{l}", rows(inputs["gdn_dt_bias"][l]))
        put(f"a_log{l}", rows(inputs["gdn_a_log"][l]))
    for i in range(DEPTH):
        put(f"norm_g{i}", cols(inputs["norm_g_2"][i]))
        put(f"mod_b{i}", cols(inputs["mod_b_2"][i]))
    put("q_gain", np.tile(inputs["a_q_gain_2"][0], 2)[:, None])
    put("k_gain", np.tile(inputs["a_k_gain_2"][0], 2)[:, None])
    put("sink", rows(inputs["b_sink_2"][0]))
    put("dw_w", inputs["c_dw_w_2"][0].reshape(CT, CC, P).transpose(2, 1, 0).reshape(P, -1))
    put("dw_b", cols(inputs["c_dw_b_2"][0]))
    put("ln_g", cols(inputs["c_ln_g_2"][0]))
    put("ln_b", cols(inputs["c_ln_b_2"][0]))
    put("final_g", cols(inputs["final_g_2"]))
    put("cond", np.stack([cols(inputs["c_2"][0]), cols(inputs["c_ctx_2"])], -1).reshape(P, -1))
    return out


def const_columns():
    c = Columns()
    for name in ("ident", "ones", "upto", "neg_future", "rope1", "rope2", "head_ones"):
        c.add(name, P)
    for s in range(7):
        c.add(f"level{s}", P)
    c.add("inv_freq", 1)
    c.add("eps", 1)
    c.add("eps_q", 1)
    c.add("zero", 1)
    return c


def constants():
    c = const_columns()
    out = np.zeros((P, c.n), np.float32)
    j, i = np.arange(P)[:, None], np.arange(P)[None, :]

    def put(name, a):
        at, width = c[name]
        out[:, at:at + width] = a

    put("ident", j == i)
    put("ones", 1.0)
    put("upto", j <= i)
    put("neg_future", np.where(i >= j, 0.0, NEG))
    swap = np.zeros((P, P), np.float32)
    for h in range(0, P, AD):
        for r in range(ROPE_HALF):
            swap[h + ROPE_HALF + r, h + r] = -1.0
            swap[h + r, h + ROPE_HALF + r] = 1.0
    put("rope1", swap)
    swap = np.zeros((P, P), np.float32)
    for r in range(0, P, 2):
        swap[r + 1, r] = -1.0
        swap[r, r + 1] = 1.0
    put("rope2", swap)
    put("head_ones", (j // 64) == (i // 64))
    for s in range(7):
        put(f"level{s}", ((i >> s) % 2 == 1) & ((j >> s) == (i >> s) - 1))
    freq = np.float32(500000.0) ** (-np.arange(0, 2 * ROPE_HALF, 2, dtype=np.float32) / (2 * ROPE_HALF))
    lane = np.arange(P) % AD
    put("inv_freq", np.where(lane < 2 * ROPE_HALF, freq[lane % ROPE_HALF], 0.0)[:, None])
    put("eps", EPS)
    put("eps_q", EPS * GD)
    return out


def count_mask():
    q, k = np.arange(P)[:, None], np.arange(S)[None, :]
    dist = q + (S - P) - k
    n = (dist <= 128).astype(int) + (dist % 4 == 0) + (dist % 16 == 0)
    n = np.where(dist >= 0, n, 0)
    return np.where(n > 0, np.log(np.maximum(n, 1)), NEG).astype(np.float32)


def axial_tables():
    t = np.arange(S)
    row, col = (t // GW).astype(np.float32), (t % GW).astype(np.float32)
    freqs = np.float32(10000.0) ** (-np.arange(0, 32, 2, dtype=np.float32) / 32)
    ang = np.concatenate([row[:, None] * freqs, col[:, None] * freqs], -1)
    ang = np.repeat(ang, 2, axis=1)
    ang = np.concatenate([ang, ang], 1).T
    return np.ascontiguousarray(np.stack([np.cos(ang), np.sin(ang)], 1).astype(np.float32))


def band_mask():
    q, k = np.arange(P)[:, None], np.arange(3 * P)[None, :] - P
    return np.where(np.abs(k - q) <= 128, 0.0, NEG).astype(np.float32)


def column_mask():
    cols = np.arange(GW)
    start = np.clip(cols - 8, 0, GW - 16)
    inside = (cols[None] >= start[:, None]) & (cols[None] < start[:, None] + 16)
    return np.tile(np.where(inside, 0.0, NEG), (2, 1)).astype(np.float32)


class Book:

    def __init__(self, known=None):
        self.known = known
        self.marks, self.count, self.jobs, self.tiles = {}, {}, {}, 0
        self.uses, self.next_bank, self.held = [0] * BANKS, 0, set()
        self.sem = None

    def mark(self, event, name, value):
        assert event not in self.marks, event
        self.marks[event] = name, value

    def done(self, name, *key, by=1):
        self.count[name] = self.count.get(name, 0) + by
        self.mark((name, *key), name, self.count[name])
        return self.sem(name), by

    def loaded(self, name, *key):
        return self.done(name, *key, by=16)

    def when(self, *event):
        name, value = self.known.marks[event] if self.known else ("start", 1)
        if name == "bank_free":
            n, use = self.known.jobs[value]
            name, value = f"bank_free{n}", use + 1
        return self.sem(name), value

    def claim(self, pe, banks, *key, hold=False):
        n = self.next_bank
        while n in self.held:
            n = (n + 1) % BANKS
        self.next_bank = (n + 1) % BANKS
        assert key not in self.jobs, key
        self.jobs[key] = n, self.uses[n]
        if self.uses[n]:
            pe.wait_ge(self.sem(f"bank_free{n}"), self.uses[n])
        self.uses[n] += 1
        if hold:
            self.held.add(n)
        return banks[n]

    def release(self, *key):
        self.held.discard(self.jobs[key][0])

    def filled(self, *key):
        return self.done("bank_filled", *key)

    def bank(self, eng, banks, *key):
        eng.wait_ge(*self.when("bank_filled", *key))
        return banks[self.known.jobs[key][0] if self.known else 0]

    def freed(self, *key, also=None):
        n = self.known.jobs[key][0] if self.known else 0
        if also:
            self.mark(also, "bank_free", key)
        return self.sem(f"bank_free{n}"), 1

    def tile_used(self, *key):
        self.tiles += 1
        if key:
            self.mark(("bank_filled", *key), "w_used", self.tiles)
        return self.sem("w_used"), 1


def build(nc, dram, out, book):
    f32, f32r, i32 = mybir.dt.float32, mybir.dt.float32r, mybir.dt.int32
    ALU, ACT, AX = mybir.AluOpType, mybir.ActivationFunctionType, mybir.AxisListType
    done, loaded, when = book.done, book.loaded, book.when
    pc, cc = param_columns(), const_columns()
    ctx = ExitStack()
    sems = {}

    def sem(name):
        if name not in sems:
            sems[name] = ctx.enter_context(nc.semaphore(name))
        return sems[name]

    book.sem = sem

    def sb(stack, name, shape, dt=f32):
        return stack.enter_context(nc.sbuf_tensor(name, shape, dt))

    with ctx:
        hT = sb(ctx, "hT", [P, KC, S])
        w_raw = sb(ctx, "w_raw", [P, RAW, KC * P])
        w_hi = sb(ctx, "w_hi", [P, SPLIT, KC * P], f32r)
        w_lo = sb(ctx, "w_lo", [P, SPLIT, KC * P], f32r)
        par = sb(ctx, "par", [P, pc.n])
        con = sb(ctx, "con", [P, cc.n])
        rope_t = sb(ctx, "rope_t", [P, 2, S])
        rstd = sb(ctx, "rstd", [P, S])
        mod = sb(ctx, "mod", [P, DEPTH, 3 * KC, 2])
        mod_sum = sb(ctx, "mod_sum", [P, 2, P])
        mod_gain = sb(ctx, "mod_gain", [P, 2, KC])
        cond = sb(ctx, "cond", [P, KC, 2])
        col = sb(ctx, "col", [P, 256])
        with ExitStack() as a1:
            a_hi = sb(a1, "a_hi", [P, KC, S], f32r)
            a_lo = sb(a1, "a_lo", [P, KC, S], f32r)
            tmp = sb(a1, "tmp", [P, KC, S])
            with ExitStack() as a1n:
                sq = sb(a1n, "sq", [P, 2, S])
                sqacc = sb(a1n, "sqacc", [P, S])
                spread = sb(a1n, "spread", [P, S])
            mod_raw = sb(a1, "mod_raw", [P, 2, KC * P])
        with ExitStack() as a2:
            x_inv = sb(a2, "x_inv", [P, TT, S])
            xt_inv = sb(a2, "xt_inv", [P, TT, S])
            at_mat = sb(a2, "at_mat", [P, TT, S])
            rel_t = sb(a2, "rel_t", [P, TT, S])
        with ExitStack() as a3:
            b_hi = sb(a3, "b_hi", [P, KC, S + M], f32r)
            b_lo = sb(a3, "b_lo", [P, KC, S + M], f32r)
            e_gate_a = sb(a3, "e_gate_a", [P, 2, S + M])
        with ExitStack() as a4:
            sb(a4, "inputs", [P, KC * (S + M) * 2])
            d_bias = sb(a4, "d_bias", [P, 2, 15 * GW])
            col_mask = sb(a4, "col_mask", [P, GW])
        top = ExitStack()
        ctx.enter_context(top)
        sb(top, "region_a", [P, KC * (S + M) * 2 + KC * M])
        with ExitStack() as u1:
            g_qkv = sb(u1, "g_qkv", [P, 12, S])
            g_gate = sb(u1, "g_gate", [P, GH, S])
            with ExitStack() as u1a:
                a_qk = sb(u1a, "a_qk", [P, 4, S])
                a_v = sb(u1a, "a_v", [P, 2, S])
                cv_in = sb(u1a, "cv_in", [P, 3, S])
                a_vt = sb(u1a, "a_vt", [P, TT, AH * AD])
                s_buf = sb(u1a, "s_buf", [P, 3, S])
                p_t = sb(u1a, "p_t", [P, TT, S])
                cmask = sb(u1a, "cmask", [P, S])
                pad = sb(u1a, "pad", [P, 2, S + 8])
                acc = sb(u1a, "acc", [P, 2, S])
                pos = sb(u1a, "pos", [P, S], i32)
                ab = sb(u1a, "ab", [8, S])
            with ExitStack() as u1b:
                attn_t = sb(u1b, "attn_t", [P, TT, S])
                k_dec = sb(u1b, "k_dec", [P, TT, S])
                v_beta = sb(u1b, "v_beta", [P, TT, S])
                dec = sb(u1b, "dec", [P, TT, S])
                state = sb(u1b, "state", [P, 2, S])
                yv = sb(u1b, "yv", [P, 4, S])
                o_t = sb(u1b, "o_t", [P, GH, S])
            with ExitStack() as u1c:
                y_mix = sb(u1c, "y_mix", [P, KC, S])
        with ExitStack() as u2:
            xq = sb(u2, "xq", [P, KC, S])
            xk = sb(u2, "xk", [P, KC, M])
            xv = sb(u2, "xv", [P, KC, M])
            y_x = sb(u2, "y_x", [P, KC, S])
            m_in = sb(u2, "m_in", [P, KC, M])
            m_hi = sb(u2, "m_hi", [P, KC, M], f32r)
            m_lo = sb(u2, "m_lo", [P, KC, M], f32r)
            xvt = sb(u2, "xvt", [P, MT, D])
            x_s = sb(u2, "x_s", [P, 3, M])
            x_pt = sb(u2, "x_pt", [P, MT, S])
        with ExitStack() as u3:
            f_hi = sb(u3, "f_hi", [P, FC, S], f32r)
            f_lo = sb(u3, "f_lo", [P, FC, S], f32r)
        with ExitStack() as u4:
            cT = sb(u4, "cT", [P, KC, M])
            with ExitStack() as u5:
                e_q = sb(u5, "e_q", [P, 2 * CC, S + M])
                e_kd = sb(u5, "e_kd", [P, 4, S + M])
                e_vt = sb(u5, "e_vt", [P, 6, 2 * P])
                bmask = sb(u5, "bmask", [P, 3 * P])
                e_t = sb(u5, "e_t", [P, 2, S + M])
                with ExitStack() as u5a:
                    e_s = sb(u5a, "e_s", [P, 3, S + M])
                    e_pt = sb(u5a, "e_pt", [P, 6, S])
                    e_gate_u = sb(u5a, "e_gate_u", [P, 3, S + M])
                with ExitStack() as u5b:
                    e_raw = sb(u5b, "e_raw", [P, 4, S + M])
        with ExitStack() as u7:
            d_s = sb(u7, "d_s", [P, 3, S + M])
            d_pt = sb(u7, "d_pt", [P, 6, S])
            with ExitStack() as u6:
                d_k = sb(u6, "d_k", [P, CC, S + M])
                d_vt = sb(u6, "d_vt", [P, 6, 4 * P])
                d_q = sb(u6, "d_q", [P, CC, S])
                d_g = sb(u6, "d_g", [P, CC, S])
                c_g = sb(u6, "c_g", [P, CC, S])
                c_u = sb(u6, "c_u", [P, CC, S + CT - 1])
                c_y = sb(u6, "c_y", [P, CC, S])
        with ExitStack() as u8:
            sb(u8, "context", [P, KC * M])
            d_v = sb(u8, "d_v", [P, CC, S + M])
        banks = [ctx.enter_context(nc.psum_tensor(f"bank{i}", [P, 512], f32)) for i in range(BANKS)]

        def C(name, a=0, b=None):
            at, w = cc[name]
            return con[:, at + a:at + (w if b is None else b)]

        def G(name, c):
            return par[:, pc[name][0] + c:pc[name][0] + c + 1]

        def head(ap, h):
            return ap[:, P * h:P * h + P]

        ones, ident = C("ones"), C("ident")
        filled, freed = book.filled, book.freed

        def claim(pe, *key, hold=False):
            return book.claim(pe, banks, *key, hold=hold)

        def bank(eng, *key):
            return book.bank(eng, banks, *key)

        tiles = book.known.tiles if book.known else UNROLL * 2
        turns = tiles // UNROLL

        def load_tile(sp, t, slot, first):
            if not first:
                sp.wait_ge(sem("w_split"), t - (RAW - 1))
            sp.dma_start(w_raw[:, slot, :], dram["w_tiles"][t]).then_inc(sem(f"w_loaded{slot}"), 16)

        def load_weights(sp):
            for t in range(RAW):
                load_tile(sp, t, t, True)
            with sp.Fori(1, tiles // RAW, 1) as n:
                for s in range(RAW):
                    load_tile(sp, n * RAW + s, s, False)
            for t in range(RAW * (tiles // RAW), tiles):
                load_tile(sp, t, t % RAW, False)

        def wait_tile(eng, t, uses, raw, first):
            eng.wait_ge(sem(f"w_loaded{raw}"), 16 * uses)
            if not first:
                eng.wait_ge(sem("w_used"), t - (SPLIT - 1))

        def split_tile(pool, t, uses, raw, slot, first, rounder, before):
            if rounder == "gpsimd":
                wait_tile(pool, t, uses, raw, first)
                zero = C("zero").broadcast_to([P, KC * P])
                nc.gpsimd.tensor_tensor(w_hi[:, slot, :], w_raw[:, raw, :], zero, ALU.add)\
                  .then_inc(sem("w_rounded_gpsimd"), 1)
            pool.wait_ge(sem(f"w_rounded_{rounder}"), t + 1 - before)
            nc.gpsimd.tensor_tensor(w_lo[:, slot, :], w_raw[:, raw, :], w_hi[:, slot, :].bitcast(f32),
                                    ALU.subtract).then_inc(sem("w_split"), 1)

        def split_range(pool, start, end, rounder, before):
            head_end, tail = min(-(-start // UNROLL) * UNROLL, end), end // UNROLL * UNROLL
            if start == 0:
                head_end = UNROLL
            for t in range(start, head_end):
                split_tile(pool, t, t // RAW + 1, t % RAW, t % SPLIT, t < SPLIT, rounder, before)
            if head_end < tail:
                with pool.Fori(head_end // UNROLL, tail // UNROLL, 1) as n:
                    for s in range(UNROLL):
                        split_tile(pool, n * UNROLL + s, n * SPLIT + s // RAW + 1, s % RAW, s % SPLIT, False, rounder, before)
            for t in range(max(head_end, tail), end):
                split_tile(pool, t, t // RAW + 1, t % RAW, t % SPLIT, False, rounder, before)

        def split_weights(pool):
            pool.wait_ge(*when("params", 1))
            start = 0
            for l in range(DEPTH):
                kv = first_tile("w_xkv", l)
                split_range(pool, start, kv, "gpsimd", 2 * KC * l)
                split_range(pool, kv, kv + 2 * KC, "scalar", kv - 2 * KC * l)
                start = kv + 2 * KC
            split_range(pool, start, max(tiles, start), "gpsimd", 2 * KC * DEPTH)

        def round_tile_act(act, t):
            wait_tile(act, t, t // RAW + 1, t % RAW, False)
            act.activation(w_hi[:, t % SPLIT, :], w_raw[:, t % RAW, :], ACT.Copy).then_inc(sem("w_rounded_scalar"), 1)

        blocks = [0]

        def product(pe, *args, **options):
            for _ in product_steps(pe, *args, **options):
                pass

        def product_steps(pe, key, inputs, kc=KC, width=P, need=None):
            outs = [claim(pe, name, *key, hold=True) for name, _, _, _ in inputs]
            for k in range(kc):
                t, b = divmod(blocks[0], KC)
                if b == 0:
                    pe.wait_ge(sem("w_split"), t + 1)
                if need:
                    for event in need(k):
                        pe.wait_ge(*when(*event))
                wh = w_hi[:, t % SPLIT, b * P:b * P + width]
                wl = w_lo[:, t % SPLIT, b * P:b * P + width]
                for i, (name, hi, lo, n) in enumerate(inputs):
                    o = outs[i][:width, :n]
                    pe.matmul(o, wh, hi[:, k, :n], start=k == 0, stop=False)
                    pe.matmul(o, wh, lo[:, k, :n], start=False, stop=False)
                    mm = pe.matmul(o, wl, hi[:, k, :n], start=False, stop=k == kc - 1)
                    last = i == len(inputs) - 1
                    if k == kc - 1 and not last:
                        mm.then_inc(*filled(name, *key))
                if b == KC - 1:
                    mm.then_inc(*book.tile_used(*((name, *key) if k == kc - 1 else ())))
                elif k == kc - 1:
                    mm.then_inc(*filled(name, *key))
                blocks[0] += 1
                if k == kc - 1:
                    for name, _, _, _ in inputs:
                        book.release(name, *key)
                yield

        def pre_norm_act(act, key, gain, src, hi, n, sources):
            for c in range(KC):
                high_act(act, key, gain, src, hi, n, sources, c)
            squares_act(act, key, lambda c: src[:, c, :n], n)
            rms_act(act, key, n)

        def high_act(act, key, gain, src, hi, n, sources, c):
            act.wait_ge(*when(*sources(c)))
            act.activation(hi[:, c, :n], src[:, c, :n], ACT.Copy, scale=G(gain, c)).then_inc(*done("hi", *key, c))

        def squares_act(act, key, src, n, wait=None):
            for c in range(KC):
                if wait:
                    act.wait_ge(*when(*wait(c)))
                if c >= 2:
                    act.wait_ge(*when("sq_added", *key, c - 2))
                act.activation(sq[:, c % 2, :n], src(c), ACT.Square).then_inc(*done("sq", *key, c))

        def rms_act(act, key, n, scale=1.0 / D):
            b = bank(act, "ssq", *key)
            act.activation(col[:, 0:n // P], b[:, 0:n // P], ACT.Sqrt, bias=C("eps"), scale=scale)\
               .then_inc(*freed("ssq", *key, also=("rms", *key)))

        def rstd_act(act, key, n):
            b = bank(act, "rstd", *key)
            act.activation(rstd[:, :n], b[:, :n], ACT.Copy).then_inc(*freed("rstd", *key, also=("rstd_in", *key)))

        def sum_squares_dve(dve, key, n):
            for c in range(KC):
                dve.wait_ge(*when("sq", *key, c))
                if c == 0:
                    op = dve.tensor_copy(sqacc[:, :n], sq[:, 0, :n])
                else:
                    dve.wait_ge(*when("sq_added", *key, c - 1))
                    op = dve.tensor_tensor(sqacc[:, :n], sqacc[:, :n], sq[:, c % 2, :n], ALU.add)
                op.then_inc(*done("sq_added", *key, c))

        def spread_dve(dve, key, n):
            m = n // P
            dve.wait_ge(*when("rms", *key))
            dve.reciprocal(col[:, 4:4 + m], col[:, 0:m]).then_inc(*done("rrms", *key))
            dve.wait_ge(*when("rrms", *key))
            for t in range(m):
                op = dve.tensor_scalar(spread[:, P * t:P * t + P], ident, col[:, 4 + t:5 + t], None, ALU.mult)
            op.then_inc(*done("spread", *key))

        def low_dve(dve, key, gain, src, hi, lo, n, c):
            dve.wait_ge(*when("hi", *key, c))
            dve.scalar_tensor_tensor(out=lo[:, c, :n], in0=src[:, c, :n], scalar=G(gain, c),
                                     in1=hi[:, c, :n].bitcast(f32), op0=ALU.mult, op1=ALU.subtract)\
               .then_inc(*done("lo", *key, c))

        def pre_norm_dve(dve, key, gain, src, hi, lo, n):
            for c in range(KC):
                low_dve(dve, key, gain, src, hi, lo, n, c)
            sum_squares_dve(dve, key, n)
            spread_dve(dve, key, n)

        def load_sqrt_act(act):
            act.activation(col[:, 15:16], C("eps"), ACT.Sqrt)

        def post_norm_act(act, key, y, between=None, rms=True):
            for c in range(KC):
                if between:
                    between(c)
                if c == KC - 1:
                    load_sqrt_act(act)
                b = bank(act, "y", *key, c)
                if c >= 2:
                    act.wait_ge(*when("sq_added", *key, c - 2))
                act.activation(sq[:, c % 2, :], b[:, :], ACT.Square).then_inc(*done("sq", *key, c))
                act.activation(y[:, c, :], b[:, :], ACT.Copy).then_inc(*freed("y", *key, c, also=("y_in", *key, c)))
            if rms:
                rms_act(act, key, S)

        def between_layers_dve(dve, post, post_gain, y, pre, pre_gain):
            sum_squares_dve(dve, post, S)
            spread_dve(dve, post, S)
            b = bank(dve, "rstd", *post)
            for c in range(KC + 2):
                if c < KC:
                    post_scale_dve(dve, post, post_gain, y, b, c)
                    post_add_dve(dve, post, y, c)
                if c >= 2 and pre:
                    low_dve(dve, pre, pre_gain, hT, a_hi, a_lo, S, c - 2)
            if pre:
                sum_squares_dve(dve, pre, S)
                spread_dve(dve, pre, S)

        def post_scale_dve(dve, key, gain, y, b, c):
            dve.wait_ge(*when("y_in", *key, c))
            dve.scalar_tensor_tensor(out=y[:, c, :], in0=y[:, c, :], scalar=G(gain, c), in1=b[:, :],
                                     op0=ALU.mult, op1=ALU.mult)\
               .then_inc(*(freed("rstd", *key, also=("y_normed", *key, c)) if c == KC - 1
                           else done("y_normed", *key, c)))

        def post_add_dve(dve, key, y, c):
            dve.wait_ge(*when("y_normed", *key, c))
            dve.tensor_tensor(hT[:, c, :], hT[:, c, :], y[:, c, :], ALU.add).then_inc(*done("h", *key, c))

        def post_apply_dve(dve, key, gain, y):
            b = bank(dve, "rstd", *key)
            for c in range(KC):
                post_scale_dve(dve, key, gain, y, b, c)
                post_add_dve(dve, key, y, c)

        def split_act(act, src, c, key, n=S, hi=None):
            act.activation((a_hi if hi is None else hi)[:, c, :n], src, ACT.Copy).then_inc(*done("hi", *key, c))

        def split_dve(dve, src, c, key, n=S, hi=None, lo=None):
            dve.wait_ge(*when("hi", *key, c))
            dve.tensor_tensor((a_lo if lo is None else lo)[:, c, :n], src,
                              (a_hi if hi is None else hi)[:, c, :n].bitcast(f32), ALU.subtract)\
               .then_inc(*done("lo", *key, c))

        def inputs_ready(key):
            return lambda k: [("hi", *key, k), ("lo", *key, k)]

        def att_scores_pe(pe, key, u, unit):
            for i, (k0, nk, mms, _) in enumerate(unit["parts"]):
                b = claim(pe, "s", *key, u, i)
                for j, (q, k) in enumerate(mms):
                    mm = pe.matmul(b[:, :nk], q, k, start=j == 0, stop=j == len(mms) - 1)
                mm.then_inc(*filled("s", *key, u, i))

        def att_turn_pe(pe, key, u, unit, s):
            pe.wait_ge(*when("p", *key, u))
            c = 0
            for i, (k0, nk, _, _) in enumerate(unit["parts"]):
                b = claim(pe, "pt", *key, u, i)
                for j in range(nk // P):
                    mm = pe.transpose(b[:, P * j:P * j + P], s[:, u % s.shape[1], c:c + P], ident)
                    c += P
                mm.then_inc(*filled("pt", *key, u, i))

        def att_values_pe(pe, key, units, us, pt, vt):
            for u in us:
                for i in range(len(units[u]["parts"])):
                    pe.wait_ge(*when("pt_in", *key, u, i))
            head_no = units[us[0]]["head"]
            spans = {}
            for u in us:
                for k0, nk, _, _ in units[u]["parts"]:
                    for kt in range(k0 // P, (k0 + nk) // P):
                        q0 = units[u]["q0"]
                        lo, hi = spans.get(kt, (q0, q0))
                        spans[kt] = (min(lo, q0), max(hi, q0 + P))
            order = sorted(spans, key=lambda kt: spans[kt][0] - spans[kt][1])
            base = units[us[0]]["q0"]
            for o in range(len(vt(0, head_no))):
                b = claim(pe, "o", *key, us[-1], o)
                for n, kt in enumerate(order):
                    lo, hi = spans[kt]
                    v = vt(kt, head_no)[o]
                    mm = pe.matmul(b[:v.shape[-1], lo - base:hi - base], v, pt[:, kt, lo - base:hi - base],
                                   start=n == 0, stop=n == len(order) - 1, skip_group_check=True)
                mm.then_inc(*filled("o", *key, us[-1], o))

        def head_end(units, u):
            return u == len(units) - 1 or units[u + 1]["group"] != units[u]["group"]

        def group_of(units, u):
            return [v for v in range(u + 1) if units[v]["group"] == units[u]["group"]]

        def attention_pe(pe, key, units, s, pt, vt, need=(), fill=None, blocks=None):
            for event in need:
                pe.wait_ge(*when(*event))
            ahead = s.shape[1] - 1
            pending = None
            for u in range(len(units) + ahead + 1):
                if u < len(units):
                    att_scores_pe(pe, key, u, units[u])
                if fill:
                    for _ in range(blocks(u)):
                        next(fill, None)
                if pending is not None:
                    att_values_pe(pe, key, units, group_of(units, pending), pt, vt)
                    pending = None
                v = u - ahead
                if 0 <= v < len(units):
                    att_turn_pe(pe, key, v, units[v], s)
                    if head_end(units, v):
                        pending = v
            if fill:
                for _ in fill:
                    pass

        def att_col(u, i):
            return col[:, 16 + 8 * (u % 2) + i:17 + 8 * (u % 2) + i]

        def attention_dve(dve, key, units, s, before=None, between=None):
            ns = s.shape[1]

            def maxima(u):
                parts = units[u]["parts"]
                if u >= ns:
                    dve.wait_ge(*when("bank_filled", "pt", *key, u - ns, len(units[u - ns]["parts"]) - 1))
                c = 0
                for i, (k0, nk, _, mask) in enumerate(parts):
                    b = bank(dve, "s", *key, u, i)
                    m = C("zero").broadcast_to([P, nk]) if mask is None else mask
                    if i:
                        dve.wait_ge(*when("s_in", *key, u, i - 1))
                    first = units[u]["sink"] if units[u].get("sink") is not None else -3.0e38
                    dve.tensor_tensor_reduce(s[:, u % ns, c:c + nk], b[:, :nk], m, 1.0,
                                             att_col(u, i - 1) if i else first, ALU.add, ALU.max,
                                             att_col(u, i))\
                       .then_inc(*freed("s", *key, u, i, also=("s_in", *key, u, i)))
                    c += nk
                dve.wait_ge(*when("s_in", *key, u, len(parts) - 1))
                if u >= 2:
                    dve.wait_ge(*when("p", *key, u - 2))
                dve.tensor_scalar(att_col(u, 2), att_col(u, len(parts) - 1), -1.0, None, ALU.mult)\
                   .then_inc(*done("max", *key, u))

            def divide(u):
                n = sum(nk for _, nk, _, _ in units[u]["parts"])
                dve.wait_ge(*when("exp", *key, u))
                if units[u].get("sink") is not None:
                    dve.tensor_tensor(att_col(u, 3), att_col(u, 3), att_col(u, 5), ALU.add)\
                       .then_inc(*done("sum_sink", *key, u))
                    dve.wait_ge(*when("sum_sink", *key, u))
                dve.reciprocal(att_col(u, 4), att_col(u, 3)).then_inc(*done("rsum", *key, u))
                dve.wait_ge(*when("rsum", *key, u))
                dve.tensor_scalar(s[:, u % ns, :n], s[:, u % ns, :n], att_col(u, 4), None, ALU.mult)\
                   .then_inc(*done("p", *key, u))

            for u in range(len(units) + 1):
                if u < len(units):
                    if before:
                        before(u)
                    maxima(u)
                if u:
                    divide(u - 1)
                if between:
                    between(u)

        def attention_act(act, key, units, s, pt, take, between=None):
            ns = s.shape[1]
            pending = None
            for u in range(len(units) + ns):
                if u < len(units):
                    n = sum(nk for _, nk, _, _ in units[u]["parts"])
                    act.wait_ge(*when("max", *key, u))
                    if units[u].get("sink") is not None:
                        act.activation(att_col(u, 5), units[u]["sink"], ACT.Exp, bias=att_col(u, 2))\
                           .then_inc(*done("exp_sink", *key, u))
                    act.activation(s[:, u % ns, :n], s[:, u % ns, :n], ACT.Exp, bias=att_col(u, 2),
                                   accum_out=att_col(u, 3)).then_inc(*done("exp", *key, u))
                if between:
                    between(u)
                if pending is not None:
                    take(act, pending)
                    pending = None
                v = u - ns + 1
                if 0 <= v < len(units):
                    unit = units[v]
                    for i, (k0, nk, _, _) in enumerate(unit["parts"]):
                        b = bank(act, "pt", *key, v, i)
                        base = units[group_of(units, v)[0]]["q0"]
                        q0 = unit["q0"] - base
                        act.activation(pt[:, k0 // P:(k0 + nk) // P, q0:q0 + P],
                                       b[:, :nk].rearrange("p (k q) -> p k q", q=P), ACT.Copy)\
                           .then_inc(*freed("pt", *key, v, i, also=("pt_in", *key, v, i)))
                    if head_end(units, v):
                        pending = v

        JOBS = [job for job in in_jobs() if job[0][:2] != "gg"]
        EARLY = (13, 15, 18, 20)
        GDN = [n for n, _, _ in JOBS if n[:2] in ("gk", "gq", "gv")]

        def g_index(name):
            return 3 * int(name[2]) + {"gq": 0, "gk": 1, "gv": 2}[name[:2]]

        def conv_index(name):
            return int(name[2]) + {"gq": 0, "gk": 4, "gv": 8}[name[:2]]

        def att_units(l):
            units = []
            for h in range(AH):
                lo = AD * (h % 2)
                for t in range(TT):
                    q = a_qk[lo:lo + AD, 2 * (h // 2), P * t:P * t + P]
                    k = a_qk[lo:lo + AD, 2 * (h // 2) + 1, 0:P * (t + 1)]
                    units.append({"head": h, "group": h, "q0": P * t,
                                  "parts": [(0, P * (t + 1), [(q, k)], cmask[:, P * (TT - 1 - t):S])]})
            return units

        def in_product_pe(pe, l):
            for i, (name, _, width) in enumerate(JOBS):
                product(pe, (l,), [(name, a_hi, a_lo, S)], width=width,
                        need=inputs_ready(("mix", l)) if i == 0 else None)
                if i == 2:
                    ssq_pe(pe, ("mix", l), S)
                if i == 4:
                    rstd_pe(pe, ("mix", l), S)
                for c, first in enumerate(EARLY):
                    if i == first + 2:
                        modulation_sum_pe(pe, l, c)

        def in_product_dve(dve, l):
            for r in range(2):
                dve.memset(pad[:, r, 0:GK - 1], 0.0).then_inc(*done("pad_zero", l, r))
            dve.wait_ge(*when("pad_zero", l, 1))
            dve.wait_ge(*when("rstd_in", "mix", l))
            for job, (name, _, width) in enumerate(JOBS):
                b = bank(dve, name, l)
                kind = name[:2]
                if name in GDN:
                    i = GDN.index(name)
                    x, y, w = pad[:, i % 2, :], acc[:, i % 2, :], conv_index(name) * GK
                    dve.tensor_tensor(x[:, GK - 1:GK - 1 + S], b[:, :], rstd[:, :], ALU.mult)\
                       .then_inc(*freed(name, l, also=("conv_in", l, i)))
                    dve.wait_ge(*when("conv_in", l, i))
                    if i >= 2:
                        dve.wait_ge(*when("silu", l, i - 2))
                    for j in range(GK):
                        tap = G(f"conv_gdn{l}", w + j)
                        if j == 0:
                            op = dve.tensor_scalar(y, x[:, 0:S], tap, None, ALU.mult)
                        else:
                            dve.wait_ge(*when("tap", l, i, j - 1))
                            op = dve.scalar_tensor_tensor(out=y, in0=x[:, j:j + S], scalar=tap, in1=y,
                                                          op0=ALU.mult, op1=ALU.add)
                        op.then_inc(*done("tap", l, i, j))
                elif kind == "ab":
                    dve.tensor_tensor(ab[:, :], b[0:2 * GH, :], rstd[0:2 * GH, :], ALU.mult)\
                       .then_inc(*freed(name, l, also=("ab_in", l)))
                elif kind in ("aq", "ak"):
                    c = int(name[2])
                    dve.scalar_tensor_tensor(out=a_qk[:, 2 * c + (kind == "ak"), :], in0=b[:, :],
                                             scalar=AD ** -0.5 if kind == "aq" else 1.0, in1=rstd[:, :],
                                             op0=ALU.mult, op1=ALU.mult)\
                       .then_inc(*freed(name, l, also=("qk_in", l, 2 * c + (kind == "ak"))))
                elif kind == "av":
                    dve.tensor_tensor(a_v[:, int(name[2]), :], b[:, :], rstd[:, :], ALU.mult)\
                       .then_inc(*freed(name, l, also=("av_in", l, int(name[2]))))
                elif kind in ("cg", "cx", "cb"):
                    j = ("cg", "cx", "cb").index(kind)
                    if j == 0 and name[2] == "1":
                        dve.wait_ge(*when("short", l, 0))
                    dve.tensor_tensor(cv_in[:, j, :], b[:, :], rstd[:, :], ALU.mult)\
                       .then_inc(*freed(name, l, also=(kind, l, int(name[2]))))
                    if kind == "cb":
                        short_conv_dve(dve, l, int(name[2]))
                if job in EARLY:
                    modulation_sum_dve(dve, l, EARLY.index(job))

        def gate_steps(pe, l):
            for h in range(GH):
                yield from product_steps(pe, (l,), [(f"gg{h}", a_hi, a_lo, S)])

        def gate_take_dve(dve, l, u):
            h, rest = divmod(u + 1, KC // 2)
            if rest == 0 and 1 <= h <= GH:
                b = bank(dve, f"gg{h - 1}", l)
                dve.tensor_tensor(g_gate[:, h - 1, :], b[:, :], rstd[:, :], ALU.mult)\
                   .then_inc(*freed(f"gg{h - 1}", l, also=("gate_in", l, h - 1)))

        def gate_act(act, l):
            for h in range(GH):
                act.wait_ge(*when("gate_in", l, h))
                act.activation(g_gate[:, h, :], g_gate[:, h, :], ACT.Silu).then_inc(*done("gate", l, h))

        def short_conv_dve(dve, l, c):
            x, y = pad[:, c, :], acc[:, c, :]
            dve.wait_ge(*when("cx", l, c))
            dve.wait_ge(*when("silu", l, len(GDN) - 1))
            dve.tensor_tensor(x[:, GK - 1:GK - 1 + S], cv_in[:, 0, :], cv_in[:, 1, :], ALU.mult)\
               .then_inc(*done("short_in", l, c))
            dve.wait_ge(*when("short_in", l, c))
            for j in range(CK):
                tap = G(f"conv_short{l}", CK * c + j)
                xs = x[:, GK - CK + j:GK - CK + j + S]
                if j == 0:
                    op = dve.tensor_scalar(y, xs, tap, None, ALU.mult)
                else:
                    dve.wait_ge(*when("short_tap", l, c, j - 1))
                    op = dve.scalar_tensor_tensor(out=y, in0=xs, scalar=tap, in1=y, op0=ALU.mult, op1=ALU.add)
                op.then_inc(*done("short_tap", l, c, j))
            dve.wait_ge(*when("short_tap", l, c, CK - 1))
            dve.wait_ge(*when("cb", l, c))
            dve.tensor_tensor(tmp[:, 2 + c, :], cv_in[:, 2, :], y, ALU.mult).then_inc(*done("short", l, c))

        def in_product_act(act, l):
            for i, name in enumerate(GDN):
                act.wait_ge(*when("tap", l, i, GK - 1))
                act.activation(g_qkv[:, g_index(name), :], acc[:, i % 2, :], ACT.Silu).then_inc(*done("silu", l, i))
            squares_of_act(act, l)
            for c in range(len(EARLY)):
                if c + 2 < len(EARLY):
                    modulation_load_act(act, l, c + 2)
                modulation_bias_act(act, l, c)

        def att_prep_pe(pe, l):
            for i in range(4):
                pe.wait_ge(*when("qk_in", l, i))
                b = claim(pe, "swap", l, i)
                pe.matmul(b[:, :], C("rope1"), a_qk[:, i, :], start=True, stop=True).then_inc(*filled("swap", l, i))
            pe.wait_ge(*when("av_in", l, 0))
            pe.wait_ge(*when("av_in", l, 1))
            for g in range(2):
                b = claim(pe, "avt", l, g)
                for t in range(2):
                    for c in range(2):
                        mm = pe.transpose(b[:, P * (2 * t + c):P * (2 * t + c) + P],
                                          a_v[:, c, P * (2 * g + t):P * (2 * g + t) + P], ident)
                mm.then_inc(*filled("avt", l, g))

        def att_prep_dve(dve, l):
            dve.wait_ge(*when("rope_table", 1))
            for i in range(4):
                b = bank(dve, "swap", l, i)
                dve.tensor_tensor(s_buf[:, i % 2, :], b[:, :], rope_t[:, 1, :], ALU.mult)\
                   .then_inc(*freed("swap", l, i, also=("swapped", l, i)))
                dve.tensor_tensor(a_qk[:, i, :], a_qk[:, i, :], rope_t[:, 0, :], ALU.mult)\
                   .then_inc(*done("cos_part", l, i))
                if i == 2:
                    gdn_rates_dve(dve, l)
                dve.wait_ge(*when("swapped", l, i))
                dve.wait_ge(*when("cos_part", l, i))
                dve.tensor_tensor(a_qk[:, i, :], a_qk[:, i, :], s_buf[:, i % 2, :], ALU.add)\
                   .then_inc(*done("roped", l, i))
            gdn_decay_dve(dve, l)
            dve.wait_ge(*when("roped", l, 3))

        def att_prep_act(act, l):
            act.dma_start(cmask[:, :], dram["count_mask"]).then_inc(*loaded("cmask", l))
            for g in range(2):
                b = bank(act, "avt", l, g)
                act.activation(a_vt[:, 2 * g:2 * g + 2, :], b[:, :].rearrange("p (t n) -> p t n", t=2), ACT.Copy)\
                   .then_inc(*freed("avt", l, g, also=("avt_in", l, g)))

        def att_take_act(l):
            def take(act, u):
                h = u // TT
                b = bank(act, "o", "att", l, u, 0)
                act.activation(tmp[AD * (h % 2):AD * (h % 2) + AD, h // 2, :], b[0:AD, :], ACT.Copy)\
                   .then_inc(*freed("o", "att", l, u, 0, also=("att_out", l, h)))
            return take

        def ssq_pe(pe, key, n):
            pe.wait_ge(*when("sq_added", *key, KC - 1))
            b = claim(pe, "ssq", *key)
            for t in range(n // P):
                mm = pe.matmul(b[:, t:t + 1], sqacc[:, P * t:P * t + P], ones[:, 0:1], start=True, stop=True)
            mm.then_inc(*filled("ssq", *key))

        def rstd_pe(pe, key, n):
            pe.wait_ge(*when("spread", *key))
            b = claim(pe, "rstd", *key)
            pe.matmul(b[:, :n], ones, spread[:, :n], start=True, stop=True).then_inc(*filled("rstd", *key))

        AB, Z, EX, GL, BE, L2, DC, CD, KD, NB, NA = 32, 64, 80, 96, 112, 128, 160, 192, 208, 224, 240
        NH = TT * GH

        def cols(at, n=NH):
            return col[:, at:at + n]

        def colnh(at, n, h):
            return col[:, at + GH * n + h:at + GH * n + h + 1]

        def by_head(first, n):
            return g_qkv[:, first:12:3, P * n:P * n + P]

        def banked(b):
            return b[:, :].rearrange("p (h n) -> p h n", h=GH)

        def over_heads(ap):
            return ap[:, None, :].broadcast_to([P, GH, P])

        ROWS = ("decay", "rk", "rq", "beta")

        def square_of(i):
            return tmp[:, 4 + i, :] if i < GH else p_t[:, i - GH, :]

        def gdn_first_pe(pe, l):
            b = claim(pe, "l2", l)
            for i in range(2 * GH):
                pe.wait_ge(*when("l2_sq", l, i))
                w, h = divmod(i, GH)
                for n in range(TT):
                    at = NH * w + GH * n + h
                    mm = pe.matmul(b[:, at:at + 1], square_of(i)[:, P * n:P * n + P], ones[:, 0:1],
                                   start=True, stop=True)
            mm.then_inc(*filled("l2", l))
            pe.wait_ge(*when("ab_in", l))
            b = claim(pe, "abt", l)
            for n in range(TT):
                mm = pe.transpose(b[:, 8 * n:8 * n + 8], ab[0:8, P * n:P * n + P], ident[0:8, 0:8])
            mm.then_inc(*filled("abt", l))

        def gdn_decay_pe(pe, l):
            pe.wait_ge(*when("g", l))
            b = claim(pe, "decay", l)
            pe.matmul(b[:, 0:NH], C("upto"), cols(GL), start=True, stop=True)
            pe.matmul(b[:, NH:2 * NH], ones, cols(GL), start=True, stop=True).then_inc(*filled("decay", l))

        def gdn_pe(pe, l):
            for n in range(TT):
                for w, name in enumerate(ROWS):
                    pe.wait_ge(*when("diag", l, n, w))
                    b = claim(pe, "row", l, n, w)
                    pe.matmul(b[:, :], ones, (spread if w % 2 == 0 else sqacc)[:, :], start=True, stop=True)\
                      .then_inc(*filled("row", l, n, w))
            for n in range(TT):
                pe.wait_ge(*when("normed", l, n, 0))
                pe.wait_ge(*when("normed", l, n, 1))
                tok = slice(P * n, P * n + P)
                b = claim(pe, "kk", l, n)
                for h in range(GH):
                    k = g_qkv[:, 3 * h + 1, tok]
                    mm = pe.matmul(head(b, h), k, k, start=True, stop=True)
                mm.then_inc(*filled("kk", l, n))
                b = claim(pe, "kq", l, n)
                for h in range(GH):
                    mm = pe.matmul(head(b, h), g_qkv[:, 3 * h + 1, tok], g_qkv[:, 3 * h, tok], start=True, stop=True)
                mm.then_inc(*filled("kq", l, n))
                for name, j in (("kt", 1), ("vt", 2)):
                    b = claim(pe, name, l, n)
                    for h in range(GH):
                        mm = pe.transpose(head(b, h), g_qkv[:, 3 * h + j, tok], ident)
                    mm.then_inc(*filled(name, l, n))
            for n in range(TT):
                pe.wait_ge(*when("xt", l, 0, n))
                b = claim(pe, "x1", l, n)
                for h in range(GH):
                    mm = pe.transpose(head(b, h), head(xt_inv[:, n, :], h), ident)
                mm.then_inc(*filled("x1", l, n))
            for s in range(1, 7):
                for n in range(TT):
                    pe.wait_ge(*when("level", l, s, n))
                    pe.wait_ge(*when("x", l, s - 1, n))
                    b = claim(pe, "y", l, s, n)
                    for h in range(GH):
                        mm = pe.matmul(head(b, h), head(tmp[:, 4 + n, :], h), head(x_inv[:, n, :], h),
                                       start=True, stop=True)
                    mm.then_inc(*filled("y", l, s, n))
                for n in range(TT):
                    pe.wait_ge(*when("y_in", l, s, n))
                    pe.wait_ge(*when("xt", l, s - 1, n))
                    if s < 6:
                        b = claim(pe, "px", l, s, n)
                        for h in range(GH):
                            mm = pe.matmul(head(b, h), head(xt_inv[:, n, :], h), head(yv[:, n, :], h),
                                           start=True, stop=True)
                        mm.then_inc(*filled("px", l, s, n))
                    b = claim(pe, "pxt", l, s, n)
                    for h in range(GH):
                        mm = pe.matmul(head(b, h), head(yv[:, n, :], h), head(xt_inv[:, n, :], h),
                                       start=True, stop=True)
                    mm.then_inc(*filled("pxt", l, s, n))
            for n in range(TT):
                tok = slice(P * n, P * n + P)
                st = state[:, (n - 1) % 2, :]
                if n:
                    pe.wait_ge(*when("state", l, n - 1))
                    b = claim(pe, "ks", l, n)
                    for h in range(GH):
                        mm = pe.matmul(head(b, h), g_qkv[:, 3 * h + 1, tok], head(st, h), start=True, stop=True)
                    mm.then_inc(*filled("ks", l, n))
                    out_sums_pe(pe, l, n - 1)
                    pe.wait_ge(*when("rhs", l, n))
                else:
                    pe.wait_ge(*when("vbeta", l, 0))
                pe.wait_ge(*when("xt", l, 6, n))
                rhs = yv[:, n % 2, :] if n else v_beta[:, 0, :]
                b = claim(pe, "vn", l, n)
                for h in range(GH):
                    mm = pe.matmul(head(b, h), head(xt_inv[:, n, :], h), head(rhs, h), start=True, stop=True)
                mm.then_inc(*filled("vn", l, n))
                pe.wait_ge(*when("vn_in", l, n))
                vn = yv[:, 2 + n % 2, :]
                if n < TT - 1:
                    b = claim(pe, "su", l, n)
                    for h in range(GH):
                        mm = pe.matmul(head(b, h), head(k_dec[:, n, :], h), head(vn, h), start=True, stop=True)
                    mm.then_inc(*filled("su", l, n))
                pe.wait_ge(*when("q_dec", l, n))
                b = claim(pe, "go", l, n)
                for h in range(GH):
                    if n:
                        pe.matmul(head(b, h), head(st, h), g_qkv[:, 3 * h, tok], start=True, stop=False)
                    mm = pe.matmul(head(b, h), head(vn, h), head(attn_t[:, n, :], h), start=n == 0, stop=True)
                mm.then_inc(*filled("go", l, n))
                if n:
                    out_row_pe(pe, l, n - 1)
            out_sums_pe(pe, l, TT - 1)
            out_row_pe(pe, l, TT - 1)

        def out_sums_pe(pe, l, n):
            pe.wait_ge(*when("o_sq", l, n))
            b = claim(pe, "l2o", l, n)
            for h in range(GH):
                mm = pe.matmul(b[:, h:h + 1], head(tmp[:, 4 + n, :], h), ones[:, 0:1], start=True, stop=True)
            mm.then_inc(*filled("l2o", l, n))

        def out_row_pe(pe, l, n):
            pe.wait_ge(*when("o_diag", l, n))
            b = claim(pe, "o_row", l, n)
            pe.matmul(b[:, :], ones, (spread if n % 2 == 0 else sqacc)[:, :], start=True, stop=True)\
              .then_inc(*filled("o_row", l, n))

        def squares_of_act(act, l):
            for i in range(2 * GH):
                w, h = divmod(i, GH)
                act.wait_ge(*when("silu", l, len(GDN) - 1))
                act.activation(square_of(i), g_qkv[:, 3 * h + w, :], ACT.Square).then_inc(*done("l2_sq", l, i))

        def gdn_first_act(act, l):
            b = bank(act, "l2", l)
            act.activation(cols(L2), b[:, 0:NH], ACT.Sqrt, bias=C("eps_q"), scale=float(GD)).then_inc(*done("rms_q", l))
            act.activation(cols(L2 + NH), b[:, NH:2 * NH], ACT.Sqrt, bias=C("eps"))\
               .then_inc(*freed("l2", l, also=("rms_k", l)))
            act.wait_ge(*when("abs_z", l))
            act.activation(cols(EX), cols(EX), ACT.Exp, scale=-1.0).then_inc(*done("exp_z", l))
            act.activation(cols(BE).rearrange("p (n h) -> p n h", h=GH),
                           cols(AB, 2 * NH).rearrange("p (n h) -> p n h", h=2 * GH)[:, :, GH:2 * GH],
                           ACT.Exp, scale=-1.0).then_inc(*done("exp_b", l))
            act.activation(cols(NA, GH), par[:, pc[f"a_log{l}"][0]:pc[f"a_log{l}"][0] + GH], ACT.Exp)\
               .then_inc(*done("exp_a", l))
            act.wait_ge(*when("exp_z", l))
            act.activation(cols(EX), cols(EX), ACT.Ln, bias=ones[:, 0:1]).then_inc(*done("ln_z", l))

        def gdn_decay_act(act, l):
            act.wait_ge(*when("kd", l))
            act.activation(cols(CD), cols(DC + NH), ACT.Exp).then_inc(*done("chunk_decay", l))
            act.activation(cols(KD), cols(KD), ACT.Exp).then_inc(*done("k_decay", l))
            act.activation(cols(NB), cols(DC), ACT.Exp).then_inc(*done("exp_d", l))

        def gdn_act(act, l):
            for n in range(TT):
                b = bank(act, "row", l, n, 0)
                act.activation(dec[:, n, :], b[:, :], ACT.Exp).then_inc(*done("dec", l, n))
                act.wait_ge(*when("rel_in", l, n))
                act.activation(rel_t[:, n, :], rel_t[:, n, :], ACT.Exp).then_inc(*done("rel", l, n))
            for n in range(TT):
                act.wait_ge(*when("k_decay", l))
                b = bank(act, "kt", l, n)
                for h in range(GH):
                    op = act.activation(head(k_dec[:, n, :], h), head(b, h), ACT.Copy, scale=colnh(KD, n, h))
                op.then_inc(*freed("kt", l, n, also=("kdec", l, n)))
                if n == 0:
                    act.wait_ge(*when("beta", l))
                b = bank(act, "vt", l, n)
                for h in range(GH):
                    op = act.activation(head(v_beta[:, n, :], h), head(b, h), ACT.Copy, scale=colnh(BE, n, h))
                op.then_inc(*freed("vt", l, n, also=("vbeta", l, n)))
            for n in range(TT):
                b = bank(act, "x1", l, n)
                act.activation(x_inv[:, n, :], b[:, :], ACT.Copy).then_inc(*freed("x1", l, n, also=("x", l, 0, n)))
            gate_act(act, l)
            for s in range(1, 7):
                for n in range(TT):
                    if s >= 2:
                        act.wait_ge(*when("xt", l, s - 1, n))
                    b = bank(act, "y", l, s, n)
                    act.activation(yv[:, n, :], b[:, :], ACT.Copy).then_inc(*freed("y", l, s, n, also=("y_in", l, s, n)))
            act.wait_ge(*when("att_out", l, AH - 1))
            act.wait_ge(*when("short", l, 1))
            for c in range(4):
                split_act(act, tmp[:, c, :], c, ("out", l))
            for n in range(TT):
                if n:
                    out_rms_act(act, l, n - 1)
                b = bank(act, "vn", l, n)
                if n == 0:
                    act.wait_ge(*when("xt", l, 6, TT - 1))
                act.activation(yv[:, 2 + n % 2, :], b[:, :], ACT.Copy).then_inc(*freed("vn", l, n, also=("vn_in", l, n)))
                b = bank(act, "go", l, n)
                act.activation(tmp[:, 4 + n, :], b[:, :], ACT.Square).then_inc(*done("o_sq", l, n))
                act.activation(o_t[:, :, P * n:P * n + P], banked(b), ACT.Copy)\
                   .then_inc(*freed("go", l, n, also=("o", l, n)))
            out_rms_act(act, l, TT - 1)
            for h in range(GH):
                act.wait_ge(*when("gated", l, TT - 1))
                split_act(act, o_t[:, h, :], 4 + h, ("out", l))

        def out_rms_act(act, l, n):
            b = bank(act, "l2o", l, n)
            act.activation(cols(L2 + GH * n, GH), b[:, 0:GH], ACT.Sqrt, bias=C("eps"), scale=1.0 / GD)\
               .then_inc(*freed("l2o", l, n, also=("rms_o", l, n)))

        def NHv(at):
            return cols(at).rearrange("p (n h) -> p n h", h=GH)

        def gdn_first_dve(dve, l):
            b = bank(dve, "abt", l)
            dve.tensor_copy(cols(AB, 2 * NH), b[:, 0:2 * NH]).then_inc(*freed("abt", l, also=("ab_col", l)))
            dve.wait_ge(*when("ab_col", l))
            dt = par[:, pc[f"dt_bias{l}"][0]:pc[f"dt_bias{l}"][0] + GH]
            abv = cols(AB, 2 * NH).rearrange("p (n h) -> p n h", h=2 * GH)
            dve.tensor_tensor(NHv(Z), abv[:, :, 0:GH], dt[:, None, :].broadcast_to([P, TT, GH]), ALU.add)\
               .then_inc(*done("z", l))
            dve.wait_ge(*when("z", l))
            dve.scalar_tensor_tensor(out=cols(EX), in0=cols(Z), scalar=-1.0, in1=cols(Z), op0=ALU.mult, op1=ALU.max)\
               .then_inc(*done("abs_z", l))

        def gdn_rates_dve(dve, l):
            dve.wait_ge(*when("ln_z", l))
            dve.scalar_tensor_tensor(out=cols(GL), in0=cols(Z), scalar=0.0, in1=cols(EX), op0=ALU.max, op1=ALU.add)\
               .then_inc(*done("softplus", l))
            dve.tensor_scalar(cols(BE), cols(BE), 1.0, None, ALU.add).then_inc(*done("one_exp_b", l))
            dve.wait_ge(*when("softplus", l))
            dve.scalar_tensor_tensor(out=NHv(GL), in0=NHv(GL), scalar=-1.0,
                                     in1=cols(NA, GH)[:, None, :].broadcast_to([P, TT, GH]),
                                     op0=ALU.mult, op1=ALU.mult).then_inc(*done("g", l))
            dve.wait_ge(*when("one_exp_b", l))
            dve.reciprocal(cols(BE), cols(BE)).then_inc(*done("beta", l))

        def gdn_decay_dve(dve, l):
            b = bank(dve, "decay", l)
            dve.tensor_copy(cols(DC, 2 * NH), b[:, 0:2 * NH]).then_inc(*freed("decay", l, also=("decays", l)))
            dve.wait_ge(*when("decays", l))
            dve.tensor_tensor(cols(KD), cols(DC + NH), cols(DC), ALU.subtract).then_inc(*done("kd", l))

        def gdn_dve(dve, l):
            dve.wait_ge(*when("exp_d", l))
            dve.wait_ge(*when("beta", l))
            dve.scalar_tensor_tensor(out=cols(NB), in0=cols(NB), scalar=-1.0, in1=cols(BE), op0=ALU.mult,
                                     op1=ALU.mult).then_inc(*done("neg_beta_exp_d", l))
            dve.wait_ge(*when("rms_k", l))
            dve.reciprocal(cols(L2, 2 * NH), cols(L2, 2 * NH)).then_inc(*done("l2_inv", l))
            dve.wait_ge(*when("l2_inv", l))
            sources = (GL, L2 + NH, L2, BE)

            def diag(n, w):
                i = 4 * n + w
                if i >= 2:
                    dve.wait_ge(*when("bank_filled", "row", l, (i - 2) // 4, (i - 2) % 4))
                buf = spread if w % 2 == 0 else sqacc
                for h in range(GH):
                    op = dve.tensor_scalar(head(buf[:, :], h), C("upto") if w == 0 else ident,
                                           colnh(sources[w], n, h), None, ALU.mult)
                op.then_inc(*done("diag", l, n, w))

            def rows(n, w):
                b = bank(dve, "row", l, n, w)
                if w == 0:
                    dve.wait_ge(*when("dec", l, n))
                    for h in range(GH):
                        op = dve.scalar_tensor_tensor(out=head(rel_t[:, n, :], h), in0=head(b, h),
                                                      scalar=colnh(DC, n, h), in1=C("neg_future"),
                                                      op0=ALU.subtract, op1=ALU.add)
                    op.then_inc(*freed("row", l, n, w, also=("rel_in", l, n)))
                elif w < 3:
                    x = by_head(2 - w, n)
                    dve.tensor_tensor(x, x, banked(b), ALU.mult)\
                       .then_inc(*freed("row", l, n, w, also=("normed", l, n, 2 - w)))
                else:
                    dve.tensor_copy(at_mat[:, n, :], b[:, :]).then_inc(*freed("row", l, n, w, also=("beta_row", l, n)))

            steps = [(n, w) for n in range(TT) for w in range(4)]
            for i in range(len(steps) + 1):
                if i < len(steps):
                    diag(*steps[i])
                if i:
                    rows(*steps[i - 1])
            for n in range(TT):
                dve.wait_ge(*when("rel", l, n))
                dve.wait_ge(*when("beta_row", l, n))
                dve.tensor_tensor(at_mat[:, n, :], at_mat[:, n, :], rel_t[:, n, :], ALU.mult).then_inc(*done("beta_rel", l, n))
                dve.wait_ge(*when("beta_rel", l, n))
                b = bank(dve, "kk", l, n)
                dve.tensor_tensor(at_mat[:, n, :], at_mat[:, n, :], b[:, :], ALU.mult)\
                   .then_inc(*freed("kk", l, n, also=("a", l, n)))
                b = bank(dve, "kq", l, n)
                dve.tensor_tensor(attn_t[:, n, :], rel_t[:, n, :], b[:, :], ALU.mult)\
                   .then_inc(*freed("kq", l, n, also=("attn", l, n)))
                x = by_head(0, n)
                dve.wait_ge(*when("attn", l, n))
                dve.tensor_tensor(x, x, dec[:, n, :].rearrange("p (h n) -> p h n", h=GH), ALU.mult)\
                   .then_inc(*done("q_dec", l, n))
                dve.wait_ge(*when("a", l, n))
                xt3 = xt_inv[:, n, :].rearrange("p (h n) -> p h n", h=GH)
                dve.tensor_tensor(xt3, at_mat[:, n, :].rearrange("p (h n) -> p h n", h=GH),
                                  over_heads(C("level0")), ALU.mult).then_inc(*done("level0", l, n))
                dve.wait_ge(*when("level0", l, n))
                dve.tensor_tensor(xt3, over_heads(ident), xt3, ALU.subtract).then_inc(*done("xt", l, 0, n))
            for s in range(1, 7):
                for n in range(TT):
                    if s >= 2:
                        dve.wait_ge(*when("bank_filled", "y", l, s - 1, n))
                    else:
                        dve.wait_ge(*when("a", l, n))
                    dve.tensor_tensor(tmp[:, 4 + n, :].rearrange("p (h n) -> p h n", h=GH),
                                      at_mat[:, n, :].rearrange("p (h n) -> p h n", h=GH),
                                      over_heads(C(f"level{s}")), ALU.mult).then_inc(*done("level", l, s, n))
                for n in range(TT):
                    if s < 6:
                        b = bank(dve, "px", l, s, n)
                        dve.tensor_tensor(x_inv[:, n, :], x_inv[:, n, :], b[:, :], ALU.subtract)\
                           .then_inc(*freed("px", l, s, n, also=("x", l, s, n)))
                    b = bank(dve, "pxt", l, s, n)
                    dve.tensor_tensor(xt_inv[:, n, :], xt_inv[:, n, :], b[:, :], ALU.subtract)\
                       .then_inc(*freed("pxt", l, s, n, also=("xt", l, s, n)))
            for c in range(4):
                split_dve(dve, tmp[:, c, :], c, ("out", l))
            for n in range(TT):
                if n:
                    b = bank(dve, "ks", l, n)
                    for h in range(GH):
                        op = dve.scalar_tensor_tensor(out=head(yv[:, n % 2, :], h), in0=head(b, h),
                                                      scalar=colnh(NB, n, h), in1=head(v_beta[:, n, :], h),
                                                      op0=ALU.mult, op1=ALU.add)
                    op.then_inc(*freed("ks", l, n, also=("rhs", l, n)))
                    out_diag_dve(dve, l, n - 1)
                if n < TT - 1:
                    b = bank(dve, "su", l, n)
                    if n == 0:
                        dve.tensor_copy(state[:, 0, :], b[:, :]).then_inc(*freed("su", l, n, also=("state", l, n)))
                    else:
                        dve.wait_ge(*when("state", l, n - 1))
                        for h in range(GH):
                            op = dve.scalar_tensor_tensor(out=head(state[:, n % 2, :], h),
                                                          in0=head(state[:, (n - 1) % 2, :], h),
                                                          scalar=colnh(CD, n, h), in1=head(b, h),
                                                          op0=ALU.mult, op1=ALU.add)
                        op.then_inc(*freed("su", l, n, also=("state", l, n)))
                if n:
                    out_gated_dve(dve, l, n - 1)
            out_diag_dve(dve, l, TT - 1)
            out_gated_dve(dve, l, TT - 1)
            for h in range(GH):
                split_dve(dve, o_t[:, h, :], 4 + h, ("out", l))

        def out_diag_dve(dve, l, n):
            dve.wait_ge(*when("rms_o", l, n))
            dve.reciprocal(cols(L2 + GH * n, GH), cols(L2 + GH * n, GH)).then_inc(*done("o_inv", l, n))
            dve.wait_ge(*when("o_inv", l, n))
            if n >= 2:
                dve.wait_ge(*when("bank_filled", "o_row", l, n - 2))
            buf = spread if n % 2 == 0 else sqacc
            for h in range(GH):
                op = dve.tensor_scalar(head(buf[:, :], h), ident, colnh(L2, n, h), None, ALU.mult)
            op.then_inc(*done("o_diag", l, n))

        def out_gated_dve(dve, l, n):
            b = bank(dve, "o_row", l, n)
            x = o_t[:, :, P * n:P * n + P]
            dve.wait_ge(*when("o", l, n))
            dve.tensor_tensor(x, x, banked(b), ALU.mult).then_inc(*freed("o_row", l, n, also=("o_normed", l, n)))
            if n == 0:
                dve.wait_ge(*when("gate", l, GH - 1))
            dve.wait_ge(*when("o_normed", l, n))
            dve.scalar_tensor_tensor(out=x, in0=x, scalar=G(f"gdn_norm{l}", 0), in1=g_gate[:, :, P * n:P * n + P],
                                     op0=ALU.mult, op1=ALU.mult).then_inc(*done("gated", l, n))

        LAT, CTX = slice(0, S), slice(S, S + M)
        PARTS = (("lat", hT, LAT, S, 0), ("ctx", None, CTX, M, 1))
        EJ = even_jobs()
        OJ = odd_jobs()

        def stream(p):
            return hT if p == "lat" else cT

        def mod_gain_dve(dve, i):
            g = par[:, pc[f"norm_g{i}"][0]:pc[f"norm_g{i}"][0] + KC]
            if i:
                dve.wait_ge(*when("shifted_in", 0, "ctx", KC - 1))
            dve.wait_ge(*when("mod_out", i, 3 * KC - 1))
            for w in range(2):
                dve.scalar_tensor_tensor(out=mod_gain[:, w, :], in0=mod[:, i, KC:2 * KC, w], scalar=1.0, in1=g,
                                         op0=ALU.add, op1=ALU.mult).then_inc(*done("mod_gain", i, w))
            dve.wait_ge(*when("mod_gain", i, 1))

        def chunk_parts(ctx_first):
            if ctx_first:
                return [(e, q) for q in reversed(PARTS) for e in range(KC)]
            return [(e, q) for e in range(KC) for q in PARTS]

        def square_buffer(p, c):
            return sq[:, c % 2, :] if p == "lat" else sqacc[:, M * (c % 2):M * (c % 2) + M]

        def sums_act(act, key, order, sources):
            for c, (p, _, _, n, _) in order:
                act.wait_ge(*when(*sources(p, c)))
                if c >= 2:
                    act.wait_ge(*when("sq_summed", *key, p, c - 2))
                act.activation(square_buffer(p, c)[:, :n], stream(p)[:, c, :n], ACT.Square)\
                   .then_inc(*done("sq", *key, p, c))

        def sums_pe(pe, key, order):
            b = claim(pe, "ssq", *key)
            pe.matmul(b[:, 0:6], ident, C("zero").broadcast_to([P, 6]), start=True, stop=True)
            for i, (c, (p, _, sl, n, _)) in enumerate(order):
                pe.wait_ge(*when("sq", *key, p, c))
                for t in range(n // P):
                    at = sl.start // P + t
                    mm = pe.matmul(b[:, at:at + 1], square_buffer(p, c)[:, P * t:P * t + P], ones[:, 0:1],
                                   start=False, stop=True, skip_group_check=True)
                mm.then_inc(*(filled("ssq", *key) if i == len(order) - 1 else done("sq_summed", *key, p, c)))

        FINAL = [(c, PARTS[0]) for c in range(KC)]

        def sums_order(i):
            return chunk_parts(i == 0)

        def mod_norm_act(act, i, sources):
            key = ("m2", i)
            load_sqrt_act(act)
            sums_act(act, key, sums_order(i), sources)
            b = bank(act, "ssq", *key)
            act.activation(col[:, 0:6], b[:, 0:6], ACT.Sqrt, bias=C("eps"), scale=1.0 / D)\
               .then_inc(*freed("ssq", *key, also=("rms", *key)))
            for c in range(KC):
                for p, _, sl, n, w in PARTS:
                    act.wait_ge(*when("scaled", i, p, c))
                    act.activation(b_hi[:, c, sl], mod_tmp(i)[:, c % 2, sl], ACT.Identity, bias=mod[:, i, c, w:w + 1])\
                       .then_inc(*done("hi", i, p, c))

        def mod_tmp(i):
            if i == 0:
                return e_t
            return c_y[:, :, :].rearrange("p a b -> p (a b)")[:, :2 * (S + M)].rearrange("p (a b) -> p a b", a=2)

        def mod_norm_dve(dve, i):
            key = ("m2", i)
            dve.wait_ge(*when("rms", *key))
            dve.reciprocal(col[:, 8:14], col[:, 0:6]).then_inc(*done("rrms", *key))
            dve.wait_ge(*when("rrms", *key))
            spreads = {"lat": spread, "ctx": mod_sum[:, :, :].rearrange("p a b -> p (a b)")}
            for p, _, sl, n, _ in PARTS:
                for t in range(n // P):
                    at = 8 + sl.start // P + t
                    op = dve.tensor_scalar(spreads[p][:, P * t:P * t + P], ident, col[:, at:at + 1], None, ALU.mult)
                op.then_inc(*done("spread", *key, p))
            t = mod_tmp(i)
            rows = {p: bank(dve, "rstd", *key, p) for p, *_ in PARTS}
            for c in range(KC + 1):
                for p, _, sl, n, w in PARTS if c < KC else ():
                    if c >= 2:
                        dve.wait_ge(*when("shifted_in", i, p, c - 2))
                    dve.scalar_tensor_tensor(out=t[:, c % 2, sl], in0=stream(p)[:, c, :n],
                                             scalar=mod_gain[:, w, c:c + 1], in1=rows[p][:, :n],
                                             op0=ALU.mult, op1=ALU.mult)\
                       .then_inc(*(freed("rstd", *key, p, also=("scaled", i, p, c)) if c == KC - 1
                                   else done("scaled", i, p, c)))
                for p, _, sl, n, w in PARTS if c else ():
                    e = c - 1
                    dve.wait_ge(*when("hi", i, p, e))
                    dve.scalar_tensor_tensor(out=b_lo[:, e, sl], in0=t[:, e % 2, sl],
                                             scalar=mod[:, i, e, w:w + 1], in1=b_hi[:, e, sl].bitcast(f32),
                                             op0=ALU.add, op1=ALU.subtract).then_inc(*done("shifted_in", i, p, e))

        def mod_norm_pe(pe, i):
            key = ("m2", i)
            sums_pe(pe, key, sums_order(i))
            spreads = {"lat": spread, "ctx": mod_sum[:, :, :].rearrange("p a b -> p (a b)")}
            for p, _, _, n, _ in PARTS:
                pe.wait_ge(*when("spread", *key, p))
                b = claim(pe, "rstd", *key, p)
                pe.matmul(b[:, :n], ones, spreads[p][:, :n], start=True, stop=True).then_inc(*filled("rstd", *key, p))

        def both(name):
            return [(f"{name}/lat", b_hi, b_lo, S), (f"{name}/ctx", b_hi[:, :, S:], b_lo[:, :, S:], M)]

        def mod_ready(i):
            return lambda k: [("shifted_in", i, "lat", k), ("shifted_in", i, "ctx", k)]

        def e_place(name):
            if name in ("ak", "av", "bk", "bv"):
                return e_raw[:, ("ak", "bk", "av", "bv").index(name), :]
            return e_q[:, int(name[2]) + (CC if name[0] == "b" else 0), :]

        E_IN = [n for n, _, _ in EJ if n[1] in "kvq"]
        E_GATE = [n for n, _, _ in EJ if n[1] == "g"]
        NORMED = ["ak"] + [f"aq{c}" for c in range(CC)]

        FIRST = CC
        SWAPS = ["bk"] + NORMED + [f"bq{c}" for c in range(CC)]
        SWAPS_AFTER = {7: SWAPS[0:2], 8: SWAPS[2:3], 9: SWAPS[3:4], 10: SWAPS[4:5], 11: SWAPS[5:]}
        TURNS = [(j, name, g) for j, name in enumerate(("av", "bv")) for g in range(2)]

        def even_in_pe(pe):
            for i, name in enumerate(E_IN):
                product(pe, (0,), both(name), need=mod_ready(0) if i == 0 else None)
                if 0 <= i - FIRST - 1 < len(NORMED):
                    norm = NORMED[i - FIRST - 1]
                    for p, _, sl, n, _ in PARTS:
                        pe.wait_ge(*when("e_sq", norm, p))
                        b = claim(pe, "e_ssq", norm, p)
                        pe.matmul(b[:, :n], C("head_ones"), e_t[:, (i - FIRST - 1) % 2, sl], start=True, stop=True)\
                          .then_inc(*filled("e_ssq", norm, p))
                if 0 <= i - FIRST < len(TURNS):
                    _, values, g = TURNS[i - FIRST]
                    pe.wait_ge(*when("e_in", values, "ctx"))
                    b = claim(pe, "e_vt", values, g)
                    for m, t in enumerate(range(4 * g, min(4 * g + 4, 6))):
                        mm = pe.transpose(b[:, P * m:P * m + P], e_place(values)[:, P * t:P * t + P], ident)
                    mm.then_inc(*filled("e_vt", values, g))
                for swap in SWAPS_AFTER.get(i, ()):
                    pe.wait_ge(*(when("e_normed", swap, "lat") if swap in NORMED else when("e_in", swap, "lat")))
                    b = claim(pe, "e_swap", swap)
                    pe.matmul(b[:, :], C("rope2"), e_place(swap)[:, LAT], start=True, stop=True)\
                      .then_inc(*filled("e_swap", swap))

        def even_in_act(act):
            for i, name in enumerate(E_IN):
                scale = AD ** -0.5 if name[:2] == "bq" else 1.0
                for p, _, sl, n, _ in PARTS:
                    b = bank(act, f"{name}/{p}", 0)
                    act.activation(e_place(name)[:, sl], b[:, :n], ACT.Copy, scale=scale)\
                       .then_inc(*freed(f"{name}/{p}", 0, also=("e_in", name, p)))
                v = i - FIRST - 1
                if 0 <= v < len(NORMED):
                    norm = NORMED[v]
                    for p, _, sl, n, _ in PARTS:
                        b = bank(act, "e_ssq", norm, p)
                        act.activation(e_t[:, v % 2, sl], b[:, :n], ACT.Sqrt, bias=C("eps"), scale=1.0 / AD)\
                           .then_inc(*freed("e_ssq", norm, p, also=("e_rms", norm, p)))
                if 0 <= i - FIRST < len(TURNS):
                    j, values, g = TURNS[i - FIRST]
                    b = bank(act, "e_vt", values, g)
                    n = 4 if g == 0 else 2
                    act.activation(e_vt[:, 4 * g:4 * g + n, P * j:P * j + P],
                                   b[:, :P * n].rearrange("p (t n) -> p t n", n=P), ACT.Copy)\
                       .then_inc(*freed("e_vt", values, g, also=("e_vt_in", values, g)))
                v = i - FIRST
                if 0 <= v < len(NORMED):
                    norm = NORMED[v]
                    for p, _, sl, n, _ in PARTS:
                        act.wait_ge(*when("e_in", norm, p))
                        if v >= 2:
                            act.wait_ge(*when("e_normed", NORMED[v - 2], p))
                        act.activation(e_t[:, v % 2, sl], e_place(norm)[:, sl], ACT.Square)\
                           .then_inc(*done("e_sq", norm, p))
            for j, name in enumerate(("ak", "bk")):
                act.wait_ge(*when("e_roped", name))
                for g in range(2):
                    for half in range(2):
                        act.activation(e_kd[AD * half:AD * half + AD, 2 * j + g, :],
                                       e_place(name)[AD * g:AD * g + AD, :], ACT.Copy)\
                           .then_inc(*done("e_kd", j, g, half))

        def even_prep_dve(dve):
            dve.tensor_scalar(col[:, 16:17], G("q_gain", 0), AD ** -0.5, None, ALU.mult).then_inc(*done("q_gain8"))
            dve.wait_ge(*when("q_gain8"))
            for i in range(len(NORMED) + 1):
                if i < len(NORMED):
                    head_norm_dve(dve, i)
                if i == 2:
                    dve.wait_ge(*when("axial"))
                    rope_dve(dve, 0)
                    rope_dve(dve, 1)
                elif i > 2:
                    rope_dve(dve, i - 1)
            for i in range(len(NORMED), len(SWAPS)):
                rope_dve(dve, i)

        def head_norm_dve(dve, i):
            name = NORMED[i]
            for p, _, sl, n, _ in PARTS:
                dve.wait_ge(*when("e_rms", name, p))
                dve.reciprocal(e_t[:, i % 2, sl], e_t[:, i % 2, sl]).then_inc(*done("e_rrms", name, p))
                dve.wait_ge(*when("e_rrms", name, p))
                dve.scalar_tensor_tensor(out=e_place(name)[:, sl], in0=e_place(name)[:, sl],
                                         scalar=G("k_gain", 0) if name == "ak" else col[:, 16:17],
                                         in1=e_t[:, i % 2, sl], op0=ALU.mult, op1=ALU.mult)\
                   .then_inc(*done("e_normed", name, p))

        def rope_dve(dve, i):
            name = SWAPS[i]
            x = e_place(name)[:, LAT]
            t = e_gate_u[:, i % 2, LAT]
            if i >= 2:
                dve.wait_ge(*when("e_roped", SWAPS[i - 2]))
            b = bank(dve, "e_swap", name)
            dve.tensor_tensor(t, b[:, :], rope_t[:, 1, :], ALU.mult)\
               .then_inc(*freed("e_swap", name, also=("e_sin", name)))
            dve.tensor_tensor(x, x, rope_t[:, 0, :], ALU.mult).then_inc(*done("e_cos", name))
            dve.wait_ge(*when("e_sin", name))
            dve.wait_ge(*when("e_cos", name))
            dve.tensor_tensor(x, x, t, ALU.add).then_inc(*done("e_roped", name))

        def even_units():
            units = []
            for x in range(2):
                for h in range(QH):
                    lo, g = AD * (h % 2), h // 4
                    q = e_q[lo:lo + AD, CC * x + h // 2, :]
                    k = e_kd[lo:lo + AD, 2 * x + g, :]
                    sink = G("sink", h) if x else None
                    for t in range(TT):
                        qt = q[:, P * t:P * t + P]
                        a, z = (0, TT) if x == 0 else (max(0, t - 1), min(TT, t + 2))
                        mask = bmask[:, P * (a - t + 1):P * (z - t + 1)] if x else None
                        units.append({"head": QH * x + h, "group": (x, h, "lat"), "q0": P * t, "sink": sink,
                                      "parts": [(P * a, P * (z - a), [(qt, k[:, P * a:P * z])], mask),
                                                (S, M, [(qt, k[:, CTX])], None)]})
                    for t in range(MT):
                        qt = q[:, S + P * t:S + P * t + P]
                        units.append({"head": QH * x + h, "group": (x, h, "ctx"), "q0": S + P * t, "sink": sink,
                                      "parts": [(S, M, [(qt, k[:, CTX])], None)]})
            return units

        def even_values(kt, h):
            x, g = h // QH, (h % QH) // 4
            return [e_vt[:, kt, P * x + AD * g:P * x + AD * g + AD]]

        def even_take(units):
            def take(act, u):
                h = units[u]["head"]
                lo = AD * (h % 2)
                sl, n = (LAT, S) if units[u]["group"][2] == "lat" else (CTX, M)
                b = bank(act, "o", "even", u, 0)
                act.activation(e_q[lo:lo + AD, h // 2, sl], b[0:AD, :n], ACT.Copy)\
                   .then_inc(*freed("o", "even", u, 0, also=("e_out", h, units[u]["group"][2])))
            return take

        GATE_STEPS = KC

        def even_gate(c):
            if c < 2:
                return e_t[:, c, :]
            if c < 4:
                return e_gate_a[:, c - 2, :]
            if c < 7:
                return e_gate_u[:, c - 4, :]
            return rope_t[:, :, :].rearrange("p a b -> p (a b)")[:, :S + M]

        def even_gate_blocks(u):
            return int(u % 3 != 2)

        def even_gate_steps(pe):
            for name in E_GATE:
                yield from product_steps(pe, (0,), both(name))

        def even_gate_take_act(act, u):
            c, rest = divmod(sum(even_gate_blocks(v) for v in range(u + 1)), GATE_STEPS)
            c -= 1
            if rest == 0 and 0 <= c < KC and even_gate_blocks(u):
                for p, _, sl, n, _ in PARTS:
                    b = bank(act, f"{E_GATE[c]}/{p}", 0)
                    act.activation(even_gate(c)[:, sl], b[:, :n], ACT.Copy)\
                       .then_inc(*freed(f"{E_GATE[c]}/{p}", 0, also=("e_gate_raw", c, p)))

        def even_gate_act(act):
            for c in range(KC + 2):
                if c < KC:
                    g = even_gate(c)
                    act.wait_ge(*when("e_gate_raw", c, "lat"))
                    act.wait_ge(*when("e_gate_raw", c, "ctx"))
                    act.activation(g, g, ACT.Silu).then_inc(*done("e_gate", c))
                if c >= 2:
                    act.wait_ge(*when("e_gated", c - 2))
                    split_act(act, e_q[:, c - 2, :], c - 2, ("e_mix",), n=S + M, hi=b_hi)

        def even_gate_dve(dve):
            for c in range(KC):
                dve.wait_ge(*when("e_gate", c))
                for p in ("lat", "ctx"):
                    dve.wait_ge(*when("e_out", 2 * c + 1, p))
                dve.tensor_tensor(e_q[:, c, :], e_q[:, c, :], even_gate(c), ALU.mult).then_inc(*done("e_gated", c))
            for c in range(KC):
                split_dve(dve, e_q[:, c, :], c, ("e_mix",), n=S + M, hi=b_hi, lo=b_lo)

        def even_out_pe(pe):
            for c in range(KC):
                product(pe, (0, c), both("e_y"), need=inputs_ready(("e_mix",)) if c == 0 else None)

        def even_out_dve(dve):
            for c in range(KC):
                for p, _, sl, n, w in PARTS:
                    b = bank(dve, f"e_y/{p}", 0, c)
                    x = stream(p)[:, c, :n]
                    dve.scalar_tensor_tensor(out=x, in0=b[:, :n], scalar=mod[:, 0, 2 * KC + c, w:w + 1], in1=x,
                                             op0=ALU.mult, op1=ALU.add)\
                       .then_inc(*freed(f"e_y/{p}", 0, c, also=("h2", p, c)))

        def odd_in_pe(pe):
            for i, (name, _, _, with_ctx) in enumerate(OJ):
                if name[:2] not in LATE:
                    product(pe, (1,), both(name) if with_ctx else both(name)[:1], need=mod_ready(1) if i == 0 else None)

        LATE = ("cg", "dg")
        ODD_GATE = [f"{kind}{c}" for kind in LATE for c in range(CC)]

        def odd_gate_steps(pe):
            for name in ODD_GATE:
                yield from product_steps(pe, (1,), both(name)[:1])

        def odd_gate(i):
            return (c_g if i < CC else d_g)[:, i % CC, :]

        def odd_gate_take_act(act, u):
            i, rest = divmod(u + 1, KC // 2)
            if rest == 0 and 1 <= i <= 2 * CC:
                name = ODD_GATE[i - 1]
                b = bank(act, f"{name}/lat", 1)
                if name[0] == "c":
                    act.wait_ge(*when("c_in", i - 1))
                act.activation(odd_gate(i - 1), b[:, :], ACT.Copy)\
                   .then_inc(*freed(f"{name}/lat", 1, also=("odd_gate_raw", i - 1)))

        def odd_in_act(act):
            for name, _, _, with_ctx in OJ:
                c, kind = int(name[2]), name[:2]
                if kind in LATE:
                    continue
                b = bank(act, f"{name}/lat", 1)
                if kind == "cv":
                    act.activation(c_u[:, c, CT // 2:CT // 2 + S], b[:, :], ACT.Copy)\
                       .then_inc(*freed(f"{name}/lat", 1, also=("c_val", c)))
                elif kind == "cl":
                    act.activation(c_g[:, c, :], b[:, :], ACT.Sigmoid)\
                       .then_inc(*freed(f"{name}/lat", 1, also=("c_glu", c)))
                elif kind == "dq":
                    act.activation(d_q[:, c, :], b[:, :], ACT.Copy, scale=AD ** -0.5)\
                       .then_inc(*freed(f"{name}/lat", 1, also=("dq", c)))
                else:
                    to = d_k if kind == "dk" else d_v
                    act.activation(to[:, c, LAT], b[:, :], ACT.Copy).then_inc(*freed(f"{name}/lat", 1, also=(kind, c, "lat")))
                    b = bank(act, f"{name}/ctx", 1)
                    act.activation(to[:, c, CTX], b[:, :M], ACT.Copy).then_inc(*freed(f"{name}/ctx", 1, also=(kind, c, "ctx")))

        def conformer_dve(dve):
            side = CT // 2
            for c in range(CC):
                for w, at in ((0, 0), (1, side + S)):
                    dve.memset(c_u[:, c, at:at + side], 0.0).then_inc(*done("c_zero", c, w))
            dve.wait_ge(*when("c_zero", CC - 1, 1))
            for c in range(CC):
                dve.wait_ge(*when("c_val", c))
                dve.wait_ge(*when("c_glu", c))
                u = c_u[:, c, side:side + S]
                dve.tensor_tensor(u, u, c_g[:, c, :], ALU.mult).then_inc(*done("c_in", c))
                dve.wait_ge(*when("c_in", c))
                for j in range(CT):
                    if j == 0:
                        op = dve.tensor_scalar(c_y[:, c, :], c_u[:, c, 0:S], G("dw_w", CT * c), G("dw_b", c),
                                               ALU.mult, ALU.add)
                    else:
                        dve.wait_ge(*when("c_tap", c, j - 1))
                        op = dve.scalar_tensor_tensor(out=c_y[:, c, :], in0=c_u[:, c, j:j + S],
                                                      scalar=G("dw_w", CT * c + j), in1=c_y[:, c, :],
                                                      op0=ALU.mult, op1=ALU.add)
                    op.then_inc(*done("c_tap", c, j))
            b = bank(dve, "c_sum")
            dve.wait_ge(*when("c_tap", CC - 1, CT - 1))
            dve.tensor_scalar(sqacc[:, :], b[:, :], 1.0 / (CC * P), None, ALU.mult)\
               .then_inc(*freed("c_sum", also=("c_mean",)))
            dve.wait_ge(*when("c_mean"))
            for c in range(CC):
                dve.tensor_tensor(c_y[:, c, :], c_y[:, c, :], sqacc[:, :], ALU.subtract).then_inc(*done("c_centred", c))
            dve.wait_ge(*when("c_std"))
            dve.reciprocal(spread[:, :], spread[:, :]).then_inc(*done("c_rstd"))
            dve.wait_ge(*when("c_rstd"))
            for c in range(CC):
                dve.wait_ge(*when("c_centred", c))
                dve.scalar_tensor_tensor(out=c_y[:, c, :], in0=c_y[:, c, :], scalar=G("ln_g", c), in1=spread[:, :],
                                         op0=ALU.mult, op1=ALU.mult).then_inc(*done("c_scaled", c))

        def conformer_pe(pe):
            b = claim(pe, "c_sum")
            for c in range(CC):
                pe.wait_ge(*when("c_tap", c, CT - 1))
                mm = pe.matmul(b[:, :], ones, c_y[:, c, :], start=c == 0, stop=c == CC - 1)
            mm.then_inc(*filled("c_sum"))
            b = claim(pe, "c_var")
            for c in range(CC):
                pe.wait_ge(*when("c_sq", c))
                mm = pe.matmul(b[:, :], ones, sq[:, c % 2, :], start=c == 0, stop=c == CC - 1)
                mm.then_inc(*(filled("c_var") if c == CC - 1 else done("c_sq_used", c)))

        def conformer_act(act):
            for c in range(CC):
                act.wait_ge(*when("c_centred", c))
                if c >= 2:
                    act.wait_ge(*when("c_sq_used", c - 2))
                act.activation(sq[:, c % 2, :], c_y[:, c, :], ACT.Square).then_inc(*done("c_sq", c))
            b = bank(act, "c_var")
            act.activation(spread[:, :], b[:, :], ACT.Sqrt, bias=C("eps"), scale=1.0 / (CC * P))\
               .then_inc(*freed("c_var", also=("c_std",)))
            for c in range(CC):
                act.wait_ge(*when("c_scaled", c))
                act.activation(c_y[:, c, :], c_y[:, c, :], ACT.Silu, bias=G("ln_b", c)).then_inc(*done("c_silu", c))

        def odd_turn_pe(pe):
            for kt in range(6):
                pe.wait_ge(*when("dv", CC - 1, "ctx"))
                b = claim(pe, "d_vt", kt)
                for c in range(CC):
                    mm = pe.transpose(b[:, P * c:P * c + P], d_v[:, c, P * kt:P * kt + P], ident)
                mm.then_inc(*filled("d_vt", kt))

        def odd_turn_act(act):
            for kt in range(6):
                b = bank(act, "d_vt", kt)
                act.activation(d_vt[:, kt, :], b[:, :], ACT.Copy).then_inc(*freed("d_vt", kt, also=("d_vt_in", kt)))

        ROWS15, WIDE = 2 * NROW - 1, 127

        def load_bias(act, h):
            rows = dram["rpb_rows"]
            if h == 0:
                act.wait_ge(*when("c_silu", CC - 1))
            for half in range(2):
                src = bass.AP(rows.tensor, (h * ROWS15 + 1 - half) * GW * WIDE + GW - 1,
                              [[WIDE - 1, GW], [GW * WIDE, ROWS15 - 1], [1, GW]])
                dst = d_bias[GW * half:GW * half + GW, h % 2, GW:].rearrange("p (r k) -> p r k", k=GW)
                act.dma_start(dst, src).then_inc(*loaded(f"bias_in{h % 2}", h, half))

        def odd_units():
            units = []
            for h in range(QH):
                lo, c = AD * (h % 2), h // 2
                for t in range(TT):
                    q = d_q[lo:lo + AD, c, P * t:P * t + P]
                    at = GW * (NROW - 1 - 2 * t)
                    units.append({"head": h, "group": h, "q0": P * t,
                                  "parts": [(0, S, [(q, d_k[lo:lo + AD, c, LAT])], d_bias[:, h % 2, at:at + S]),
                                            (S, M, [(q, d_k[lo:lo + AD, c, CTX])], None)]})
            return units

        def bias_dve(dve, h):
            dve.wait_ge(*when(f"bias_in{h % 2}", h, 1))
            if h == 0:
                dve.wait_ge(*when("col_mask"))
            x = d_bias[:, h % 2, GW:].rearrange("p (r k) -> p r k", k=GW)
            dve.tensor_tensor(x, x, col_mask[:, None, :].broadcast_to([P, ROWS15 - 1, GW]), ALU.add)\
               .then_inc(*done("bias", h))
            dve.wait_ge(*when("bias", h))

        def odd_take(act, u):
            h = u // TT
            lo = AD * (h % 2)
            b = bank(act, "o", "odd", u, 0)
            act.activation(d_q[lo:lo + AD, h // 2, :], b[0:AD, :], ACT.Copy)\
               .then_inc(*freed("o", "odd", u, 0, also=("d_out", h)))
            if h + 2 < QH:
                act.wait_ge(*when("s_in", "odd", u, 0))
                load_bias(act, h + 2)

        def odd_out_act(act):
            for i in range(KC + 2):
                if i < KC:
                    act.wait_ge(*when("odd_gate_raw", i))
                    act.activation(odd_gate(i), odd_gate(i), ACT.Silu).then_inc(*done("odd_gate", i))
                if i >= 2:
                    c = i - 2
                    act.wait_ge(*when("odd_gated", c))
                    split_act(act, (c_y if c < CC else d_q)[:, c % CC, :], c, ("d_mix",), hi=b_hi)

        def odd_out_dve(dve):
            for c in range(KC):
                dve.wait_ge(*(when("c_silu", c) if c < CC else when("d_out", 2 * (c - CC) + 1)))
                dve.wait_ge(*when("odd_gate", c))
                x = (c_y if c < CC else d_q)[:, c % CC, :]
                dve.tensor_tensor(x, x, odd_gate(c), ALU.mult).then_inc(*done("odd_gated", c))
            for c in range(KC):
                split_dve(dve, (c_y if c < CC else d_q)[:, c % CC, :], c, ("d_mix",), hi=b_hi, lo=b_lo)

        def second_pe(pe):
            mod_norm_pe(pe, 0)
            even_in_pe(pe)
            attention_pe(pe, ("even",), even_units(), e_s, e_pt, even_values,
                         need=[("e_roped", SWAPS[-1]), ("e_kd", 1, 1, 1), ("e_vt_in", "bv", 1)],
                         fill=even_gate_steps(pe), blocks=even_gate_blocks)
            even_out_pe(pe)
            mod_norm_pe(pe, 1)
            odd_in_pe(pe)
            conformer_pe(pe)
            odd_turn_pe(pe)
            attention_pe(pe, ("odd",), odd_units(), d_s, d_pt,
                         lambda kt, h: [d_vt[:, kt, AD * h:AD * h + AD]],
                         need=[("d_vt_in", 5), ("dq", CC - 1), ("dk", CC - 1, "ctx")],
                         fill=odd_gate_steps(pe), blocks=lambda u: 2)
            for c in range(KC):
                product(pe, (1, c), [("d_y", b_hi, b_lo, S)], need=inputs_ready(("d_mix",)) if c == 0 else None)
            sums_pe(pe, ("final",), FINAL)
            rstd_pe(pe, ("final",), S)

        def second_act(act):
            act.wait_ge(*when("bank_filled", "y", "f_post", DEPTH - 1, KC - 1))
            act.dma_start(cT[:, :, :], dram["ctxT"]).then_inc(*loaded("c_in2"))
            act.dma_start(rope_t[:, :, :], dram["axial"]).then_inc(*loaded("axial"))
            act.dma_start(bmask[:, :], dram["band_mask"]).then_inc(*loaded("bmask"))
            mod_norm_act(act, 0, lambda p, c: ("h", "f_post", DEPTH - 1, c) if p == "lat" else ("c_in2",))
            even_in_act(act)
            attention_act(act, ("even",), even_units(), e_s, e_pt, even_take(even_units()),
                          between=lambda u: even_gate_take_act(act, u))
            even_gate_act(act)
            mod_norm_act(act, 1, lambda p, c: ("h2", p, c))
            odd_in_act(act)
            conformer_act(act)
            odd_turn_act(act)
            load_bias(act, 0)
            load_bias(act, 1)
            act.dma_start(col_mask[:, :], dram["column_mask"]).then_inc(*loaded("col_mask"))
            attention_act(act, ("odd",), odd_units(), d_s, d_pt, odd_take,
                          between=lambda u: odd_gate_take_act(act, u))
            odd_out_act(act)
            load_sqrt_act(act)
            sums_act(act, ("final",), FINAL, lambda p, c: ("h3", c))
            rms_act(act, ("final",), S)
            for c in range(KC):
                act.wait_ge(*when("out_ready", c))
                act.dma_start(out[:, c, :], hT[:, c, :]).then_inc(*loaded("out", c))
            act.wait_ge(*when("out", KC - 1))

        def second_dve(dve):
            mod_gain_dve(dve, 0)
            mod_norm_dve(dve, 0)
            even_prep_dve(dve)
            dve.wait_ge(*when("bmask"))
            attention_dve(dve, ("even",), even_units(), e_s)
            even_gate_dve(dve)
            even_out_dve(dve)
            mod_gain_dve(dve, 1)
            mod_norm_dve(dve, 1)
            conformer_dve(dve)
            attention_dve(dve, ("odd",), odd_units(), d_s,
                          before=lambda u: bias_dve(dve, u // TT) if u % TT == 0 else None)
            odd_out_dve(dve)
            for c in range(KC):
                b = bank(dve, "d_y", 1, c)
                dve.scalar_tensor_tensor(out=hT[:, c, :], in0=b[:, :], scalar=mod[:, 1, 2 * KC + c, 0:1],
                                         in1=hT[:, c, :], op0=ALU.mult, op1=ALU.add)\
                   .then_inc(*freed("d_y", 1, c, also=("h3", c)))
            spread_dve(dve, ("final",), S)
            b = bank(dve, "rstd", "final")
            for c in range(KC):
                dve.scalar_tensor_tensor(out=hT[:, c, :], in0=hT[:, c, :], scalar=G("final_g", c), in1=b[:, :],
                                         op0=ALU.mult, op1=ALU.mult)\
                   .then_inc(*(freed("rstd", "final", also=("out_ready", c)) if c == KC - 1
                               else done("out_ready", c)))

        def x_units(l):
            units = []
            for h in range(XH):
                for t in range(TT):
                    mms = [(xq[:, 2 * h + j, P * t:P * t + P], xk[:, 2 * h + j, :]) for j in range(2)]
                    units.append({"head": h, "group": h, "q0": P * t, "parts": [(0, M, mms, None)]})
            return units

        def memory_product_pe(pe, l):
            for c in range(2 * KC):
                product(pe, (l, c), [("kv", m_hi, m_lo, M)], need=inputs_ready(("mem", l)) if c == 0 else None)
                if c == 0:
                    ssq_pe(pe, ("mix_post", l), S)
                if c == 2:
                    rstd_pe(pe, ("mix_post", l), S)
            for g in range(4):
                pe.wait_ge(*when("kv_in", l, 2 * KC - 1))
                b = claim(pe, "xvt", l, g)
                for j in range(4):
                    c = 4 * (g % 2) + j
                    mm = pe.transpose(b[:, P * j:P * j + P], xv[:, c, P * (g // 2):P * (g // 2) + P], ident)
                mm.then_inc(*filled("xvt", l, g))

        def memory_act(act, l):
            act.wait_ge(*when("vn_in", l, TT - 1))
            act.wait_ge(*when("bank_filled", "go", l, TT - 1))
            act.dma_start(m_in[:, :, :], dram["memT"]).then_inc(*loaded("m_in", l))

        def memory_norm_act(act, l):
            pre_norm_act(act, ("mem", l), f"mem{l}", m_in, m_hi, M, lambda c: ("m_in", l))
            rstd_act(act, ("mem", l), M)

        def memory_product_dve(dve, l):
            dve.wait_ge(*when("rstd_in", "mem", l))
            key = ("mix_post", l)
            sum_squares_dve(dve, key, S)
            for c in range(2 * KC):
                if c == 1:
                    spread_dve(dve, key, S)
                if c == 3:
                    post_apply_dve(dve, key, f"mix_post{l}", y_x)
                if c >= KC:
                    low_dve(dve, ("x", l), f"x_pre{l}", hT, a_hi, a_lo, S, c - KC)
                b = bank(dve, "kv", l, c)
                dve.tensor_tensor((xk if c < KC else xv)[:, c % KC, :], b[:, :M], rstd[:, :M], ALU.mult)\
                   .then_inc(*freed("kv", l, c, also=("kv_in", l, c)))
            sum_squares_dve(dve, ("x", l), S)
            spread_dve(dve, ("x", l), S)

        def memory_product_act(act, l):
            first = first_tile("w_xkv", l)
            key = ("mix_post", l)
            post_norm_act(act, key, y_x, rms=False,
                          between=lambda c: round_tile_act(act, first) if c == KC - 1 else None)
            for c in range(2 * KC):
                if c:
                    round_tile_act(act, first + c)
                if c == 1:
                    rms_act(act, key, S)
                if c >= KC:
                    high_act(act, ("x", l), f"x_pre{l}", hT, a_hi, S, lambda c: ("h", "mix_post", l, c), c - KC)
            squares_act(act, ("x", l), lambda c: hT[:, c, :], S)
            memory_turn_act(act, l)
            rms_act(act, ("x", l), S)
            rstd_act(act, ("x", l), S)

        def memory_turn_act(act, l):
            for g in range(4):
                b = bank(act, "xvt", l, g)
                act.activation(xvt[:, g // 2, 4 * P * (g % 2):4 * P * (g % 2) + 4 * P], b[:, :], ACT.Copy)\
                   .then_inc(*freed("xvt", l, g, also=("xvt_in", l, g)))

        def x_product_pe(pe, l):
            for c in range(KC):
                product(pe, (l, c), [("xq", a_hi, a_lo, S)], need=inputs_ready(("x", l)) if c == 0 else None)
                if c == 2:
                    ssq_pe(pe, ("x", l), S)
                if c == 4:
                    rstd_pe(pe, ("x", l), S)

        def x_product_dve(dve, l):
            dve.wait_ge(*when("rstd_in", "x", l))
            for c in range(KC):
                b = bank(dve, "xq", l, c)
                dve.scalar_tensor_tensor(out=xq[:, c, :], in0=b[:, :], scalar=XD ** -0.5, in1=rstd[:, :],
                                         op0=ALU.mult, op1=ALU.mult).then_inc(*freed("xq", l, c, also=("xq_in", l, c)))

        def x_take_act(l):
            def take(act, u):
                h = u // TT
                for o in range(2):
                    c = 2 * h + o
                    b = bank(act, "o", "x", l, u, o)
                    act.activation(tmp[:, c, :], b[:, :], ACT.Copy).then_inc(*freed("o", "x", l, u, o, also=("x_out", l, c)))
                    act.wait_ge(*when("x_out", l, c))
                    split_act(act, tmp[:, c, :], c, ("xo", l))
            return take

        def ffn_pe(pe, l):
            for j in range(FC):
                product(pe, (l, j), [("gate_p", a_hi, a_lo, S)], need=inputs_ready(("f", l)) if j == 0 else None)
                product(pe, (l, j), [("up_p", a_hi, a_lo, S)])
                if j == 0:
                    ssq_pe(pe, ("f", l), S)
                if j == 1:
                    rstd_pe(pe, ("f", l), S)
                modulation_pe(pe, l, j - 2)
            for c in range(KC):
                product(pe, ("f_post", l, c), [("y", f_hi, f_lo, S)], kc=FC,
                        need=inputs_ready(("hid", l)) if c == 0 else None)
                if c == 0:
                    modulation_pe(pe, l, FC - 2)

        def ffn_dve(dve, l):
            dve.wait_ge(*when("rstd_in", "f", l))

            def gate_up(j):
                r = 4 * (j % 2)
                if j >= 2:
                    dve.wait_ge(*when("lo", "hid", l, j - 2))
                b = bank(dve, "gate_p", l, j)
                dve.tensor_tensor(tmp[:, r, :], b[:, :], rstd[:, :], ALU.mult)\
                   .then_inc(*freed("gate_p", l, j, also=("gate_s", l, j)))
                b = bank(dve, "up_p", l, j)
                dve.tensor_tensor(tmp[:, r + 2, :], b[:, :], rstd[:, :], ALU.mult)\
                   .then_inc(*freed("up_p", l, j, also=("up_s", l, j)))

            def hidden(j):
                r = 4 * (j % 2)
                dve.wait_ge(*when("f_silu", l, j))
                dve.wait_ge(*when("up_s", l, j))
                dve.tensor_tensor(tmp[:, r + 3, :], tmp[:, r + 1, :], tmp[:, r + 2, :], ALU.mult)\
                   .then_inc(*done("hidden", l, j))
                split_dve(dve, tmp[:, r + 3, :], j, ("hid", l), hi=f_hi, lo=f_lo)

            for j in range(FC):
                gate_up(j)
                hidden(j)
                modulation_dve(dve, l, j - 1)

        def ffn_act(act, l):
            def silu(j):
                r = 4 * (j % 2)
                act.wait_ge(*when("gate_s", l, j))
                act.activation(tmp[:, r + 1, :], tmp[:, r, :], ACT.Silu).then_inc(*done("f_silu", l, j))

            def split(j):
                act.wait_ge(*when("hidden", l, j))
                split_act(act, tmp[:, 4 * (j % 2) + 3, :], j, ("hid", l), hi=f_hi)

            for j in range(FC):
                silu(j)
                split(j)
                modulation_act(act, l, j)

        def modulation_chunks(j):
            c = len(EARLY) + j - 1
            return [c] if j >= 1 and c < 3 * KC else []

        def modulation_dve(dve, l, j):
            for c in modulation_chunks(j):
                modulation_sum_dve(dve, l, c)

        def modulation_sum_dve(dve, l, c):
            dve.wait_ge(*when(f"mod_in{c % 2}", l, c))
            if c:
                dve.wait_ge(*when("bank_filled", "mod", l, c - 1))
            for k in range(KC):
                w = mod_raw[:, c % 2, P * k:P * k + P]
                if k:
                    dve.wait_ge(*when("mod_part", l, c, k - 1, 1))
                for i in range(2):
                    if k == 0:
                        op = dve.tensor_scalar(mod_sum[:, i, :], w, cond[:, k, i:i + 1], None, ALU.mult)
                    else:
                        op = dve.scalar_tensor_tensor(out=mod_sum[:, i, :], in0=w, scalar=cond[:, k, i:i + 1],
                                                      in1=mod_sum[:, i, :], op0=ALU.mult, op1=ALU.add)
                    op.then_inc(*done("mod_part", l, c, k, i))

        def modulation_pe(pe, l, j):
            for c in modulation_chunks(j):
                modulation_sum_pe(pe, l, c)

        def modulation_sum_pe(pe, l, c):
            pe.wait_ge(*when("mod_part", l, c, KC - 1, 1))
            b = claim(pe, "mod", l, c)
            for i in range(2):
                mm = pe.matmul(b[:, i:i + 1], mod_sum[:, i, :], ones[:, 0:1], start=True, stop=True)
            mm.then_inc(*filled("mod", l, c))

        def modulation_take_act(act, l, j):
            for c in modulation_chunks(j):
                modulation_bias_act(act, l, c)

        def modulation_bias_act(act, l, c):
            b = bank(act, "mod", l, c)
            act.activation(mod[:, l, c, :], b[:, 0:2], ACT.Identity, bias=G(f"mod_b{l}", c))\
               .then_inc(*freed("mod", l, c, also=("mod_out", l, c)))

        def modulation_load_act(act, l, c):
            if c >= 2:
                act.wait_ge(*when("mod_part", l, c - 2, KC - 1, 1))
            act.dma_start(mod_raw[:, c % 2, :], dram["mod_tiles"][l, c]).then_inc(*loaded(f"mod_in{c % 2}", l, c))

        def modulation_act(act, l, j):
            if j == 1:
                act.wait_ge(*when("rstd_in", "f", l))
            for c in modulation_chunks(j):
                modulation_load_act(act, l, c)
            modulation_take_act(act, l, j - 2)
            if j == FC - 1:
                modulation_take_act(act, l, FC - 2)

        def rope_table_dve(dve):
            two_pi = 2 * np.pi
            part1 = 6.28125
            part2 = two_pi - part1
            magic = 1.5 * 2.0 ** 23
            ang, n, r = acc[:, 0, :], acc[:, 1, :], pad[:, 0, 0:S]

            def step(op, i):
                op.then_inc(*done("rope_step", i))
                dve.wait_ge(*when("rope_step", i))

            dve.wait_ge(*when("pos"))
            dve.wait_ge(*when("params", 1))
            step(dve.tensor_copy(r, pos[:, :]), "f")
            step(dve.tensor_scalar(ang, r, C("inv_freq"), None, ALU.mult), "ang")
            for w, quarter in ((0, 0.25), (1, 0.0)):
                step(dve.tensor_scalar(n, ang, 1 / two_pi, quarter, ALU.mult, ALU.add), (w, 0))
                step(dve.tensor_scalar(n, n, magic, None, ALU.add), (w, 1))
                step(dve.tensor_scalar(n, n, magic, None, ALU.subtract), (w, 2))
                step(dve.scalar_tensor_tensor(out=r, in0=n, scalar=-part1, in1=ang, op0=ALU.mult, op1=ALU.add), (w, 3))
                step(dve.scalar_tensor_tensor(out=r, in0=n, scalar=-part2, in1=r, op0=ALU.mult, op1=ALU.add), (w, 4))
                step(dve.tensor_scalar(r, r, two_pi * quarter, 3.1415925, ALU.add, ALU.min), (w, 5))
                dve.tensor_scalar(rope_t[:, w, :], r, -3.1415925, None, ALU.max).then_inc(*done("angle", w))
                dve.wait_ge(*when("angle", w))

        def rope_table_act(act):
            for w in range(2):
                act.wait_ge(*when("angle", w))
                act.activation(rope_t[:, w, :], rope_t[:, w, :], ACT.Sin).then_inc(*done("rope_table", w))
            act.wait_ge(*when("rope_table", 1))

        def h_before(l):
            return (lambda c: (f"h_in{c // 2}",)) if l == 0 else (lambda c: ("h", "f_post", l - 1, c))

        block = ctx.enter_context(nc.Block())
        layers = range(DEPTH)

        @block.tensor
        def _(pe):
            pe.wait_ge(*when("params", 1))
            pe.wait_ge(*when("cond"))
            for l in layers:
                in_product_pe(pe, l)
                gdn_first_pe(pe, l)
                att_prep_pe(pe, l)
                gdn_decay_pe(pe, l)
                attention_pe(pe, ("att", l), att_units(l), s_buf, p_t,
                             lambda kt, h: [a_vt[:, kt, AD * h:AD * h + AD]],
                             need=[("roped", l, i) for i in range(4)] + [("avt_in", l, 1)],
                             fill=gate_steps(pe, l), blocks=lambda u: 2)
                gdn_pe(pe, l)
                for c in range(KC):
                    product(pe, ("mix_post", l, c), [("y", a_hi, a_lo, S)],
                            need=inputs_ready(("out", l)) if c == 0 else None)
                    if c == 3:
                        ssq_pe(pe, ("mem", l), M)
                    if c == 5:
                        rstd_pe(pe, ("mem", l), M)
                memory_product_pe(pe, l)
                x_product_pe(pe, l)
                attention_pe(pe, ("x", l), x_units(l), x_s, x_pt,
                             lambda kt, h: [xvt[:, kt, XD * h + P * o:XD * h + P * o + P] for o in range(2)],
                             need=[("xq_in", l, KC - 1), ("xvt_in", l, 3)])
                for c in range(KC):
                    product(pe, ("x_post", l, c), [("y", a_hi, a_lo, S)],
                            need=inputs_ready(("xo", l)) if c == 0 else None)
                ssq_pe(pe, ("x_post", l), S)
                rstd_pe(pe, ("x_post", l), S)
                ffn_pe(pe, l)
                ssq_pe(pe, ("f_post", l), S)
                rstd_pe(pe, ("f_post", l), S)
            second_pe(pe)

        @block.sync
        def _(sp):
            sp.dma_start(con[:, :], dram["consts"]).then_inc(*loaded("params", 0))
            sp.dma_start(par[:, :], dram["params"]).then_inc(*loaded("params", 1))
            load_weights(sp)

        @block.gpsimd
        def _(pool):
            split_weights(pool)

        @block.scalar
        def _(act):
            act.dma_start(pos[:, :], dram["positions"].broadcast_to([P, S])).then_inc(*loaded("pos"))
            for c in range(0, KC, 2):
                act.dma_start(hT[:, c:c + 2, :], dram["xT"][:, c:c + 2, :]).then_inc(*loaded(f"h_in{c // 2}"))
            act.wait_ge(*when("params", 1))
            rope_table_act(act)
            act.activation(cond[:, :, :], par[:, pc["cond"][0]:pc["cond"][0] + 2 * KC].rearrange("p (k c) -> p k c", c=2),
                           ACT.Silu).then_inc(*done("cond"))
            for l in layers:
                pre_norm_act(act, ("mix", l), f"mix_pre{l}", hT, a_hi, S, h_before(l))
                rstd_act(act, ("mix", l), S)
                for c in range(2):
                    modulation_load_act(act, l, c)
                in_product_act(act, l)
                gdn_first_act(act, l)
                att_prep_act(act, l)
                gdn_decay_act(act, l)
                attention_act(act, ("att", l), att_units(l), s_buf, p_t, att_take_act(l))
                gdn_act(act, l)
                memory_act(act, l)
                memory_norm_act(act, l)
                memory_product_act(act, l)
                attention_act(act, ("x", l), x_units(l), x_s, x_pt, x_take_act(l))
                post_norm_act(act, ("x_post", l), y_x)
                pre_norm_act(act, ("f", l), f"f_pre{l}", hT, a_hi, S, lambda c: ("h", "x_post", l, c))
                rstd_act(act, ("f", l), S)
                ffn_act(act, l)
                post_norm_act(act, ("f_post", l), tmp)
            second_act(act)

        @block.vector
        def _(dve):
            rope_table_dve(dve)
            pre_norm_dve(dve, ("mix", 0), "mix_pre0", hT, a_hi, a_lo, S)
            for l in layers:
                in_product_dve(dve, l)
                gdn_first_dve(dve, l)
                att_prep_dve(dve, l)
                dve.wait_ge(*when("cmask", l))
                attention_dve(dve, ("att", l), att_units(l), s_buf, between=lambda u: gate_take_dve(dve, l, u))
                gdn_dve(dve, l)
                pre_norm_dve(dve, ("mem", l), f"mem{l}", m_in, m_hi, m_lo, M)
                memory_product_dve(dve, l)
                x_product_dve(dve, l)
                attention_dve(dve, ("x", l), x_units(l), x_s)
                for c in range(KC):
                    split_dve(dve, tmp[:, c, :], c, ("xo", l))
                between_layers_dve(dve, ("x_post", l), f"x_post{l}", y_x, ("f", l), f"f_pre{l}")
                ffn_dve(dve, l)
                between_layers_dve(dve, ("f_post", l), f"f_post{l}", tmp,
                                   ("mix", l + 1) if l + 1 < DEPTH else None, f"mix_pre{l + 1}")
            second_dve(dve)


def host_arrays(inputs):
    def turned(a):
        return np.ascontiguousarray(np.asarray(a).reshape(-1, KC, P).transpose(2, 1, 0))

    rpb = np.asarray(inputs["d_rpb_2"][0])
    return {
        "w_tiles": packed_weights(inputs),
        "mod_tiles": np.ascontiguousarray(np.asarray(inputs["mod_w_2"]).reshape(DEPTH, KC, P, 3 * KC, P)
                                          .transpose(0, 3, 2, 1, 4).reshape(DEPTH, 3 * KC, P, KC * P)),
        "params": packed_params(inputs),
        "consts": constants(),
        "positions": np.ascontiguousarray(np.asarray(inputs["positions"]).reshape(1, S)),
        "xT": turned(inputs["x"]),
        "memT": turned(inputs["mem"]),
        "ctxT": turned(inputs["ctx_2"]),
        "count_mask": count_mask(),
        "axial": axial_tables(),
        "band_mask": band_mask(),
        "column_mask": column_mask(),
        "rpb_rows": np.repeat(np.pad(rpb, ((0, 0), (0, 0), (48, 48)))[:, :, None, :], GW, axis=2),
    }


def kernel(**inputs):
    import concourse.bacc as bacc
    from concourse.bass_utils import run_bass_kernel_spmd

    inputs = {k: np.asarray(v) for k, v in inputs.items()}
    arrays = host_arrays(inputs)

    def program(book):
        nc = bacc.Bacc("TRN2", target_bir_lowering=False, num_devices=1)
        dram = {name: nc.dram_tensor(name, a.shape, mybir.dt.from_np(a.dtype), kind="ExternalInput").ap()
                for name, a in arrays.items()}
        out = nc.dram_tensor("out", (P, KC, S), mybir.dt.float32, kind="ExternalOutput").ap()
        build(nc, dram, out, book)
        return nc

    known = Book()
    program(known)
    nc = program(Book(known))

    r = run_bass_kernel_spmd(nc, [arrays], core_ids=[0])
    out = np.asarray(r.results[0]["out"])
    return np.ascontiguousarray(out.transpose(2, 1, 0).reshape(1, S, D))
```
